# Optimizing a Trainium2 kernel written in Bass

```python
import math
import jax, jax.numpy as jnp
from jax import lax
import numpy as np

D_MODEL = 1024
BATCH = 1
SEQ = 512
DEPTH = 2

MLA_HEADS = 8
MLA_NOPE = 64
MLA_ROPE = 32
MLA_V = 64
MLA_Q_RANK = 256
MLA_KV_RANK = 128
ROPE_BASE = 10000.0
Q_BLOCK = 128
POS_MAX_OFFSET = 4096

MLSTM_HEADS = 4
MLSTM_DH = 64
MLSTM_CHUNK = 64
M_INIT = -1e30

SSD_HEADS = 4
SSD_HEADDIM = 64
SSD_GROUPS = 2
SSD_HPG = SSD_HEADS // SSD_GROUPS
SSD_STATE = 128
SSD_CONV = 5
SSD_CHUNK = 128

MLA_OUT = MLA_HEADS * MLA_V
MLSTM_W = MLSTM_HEADS * MLSTM_DH
SSD_INNER = SSD_HEADS * SSD_HEADDIM
MIX_WIDTH = MLA_OUT + MLSTM_W + SSD_INNER
SSD_CONV_DIM = SSD_INNER + 2 * SSD_GROUPS * SSD_STATE
IN_SIZES = (MLA_Q_RANK, MLA_KV_RANK, MLA_ROPE,
            MLSTM_W, MLSTM_W, MLSTM_W, MLSTM_W, 4 * MLSTM_HEADS,
            SSD_INNER, SSD_CONV_DIM, 2 * SSD_HEADS)
IN_WIDTH = sum(IN_SIZES)

N_GROUPS = 4
EXPERTS_PER_GROUP = 4
N_EXPERTS = N_GROUPS * EXPERTS_PER_GROUP
TOP_K = 2
D_EXPERT = 256

DEEPNORM_ALPHA = (2 * DEPTH) ** 0.25
DEEPNORM_BETA = (8 * DEPTH) ** -0.25


F32 = jnp.float32

def _split(t, sizes):
    out, off = [], 0
    for s in sizes:
        out.append(t[..., off:off + s])
        off += s
    return out

def _layernorm(x, g, b, eps=1e-5):
    xf = x.astype(F32)
    mu = jnp.mean(xf, -1, keepdims=True)
    var = jnp.mean(jnp.square(xf - mu), -1, keepdims=True)
    return (xf - mu) * lax.rsqrt(var + eps) * g + b

def _rmsnorm(x, g, eps=1e-6):
    xf = x.astype(F32)
    return xf * lax.rsqrt(jnp.mean(xf * xf, -1, keepdims=True) + eps) * g

def _rope_table(positions):
    inv = ROPE_BASE ** (-jnp.arange(0, MLA_ROPE, 2, dtype=F32) / MLA_ROPE)
    ang = positions.astype(F32)[..., None] * inv
    return jnp.cos(ang), jnp.sin(ang)

def _apply_rope(t, cos, sin):
    half = t.shape[-1] // 2
    t1, t2 = t[..., :half].astype(F32), t[..., half:].astype(F32)
    return jnp.concatenate([t1 * cos - t2 * sin, t2 * cos + t1 * sin], -1)

def _mla(c_q, c_kv, k_r, cos, sin, q_norm, kv_norm, w_uq, w_ukv):
    Bsz, S, _ = c_q.shape
    q = (_rmsnorm(c_q, q_norm).astype(c_q.dtype) @ w_uq).reshape(Bsz, S, MLA_HEADS, MLA_NOPE + MLA_ROPE)
    q_nope = q[..., :MLA_NOPE]
    q_rope = _apply_rope(q[..., MLA_NOPE:], cos[:, :, None], sin[:, :, None]).astype(q.dtype)
    kv = (_rmsnorm(c_kv, kv_norm).astype(c_kv.dtype) @ w_ukv).reshape(Bsz, S, MLA_HEADS, MLA_NOPE + MLA_V)
    k_nope, v = kv[..., :MLA_NOPE], kv[..., MLA_NOPE:]
    k_rope = _apply_rope(k_r, cos, sin).astype(k_r.dtype)
    scale = (MLA_NOPE + MLA_ROPE) ** -0.5
    nb = S // Q_BLOCK
    qn = q_nope.reshape(Bsz, nb, Q_BLOCK, MLA_HEADS, MLA_NOPE).transpose(1, 0, 2, 3, 4)
    qr = q_rope.reshape(Bsz, nb, Q_BLOCK, MLA_HEADS, MLA_ROPE).transpose(1, 0, 2, 3, 4)

    def block(args):
        qn_b, qr_b = args
        s = (jnp.einsum('bqhd,bkhd->bhqk', qn_b, k_nope)
             + jnp.einsum('bqhr,bkr->bhqk', qr_b, k_rope)).astype(F32) * scale
        p = jax.nn.softmax(s, axis=-1).astype(v.dtype)
        return jnp.einsum('bhqk,bkhd->bqhd', p, v)

    o = lax.map(block, (qn, qr))
    return o.transpose(1, 0, 2, 3, 4).reshape(Bsz, S, MLA_OUT)

def _mlstm_scan(q, k, v, ig, lf):
    Bsz, S, H, Dh = q.shape
    L = MLSTM_CHUNK
    nc = S // L

    def chunks(t):
        t = t.reshape((Bsz, nc, L, H) + t.shape[3:])
        return jnp.moveaxis(jnp.moveaxis(t, 1, 0), 3, 2)

    mask = jnp.tril(jnp.ones((L, L), bool))

    def step(carry, inp):
        C, n, m = carry
        qc, kc, vc, igc, lfc = inp
        b = jnp.cumsum(lfc, axis=-1)
        a = jnp.where(mask, b[..., :, None] - b[..., None, :] + igc[..., None, :], -jnp.inf)
        g = b + m[..., None]
        m_t = jnp.maximum(g, jnp.max(a, -1))
        w_intra = jnp.exp(a - m_t[..., None])
        w_inter = jnp.exp(g - m_t)
        qk = jnp.einsum('bhtd,bhsd->bhts', qc, kc).astype(F32) * w_intra
        num = (jnp.einsum('bhts,bhsd->bhtd', qk, vc)
               + w_inter[..., None] * jnp.einsum('bhtd,bhde->bhte', qc, C))
        den = jnp.sum(qk, -1) + w_inter * jnp.einsum('bhtd,bhd->bht', qc, n)
        h = num / jnp.maximum(jnp.abs(den), jnp.exp(-m_t))[..., None]
        bL = b[..., -1]
        dec = bL[..., None] - b + igc
        m_new = jnp.maximum(bL + m, jnp.max(dec, -1))
        w_s = jnp.exp(dec - m_new[..., None])
        w_c = jnp.exp(bL + m - m_new)
        C = w_c[..., None, None] * C + jnp.einsum('bhs,bhsd,bhse->bhde', w_s, kc, vc)
        n = w_c[..., None] * n + jnp.einsum('bhs,bhsd->bhd', w_s, kc)
        return (C, n, m_new), h

    init = (jnp.zeros((Bsz, H, Dh, Dh), F32), jnp.zeros((Bsz, H, Dh), F32),
            jnp.full((Bsz, H), M_INIT, F32))
    _, hs = lax.scan(step, init, (chunks(q), chunks(k), chunks(v), chunks(ig), chunks(lf)))
    hs = jnp.moveaxis(jnp.moveaxis(hs, 2, 3), 0, 1)
    return hs.reshape(Bsz, S, H, Dh)

def _mlstm(q, k, v, o, gates, gate_bias, norm_g):
    Bsz, S, _ = q.shape
    shp = (Bsz, S, MLSTM_HEADS, MLSTM_DH)
    q, k, v = q.reshape(shp), k.reshape(shp) * (MLSTM_DH ** -0.5), v.reshape(shp)
    gt = gates.reshape(Bsz, S, 4, MLSTM_HEADS).astype(F32) + gate_bias
    ig_f, lf_f = gt[:, :, 0], jax.nn.log_sigmoid(gt[:, :, 1])
    ig_b, lf_b = gt[:, :, 2], jax.nn.log_sigmoid(gt[:, :, 3])
    flip = lambda t: jnp.flip(t, axis=1)
    h = (_mlstm_scan(q, k, v, ig_f, lf_f)
         + flip(_mlstm_scan(flip(q), flip(k), flip(v), flip(ig_b), flip(lf_b))))
    mu = jnp.mean(h, -1, keepdims=True)
    var = jnp.mean(jnp.square(h - mu), -1, keepdims=True)
    hn = (h - mu) * lax.rsqrt(var + 1e-5) * norm_g.reshape(MLSTM_HEADS, MLSTM_DH)
    y = jax.nn.sigmoid(o.reshape(shp).astype(F32)) * hn
    return y.reshape(Bsz, S, MLSTM_W)

def _ssd_scan(x, dt, A, Bm, Cm):
    Bsz, S, G, E, P = x.shape
    N = Bm.shape[-1]
    L = SSD_CHUNK
    nc = S // L

    def chunks(t):
        return jnp.moveaxis(t.reshape((Bsz, nc, L) + t.shape[2:]), 1, 0)

    mask = jnp.tril(jnp.ones((L, L), bool))[None, :, :, None, None]

    def step(state, inp):
        xc, dtc, Bc, Cc = inp
        cs = jnp.cumsum(dtc * A, axis=1)
        Lm = jnp.exp(jnp.where(mask, cs[:, :, None] - cs[:, None, :], -jnp.inf))
        CB = jnp.einsum('btgn,bsgn->btsg', Cc, Bc)
        xdt = xc * dtc[..., None]
        y = jnp.einsum('btsg,btsge,bsgep->btgep', CB, Lm, xdt)
        y = y + jnp.einsum('btgn,bgepn->btgep', Cc, state) * jnp.exp(cs)[..., None]
        decay_end = jnp.exp(cs[:, -1:] - cs)
        state = (jnp.exp(cs[:, -1])[..., None, None] * state
                 + jnp.einsum('bsgn,bsge,bsgep->bgepn', Bc, decay_end, xdt))
        return state, y

    init = jnp.zeros((Bsz, G, E, P, N), F32)
    _, ys = lax.scan(step, init, (chunks(x), chunks(dt), chunks(Bm), chunks(Cm)))
    return jnp.moveaxis(ys, 0, 1).reshape(Bsz, S, G, E, P)

def _ssd(z, xbc, dt_raw, conv_w, conv_b, dt_bias, a_log, d_skip, norm_g):
    Bsz, S, Cdim = xbc.shape
    pad = SSD_CONV // 2
    xbc = lax.conv_general_dilated(xbc, conv_w[:, None, :], window_strides=(1,),
                                   padding=((pad, pad),), dimension_numbers=('NWC', 'WIO', 'NWC'),
                                   feature_group_count=Cdim) + conv_b
    xbc = jax.nn.silu(xbc)
    xs, Bm, Cm = _split(xbc, (SSD_INNER, SSD_GROUPS * SSD_STATE, SSD_GROUPS * SSD_STATE))
    x = xs.reshape(Bsz, S, SSD_GROUPS, SSD_HPG, SSD_HEADDIM)
    Bm = Bm.reshape(Bsz, S, SSD_GROUPS, SSD_STATE)
    Cm = Cm.reshape(Bsz, S, SSD_GROUPS, SSD_STATE)
    dt = jax.nn.softplus(dt_raw.reshape(Bsz, S, 2, SSD_GROUPS, SSD_HPG).astype(F32)
                         + dt_bias.reshape(2, SSD_GROUPS, SSD_HPG))
    A = -jnp.exp(a_log.astype(F32)).reshape(2, SSD_GROUPS, SSD_HPG)
    flip = lambda t: jnp.flip(t, axis=1)
    y = (_ssd_scan(x, dt[:, :, 0], A[0], Bm, Cm)
         + flip(_ssd_scan(flip(x), flip(dt[:, :, 1]), A[1], flip(Bm), flip(Cm)))
         + x * d_skip.reshape(SSD_GROUPS, SSD_HPG)[..., None])
    y = y.reshape(Bsz, S, SSD_INNER) * jax.nn.silu(z.astype(F32))
    y = _rmsnorm(y.reshape(Bsz, S, SSD_GROUPS, SSD_INNER // SSD_GROUPS),
                 norm_g.reshape(SSD_GROUPS, SSD_INNER // SSD_GROUPS))
    return y.reshape(Bsz, S, SSD_INNER)

def _hier_moe(x, wg, bg, we, be, w_gate, w_up, w_down):
    glog = (jnp.einsum('bsd,dg->bsg', x, wg) + bg).astype(F32)
    gp, gi = lax.top_k(jax.nn.softmax(glog, -1), 1)
    elog = (jnp.einsum('bsd,gde->bsge', x, we) + be).astype(F32)
    elog = jnp.einsum('bsge,bsg->bse', elog, jax.nn.one_hot(gi[..., 0], N_GROUPS, dtype=F32))
    ep, ei = lax.top_k(jax.nn.softmax(elog, -1), TOP_K)
    ep = ep / jnp.sum(ep, -1, keepdims=True)
    eid = gi * EXPERTS_PER_GROUP + ei
    combine = jnp.sum(jax.nn.one_hot(eid, N_EXPERTS, dtype=F32) * (gp * ep)[..., None], axis=2)
    h = jax.nn.silu(jnp.einsum('bsd,edf->bsef', x, w_gate)) * jnp.einsum('bsd,edf->bsef', x, w_up)
    h = h * combine[..., None].astype(h.dtype)
    return jnp.einsum('bsef,efd->bsd', h, w_down)

def first_inputs(seed: int = 0) -> dict:
    key = jax.random.key(seed)
    ks = jax.random.split(key, 32)
    nrm = lambda k, shape, s: jax.random.normal(k, shape, F32) * s
    gain = lambda k, shape: 1.0 + 0.02 * jax.random.normal(k, shape, F32)

    x = jax.random.normal(ks[0], (BATCH, SEQ, D_MODEL), F32)
    positions = (jax.random.randint(ks[1], (BATCH, 1), 0, POS_MAX_OFFSET, dtype=jnp.int32)
                 + jnp.arange(SEQ, dtype=jnp.int32)[None, :])

    w_in = nrm(ks[2], (DEPTH, D_MODEL, IN_WIDTH), D_MODEL ** -0.5)
    mla_q_norm = gain(ks[3], (DEPTH, MLA_Q_RANK))
    mla_kv_norm = gain(ks[4], (DEPTH, MLA_KV_RANK))
    mla_w_uq = nrm(ks[5], (DEPTH, MLA_Q_RANK, MLA_HEADS * (MLA_NOPE + MLA_ROPE)), MLA_Q_RANK ** -0.5)
    mla_w_ukv = nrm(ks[6], (DEPTH, MLA_KV_RANK, MLA_HEADS * (MLA_NOPE + MLA_V)), MLA_KV_RANK ** -0.5)

    lin = jnp.linspace(3.0, 6.0, MLSTM_HEADS, dtype=F32)
    zer = jnp.zeros((MLSTM_HEADS,), F32)
    mlstm_gate_bias = jnp.stack([zer, lin, zer, lin])[None] + nrm(ks[7], (DEPTH, 4, MLSTM_HEADS), 0.1)
    mlstm_norm = gain(ks[8], (DEPTH, MLSTM_W))

    ssd_conv_w = nrm(ks[9], (DEPTH, SSD_CONV, SSD_CONV_DIM), SSD_CONV ** -0.5)
    ssd_conv_b = nrm(ks[10], (DEPTH, SSD_CONV_DIM), 0.01)
    dt0 = jnp.exp(jax.random.uniform(ks[11], (DEPTH, 2, SSD_HEADS), F32, math.log(1e-3), math.log(1e-1)))
    ssd_dt_bias = dt0 + jnp.log(-jnp.expm1(-dt0))
    ssd_a_log = jnp.log(jax.random.uniform(ks[12], (DEPTH, 2, SSD_HEADS), F32, 1.0, 16.0))
    ssd_d = gain(ks[13], (DEPTH, SSD_HEADS))
    ssd_norm = gain(ks[14], (DEPTH, SSD_INNER))

    w_out = nrm(ks[15], (DEPTH, MIX_WIDTH, D_MODEL), MIX_WIDTH ** -0.5 * DEEPNORM_BETA)
    ln1_g = gain(ks[16], (DEPTH, D_MODEL))
    ln1_b = nrm(ks[17], (DEPTH, D_MODEL), 0.02)

    router_group_w = nrm(ks[18], (DEPTH, D_MODEL, N_GROUPS), D_MODEL ** -0.5)
    router_group_b = nrm(ks[19], (DEPTH, N_GROUPS), 0.01)
    router_expert_w = nrm(ks[20], (DEPTH, N_GROUPS, D_MODEL, EXPERTS_PER_GROUP), D_MODEL ** -0.5)
    router_expert_b = nrm(ks[21], (DEPTH, N_GROUPS, EXPERTS_PER_GROUP), 0.01)
    expert_w_gate = nrm(ks[22], (DEPTH, N_EXPERTS, D_MODEL, D_EXPERT), D_MODEL ** -0.5)
    expert_w_up = nrm(ks[23], (DEPTH, N_EXPERTS, D_MODEL, D_EXPERT), D_MODEL ** -0.5)
    expert_w_down = nrm(ks[24], (DEPTH, N_EXPERTS, D_EXPERT, D_MODEL), D_EXPERT ** -0.5 * DEEPNORM_BETA)
    ln2_g = gain(ks[25], (DEPTH, D_MODEL))
    ln2_b = nrm(ks[26], (DEPTH, D_MODEL), 0.02)

    return {"x": x, "positions": positions, "w_in": w_in,
            "mla_q_norm": mla_q_norm, "mla_kv_norm": mla_kv_norm,
            "mla_w_uq": mla_w_uq, "mla_w_ukv": mla_w_ukv,
            "mlstm_gate_bias": mlstm_gate_bias, "mlstm_norm": mlstm_norm,
            "ssd_conv_w": ssd_conv_w, "ssd_conv_b": ssd_conv_b, "ssd_dt_bias": ssd_dt_bias,
            "ssd_a_log": ssd_a_log, "ssd_d": ssd_d, "ssd_norm": ssd_norm,
            "w_out": w_out, "ln1_g": ln1_g, "ln1_b": ln1_b,
            "router_group_w": router_group_w, "router_group_b": router_group_b,
            "router_expert_w": router_expert_w, "router_expert_b": router_expert_b,
            "expert_w_gate": expert_w_gate, "expert_w_up": expert_w_up, "expert_w_down": expert_w_down,
            "ln2_g": ln2_g, "ln2_b": ln2_b}

def first_block(x, positions, w_in, mla_q_norm, mla_kv_norm, mla_w_uq, mla_w_ukv,
              mlstm_gate_bias, mlstm_norm, ssd_conv_w, ssd_conv_b, ssd_dt_bias,
              ssd_a_log, ssd_d, ssd_norm, w_out, ln1_g, ln1_b,
              router_group_w, router_group_b, router_expert_w, router_expert_b,
              expert_w_gate, expert_w_up, expert_w_down, ln2_g, ln2_b):
    dtype = x.dtype
    cos, sin = _rope_table(positions)
    for l in range(DEPTH):
        p = jnp.einsum('bsd,dc->bsc', x, w_in[l])
        (c_q, c_kv, k_r, m_q, m_k, m_v, m_o, m_g, s_z, s_xbc, s_dt) = _split(p, IN_SIZES)
        y_a = _mla(c_q, c_kv, k_r, cos, sin, mla_q_norm[l], mla_kv_norm[l], mla_w_uq[l], mla_w_ukv[l])
        y_b = _mlstm(m_q, m_k, m_v, m_o, m_g, mlstm_gate_bias[l], mlstm_norm[l])
        y_c = _ssd(s_z, s_xbc, s_dt, ssd_conv_w[l], ssd_conv_b[l], ssd_dt_bias[l],
                   ssd_a_log[l], ssd_d[l], ssd_norm[l])
        heads = jnp.concatenate([y_a.astype(dtype), y_b.astype(dtype), y_c.astype(dtype)], -1)
        mix = jnp.einsum('bsc,cd->bsd', heads, w_out[l])
        x = _layernorm(DEEPNORM_ALPHA * x + mix, ln1_g[l], ln1_b[l]).astype(dtype)
        ffn = _hier_moe(x, router_group_w[l], router_group_b[l], router_expert_w[l], router_expert_b[l],
                        expert_w_gate[l], expert_w_up[l], expert_w_down[l]).astype(dtype)
        x = _layernorm(DEEPNORM_ALPHA * x + ffn, ln2_g[l], ln2_b[l]).astype(dtype)
    return x


DEPTH_2 = 1

D_MIX = D_MODEL
GDN_WIDTH = D_MIX // 2
GDN_HEAD_DIM = 128
GDN_HEADS = GDN_WIDTH // GDN_HEAD_DIM
GDN_CHUNK = 64
LRU_WIDTH = D_MIX - GDN_WIDTH
LRU_BLOCKS = 8
LRU_BLOCK_DIM = LRU_WIDTH // LRU_BLOCKS
LRU_C = 8.0
CONV_WIDTH = 4
D_FF = 4 * D_MODEL
EPS = 1e-6
SPLIT_SIZES = (3 * GDN_WIDTH, GDN_WIDTH, GDN_HEADS, GDN_HEADS, LRU_WIDTH, LRU_WIDTH)
IN_COLS = sum(SPLIT_SIZES)
SPLIT_IDX = tuple(int(i) for i in np.cumsum(SPLIT_SIZES)[:-1])


def rmsnorm(x, w):
    xf = x.astype(jnp.float32)
    y = xf * lax.rsqrt(jnp.mean(xf * xf, axis=-1, keepdims=True) + EPS)
    return (y * w.astype(jnp.float32)).astype(x.dtype)

def l2norm(x):
    xf = x.astype(jnp.float32)
    return xf * lax.rsqrt(jnp.sum(xf * xf, axis=-1, keepdims=True) + EPS)

def causal_depthwise_conv(x, w):
    c = x.shape[-1]
    return lax.conv_general_dilated(
        x, w[:, None, :].astype(x.dtype), window_strides=(1,),
        padding=[(CONV_WIDTH - 1, 0)], dimension_numbers=("NWC", "WIO", "NWC"),
        feature_group_count=c)

def gated_delta_rule_chunked(q, k, v, g, beta):
    f32 = jnp.float32
    b, s, h, dk = q.shape
    dv = v.shape[-1]
    c = GDN_CHUNK
    n = s // c

    def to_chunks(t):
        t = jnp.moveaxis(t.astype(f32), 2, 1)
        return t.reshape(b, h, n, c, *t.shape[3:])

    q = to_chunks(q) * (dk ** -0.5)
    k = to_chunks(k)
    v = to_chunks(v)
    g_cum = jnp.cumsum(to_chunks(g), axis=-1)
    beta = to_chunks(beta)

    causal = jnp.tril(jnp.ones((c, c), dtype=bool))
    strict = jnp.tril(jnp.ones((c, c), dtype=bool), -1)
    diff = g_cum[..., :, None] - g_cum[..., None, :]
    decay = jnp.where(causal, jnp.exp(jnp.where(causal, diff, 0.0)), 0.0)

    k_beta = k * beta[..., None]
    v_beta = v * beta[..., None]
    a_low = jnp.where(strict, jnp.einsum("bhnid,bhnjd->bhnij", k_beta, k) * decay, 0.0)
    i_plus_a = a_low + jnp.eye(c, dtype=f32)
    rhs = jnp.concatenate([v_beta, k_beta * jnp.exp(g_cum)[..., None]], axis=-1)
    sol = lax.linalg.triangular_solve(i_plus_a, rhs, left_side=True, lower=True)
    u = sol[..., :dv]
    w = sol[..., dv:]
    qk_intra = jnp.where(causal, jnp.einsum("bhnid,bhnjd->bhnij", q, k) * decay, 0.0)

    def step(state, inp):
        q_c, k_c, u_c, w_c, attn_c, g_c = inp
        v_new = u_c - jnp.einsum("bhck,bhkv->bhcv", w_c, state)
        o_c = (jnp.einsum("bhck,bhkv->bhcv", q_c * jnp.exp(g_c)[..., None], state)
               + jnp.einsum("bhij,bhjv->bhiv", attn_c, v_new))
        g_last = g_c[..., -1]
        k_dec = k_c * jnp.exp(g_last[..., None] - g_c)[..., None]
        state = state * jnp.exp(g_last)[..., None, None] + jnp.einsum("bhck,bhcv->bhkv", k_dec, v_new)
        return state, o_c

    xs = tuple(jnp.moveaxis(t, 2, 0) for t in (q, k, u, w, qk_intra, g_cum))
    state0 = jnp.zeros((b, h, dk, dv), f32)
    _, o = lax.scan(step, state0, xs)
    o = jnp.moveaxis(o, 0, 2).reshape(b, h, s, dv)
    return jnp.moveaxis(o, 1, 2)

def rg_lru(x, wa, ba, wx, bx, a_param):
    f32 = jnp.float32
    b, s, d = x.shape
    xf = x.astype(f32)
    xb = xf.reshape(b, s, LRU_BLOCKS, LRU_BLOCK_DIM)
    r = jax.nn.sigmoid(jnp.einsum("bsgi,gij->bsgj", xb, wa.astype(f32)) + ba.astype(f32)).reshape(b, s, d)
    i = jax.nn.sigmoid(jnp.einsum("bsgi,gij->bsgj", xb, wx.astype(f32)) + bx.astype(f32)).reshape(b, s, d)
    log_a = -LRU_C * r * jax.nn.softplus(-a_param.astype(f32))
    a = jnp.exp(log_a)
    gated_x = jnp.sqrt(-jnp.expm1(2.0 * log_a)) * (i * xf)

    def combine(c1, c2):
        a1, b1 = c1
        a2, b2 = c2
        return a1 * a2, a2 * b1 + b2

    _, h = lax.associative_scan(combine, (a, gated_x), axis=1)
    return h

def hybrid_layer(x, norm_mix_w, w_in, gdn_conv_w, gdn_A_log, gdn_dt_bias, gdn_norm_w,
                 lru_conv_w, lru_conv_b, lru_gate_a_w, lru_gate_a_b, lru_gate_x_w, lru_gate_x_b,
                 lru_a_param, w_out, norm_mlp_w, w_ff1, w_ff2):
    b, s, _ = x.shape
    dt = x.dtype
    h = rmsnorm(x, norm_mix_w)
    proj = jnp.einsum("bsd,de->bse", h, w_in.astype(dt))
    qkv, z, b_logit, a_logit, lru_x, lru_gate = jnp.split(proj, SPLIT_IDX, axis=-1)

    qkv = jax.nn.silu(causal_depthwise_conv(qkv, gdn_conv_w))
    q, k, v = jnp.split(qkv, 3, axis=-1)
    q = l2norm(q.reshape(b, s, GDN_HEADS, GDN_HEAD_DIM))
    k = l2norm(k.reshape(b, s, GDN_HEADS, GDN_HEAD_DIM))
    v = v.reshape(b, s, GDN_HEADS, GDN_HEAD_DIM)
    beta = jax.nn.sigmoid(b_logit.astype(jnp.float32))
    g = -jnp.exp(gdn_A_log.astype(jnp.float32)) * jax.nn.softplus(
        a_logit.astype(jnp.float32) + gdn_dt_bias.astype(jnp.float32))
    o = gated_delta_rule_chunked(q, k, v, g, beta)
    z = z.reshape(b, s, GDN_HEADS, GDN_HEAD_DIM).astype(jnp.float32)
    o = rmsnorm(o, gdn_norm_w) * jax.nn.silu(z)
    gdn_out = o.reshape(b, s, GDN_WIDTH).astype(dt)

    xr = causal_depthwise_conv(lru_x, lru_conv_w) + lru_conv_b.astype(dt)
    hr = rg_lru(xr, lru_gate_a_w, lru_gate_a_b, lru_gate_x_w, lru_gate_x_b, lru_a_param)
    lru_out = (hr * jax.nn.gelu(lru_gate.astype(jnp.float32))).astype(dt)

    mix = jnp.concatenate([gdn_out, lru_out], axis=-1)
    x = x + jnp.einsum("bse,ed->bsd", mix, w_out.astype(dt))

    m = rmsnorm(x, norm_mlp_w)
    u = jax.nn.relu(jnp.einsum("bsd,df->bsf", m, w_ff1.astype(dt)))
    x = x + jnp.einsum("bsf,fd->bsd", u * u, w_ff2.astype(dt))
    return x

def second_inputs(seed: int = 0) -> dict:
    key = jax.random.key(seed)
    ks = jax.random.split(key, 24)
    f32 = jnp.float32
    nrm = lambda k, shape, scale: (jax.random.normal(k, shape, f32) * scale)
    x = jax.random.normal(ks[0], (BATCH, SEQ, D_MODEL), f32)
    norm_mix_w = 1.0 + nrm(ks[1], (DEPTH_2, D_MODEL), 0.02)
    w_in = nrm(ks[2], (DEPTH_2, D_MODEL, IN_COLS), D_MODEL ** -0.5)
    gdn_conv_w = nrm(ks[3], (DEPTH_2, CONV_WIDTH, 3 * GDN_WIDTH), CONV_WIDTH ** -0.5)
    gdn_A_log = jnp.log(jax.random.uniform(ks[4], (DEPTH_2, GDN_HEADS), f32, 1.0, 16.0))
    dt0 = jnp.exp(jax.random.uniform(ks[5], (DEPTH_2, GDN_HEADS), f32, math.log(1e-3), math.log(1e-1)))
    gdn_dt_bias = dt0 + jnp.log(-jnp.expm1(-dt0))
    gdn_norm_w = 1.0 + nrm(ks[6], (DEPTH_2, GDN_HEAD_DIM), 0.02)
    lru_conv_w = nrm(ks[7], (DEPTH_2, CONV_WIDTH, LRU_WIDTH), CONV_WIDTH ** -0.5)
    lru_conv_b = nrm(ks[8], (DEPTH_2, LRU_WIDTH), 0.01)
    lru_gate_a_w = nrm(ks[9], (DEPTH_2, LRU_BLOCKS, LRU_BLOCK_DIM, LRU_BLOCK_DIM), LRU_BLOCK_DIM ** -0.5)
    lru_gate_a_b = nrm(ks[10], (DEPTH_2, LRU_BLOCKS, LRU_BLOCK_DIM), 0.01)
    lru_gate_x_w = nrm(ks[11], (DEPTH_2, LRU_BLOCKS, LRU_BLOCK_DIM, LRU_BLOCK_DIM), LRU_BLOCK_DIM ** -0.5)
    lru_gate_x_b = nrm(ks[12], (DEPTH_2, LRU_BLOCKS, LRU_BLOCK_DIM), 0.01)
    a_c = jax.random.uniform(ks[13], (DEPTH_2, LRU_WIDTH), f32, 0.9, 0.999)
    sig_l = a_c ** (1.0 / LRU_C)
    lru_a_param = jnp.log(sig_l) - jnp.log1p(-sig_l)
    w_out = nrm(ks[14], (DEPTH_2, D_MIX, D_MODEL), D_MIX ** -0.5)
    norm_mlp_w = 1.0 + nrm(ks[15], (DEPTH_2, D_MODEL), 0.02)
    w_ff1 = nrm(ks[16], (DEPTH_2, D_MODEL, D_FF), D_MODEL ** -0.5)
    w_ff2 = nrm(ks[17], (DEPTH_2, D_FF, D_MODEL), D_FF ** -0.5)
    final_norm_w = 1.0 + nrm(ks[18], (D_MODEL,), 0.02)
    return {"x": x, "norm_mix_w": norm_mix_w, "w_in": w_in, "gdn_conv_w": gdn_conv_w,
            "gdn_A_log": gdn_A_log, "gdn_dt_bias": gdn_dt_bias, "gdn_norm_w": gdn_norm_w,
            "lru_conv_w": lru_conv_w, "lru_conv_b": lru_conv_b,
            "lru_gate_a_w": lru_gate_a_w, "lru_gate_a_b": lru_gate_a_b,
            "lru_gate_x_w": lru_gate_x_w, "lru_gate_x_b": lru_gate_x_b,
            "lru_a_param": lru_a_param, "w_out": w_out, "norm_mlp_w": norm_mlp_w,
            "w_ff1": w_ff1, "w_ff2": w_ff2, "final_norm_w": final_norm_w}

def second_block(x, norm_mix_w, w_in, gdn_conv_w, gdn_A_log, gdn_dt_bias, gdn_norm_w,
              lru_conv_w, lru_conv_b, lru_gate_a_w, lru_gate_a_b, lru_gate_x_w, lru_gate_x_b,
              lru_a_param, w_out, norm_mlp_w, w_ff1, w_ff2, final_norm_w):
    for layer in range(DEPTH_2):
        x = hybrid_layer(x, norm_mix_w[layer], w_in[layer], gdn_conv_w[layer], gdn_A_log[layer],
                         gdn_dt_bias[layer], gdn_norm_w[layer], lru_conv_w[layer], lru_conv_b[layer],
                         lru_gate_a_w[layer], lru_gate_a_b[layer], lru_gate_x_w[layer],
                         lru_gate_x_b[layer], lru_a_param[layer], w_out[layer], norm_mlp_w[layer],
                         w_ff1[layer], w_ff2[layer])
    return rmsnorm(x, final_norm_w)


def setup_inputs(seed=0):
    out = dict(first_inputs(seed))
    for name, value in second_inputs(seed + 1).items():
        if name != "x":
            out[name + "_2"] = value
    return out


def reference(
    x, positions, w_in, mla_q_norm, mla_kv_norm, mla_w_uq, mla_w_ukv, mlstm_gate_bias,
    mlstm_norm, ssd_conv_w, ssd_conv_b, ssd_dt_bias, ssd_a_log, ssd_d, ssd_norm, w_out, ln1_g,
    ln1_b, router_group_w, router_group_b, router_expert_w, router_expert_b, expert_w_gate,
    expert_w_up, expert_w_down, ln2_g, ln2_b, norm_mix_w_2, w_in_2, gdn_conv_w_2, gdn_A_log_2,
    gdn_dt_bias_2, gdn_norm_w_2, lru_conv_w_2, lru_conv_b_2, lru_gate_a_w_2, lru_gate_a_b_2,
    lru_gate_x_w_2, lru_gate_x_b_2, lru_a_param_2, w_out_2, norm_mlp_w_2, w_ff1_2, w_ff2_2,
    final_norm_w_2,
):
    x = first_block(
        x, positions, w_in, mla_q_norm, mla_kv_norm, mla_w_uq, mla_w_ukv, mlstm_gate_bias,
        mlstm_norm, ssd_conv_w, ssd_conv_b, ssd_dt_bias, ssd_a_log, ssd_d, ssd_norm, w_out,
        ln1_g, ln1_b, router_group_w, router_group_b, router_expert_w, router_expert_b,
        expert_w_gate, expert_w_up, expert_w_down, ln2_g, ln2_b,
    )
    return second_block(
        x, norm_mix_w_2, w_in_2, gdn_conv_w_2, gdn_A_log_2, gdn_dt_bias_2, gdn_norm_w_2,
        lru_conv_w_2, lru_conv_b_2, lru_gate_a_w_2, lru_gate_a_b_2, lru_gate_x_w_2,
        lru_gate_x_b_2, lru_a_param_2, w_out_2, norm_mlp_w_2, w_ff1_2, w_ff2_2, final_norm_w_2,
    )


_drawn_inputs = setup_inputs


def setup_inputs(seed=0):
    import zlib

    import numpy as np

    out = dict(_drawn_inputs(seed))
    spreads = {}
    factors = {'mla_q_norm': 8.0,
     'mla_kv_norm': 8.0,
     'mlstm_norm': 8.0,
     'ssd_conv_b': 5.749,
     'ssd_d': 8.0,
     'ssd_norm': 6.686,
     'router_group_b': 7.279,
     'router_expert_b': 8.0,
     'norm_mix_w_2': 3.586,
     'gdn_norm_w_2': 17.921,
     'lru_conv_b_2': 8.977,
     'lru_gate_a_b_2': 198.424,
     'lru_gate_x_b_2': 53.082,
     'norm_mlp_w_2': 11.393,
     'final_norm_w_2': 22.054}
    for name, (base, spread) in spreads.items():
        noise = np.random.default_rng([zlib.crc32(name.encode()), seed]).standard_normal(out[name].shape)
        drawn = base * np.exp(spread * noise) if base else spread * noise
        out[name] = __import__('jax').numpy.asarray(drawn.astype(out[name].dtype))
    for name, factor in factors.items():
        out[name] = (out[name] * factor).astype(out[name].dtype)
    return out
```

```python
import math
from contextlib import ExitStack, contextmanager

import numpy as np

import concourse.bass as bass
from concourse import mybir

F32 = mybir.dt.float32
F32R = mybir.dt.float32r
I32 = mybir.dt.int32
ALU = mybir.AluOpType
ACT = mybir.ActivationFunctionType
AX = mybir.AxisListType

P = 128
S = 512
NT = S // P
D = 1024
KD = D // P
DEPTH = 2
ALPHA = (2 * DEPTH) ** 0.25
NEG = -1e30

HEADS, NOPE, ROPE, VD = 8, 64, 32, 64
SCALE = (NOPE + ROPE) ** -0.5
RING, SLOT = 3, 6144
NE, FE = 16, 256
NGR = 4

C_QN, C_KVN, C_CW, C_CB, C_DS, C_SN, C_SGN, C_SB, C_AL, C_IB, C_N = 0, 2, 3, 33, 39, 41, 43, 44, 45, 46, 47
R_MN, R_RB, R_L1, R_L2, R_N = 0, 256, 276, 276 + 2 * D, 276 + 4 * D
GR = 40


class Chain:

    def __init__(self, eng, sem):
        self.eng, self.sem, self.n = eng, sem, 0

    def __call__(self, ins):
        ins.then_inc(self.sem, 1)
        self.n += 1
        self.eng.wait_ge(self.sem, self.n)


@contextmanager
def stage(nc, name, *names):
    with ExitStack() as ctx:
        sems = [ctx.enter_context(nc.semaphore(n)) for n in names]
        with nc.Block(f"{name}_{nc.next_id()}", no_gpsimd_drain=True) as block:
            yield block, sems
        nums = [s.num for s in sems]
        nc.all_engine_barrier(sems_to_clear=range(min(nums), max(nums) + 1))


def rstd(act, link, out, var, scale, eps):
    link(act.activation(out, var, ACT.Ln, scale=scale, bias=eps))
    return act.activation(out, out, ACT.Exp, scale=-0.5)


def blocks(x):
    return x.rearrange("p (b n) -> p b n", b=NT)


def every_block(x):
    return x.rearrange("p (a n) -> p a n", a=1).to_broadcast([P, NT, P])


def constants(nc, m, consts_dram, pos_dram):
    with stage(nc, "constants", "pool_step", "const_in", "pos_in", "dve_step", "angle", "sine") as (block, sems):
        pool_step, const_in, pos_in, dve_step, angle, sine = sems

        @block.sync
        def _(sp):
            sp.dma_start(m.X[:, :, :], m.x_dram.rearrange("(t p) d -> p t d", p=P)).then_inc(const_in, 16)
            sp.dma_start(m.CC[:, :], consts_dram).then_inc(const_in, 16)
            sp.dma_start(m.dup[:, :], m.dup_dram).then_inc(const_in, 16)
            sp.wait_ge(const_in, 48)

        @block.gpsimd
        def _(pool):
            link = Chain(pool, pool_step)
            link(pool.memset(m.ident[:, :], 0.0))
            link(pool.affine_select(out=m.ident[:, :], in_=m.ident[:, :], compare_op=ALU.not_equal, fill=1.0,
                                    base=0, pattern=[[-1, P]], channel_multiplier=1))
            link(pool.memset(m.ones[:, :], 1.0))
            link(pool.memset(m.zeros[:, :], 0.0))
            for d, sign in ((0, 1), (1, -1)):
                link(pool.affine_select(out=m.mask[:, d, :], in_=m.zeros[:, 0:P], compare_op=ALU.is_ge, fill=NEG, base=0,
                                        pattern=[[sign, P]], channel_multiplier=-sign))
            link(pool.affine_select(out=m.TRI[:, :], in_=m.ones[:, :], compare_op=ALU.is_gt, fill=0.0, base=0, pattern=[[1, P]], channel_multiplier=-1))
            link(pool.iota(m.IOTA[:, :], pattern=[[1, P]], base=0, channel_multiplier=0, allow_small_or_imprecise_dtypes=True))

        @block.vector
        def _(dve):
            link = Chain(dve, dve_step)
            dve.wait_ge(pos_in, 16)
            dve.wait_ge(const_in, 48)
            r = slice(64, 128)
            ang, k = m.ang[r, :], m.kk[r, :]
            link(dve.memset(m.TAB[0:64, :], 1.0))
            link(dve.tensor_copy(ang, m.posi[r, :]))
            link(dve.tensor_scalar(ang, ang, m.CC[r, 0:1], None, ALU.mult))
            link(dve.tensor_scalar(k, ang, 1.0 / (2 * math.pi), m.CC[r, 1:2], ALU.mult, ALU.add))
            link(dve.tensor_scalar(k, k, 12582912.0, None, ALU.add))
            link(dve.tensor_scalar(k, k, -12582912.0, None, ALU.add))
            for c in (6.28125, 0.0019350051879882812, 3.0199159819567e-07):
                link(dve.scalar_tensor_tensor(out=ang, in0=k, scalar=-c, in1=ang, op0=ALU.mult, op1=ALU.add))
            link(dve.tensor_scalar(ang, ang, m.CC[r, 2:3], None, ALU.add))
            link(dve.tensor_scalar(ang, ang, 3.1415925, -3.1415925, ALU.min, ALU.max))
            dve.sem_inc(angle, 1)
            dve.wait_ge(sine, 1)
            link(dve.tensor_scalar(m.TAB[r, :], k, m.CC[r, 3:4], None, ALU.mult))

        @block.scalar
        def _(act):
            act.dma_start(m.posi[:, :], pos_dram.to_broadcast([P, S])).then_inc(pos_in, 16)
            act.wait_ge(angle, 1)
            act.activation(m.kk[64:128, :], m.ang[64:128, :], ACT.Sin).then_inc(sine, 1)


def transpose_stage(nc, m, loads=None, params=None):
    with stage(nc, "transpose_stage", "transposed", "xt_act", "xt_dve", "param_in") as (block, (transposed, xt_act, xt_dve, param_in)):

        @block.sync
        def _(sp):
            if loads:
                loads(sp)
            if params:
                n = params(sp, param_in)
                sp.wait_ge(param_in, 16 * n)

        @block.tensor
        def _(pe):
            for k in range(KD):
                for t in range(NT):
                    last = pe.transpose(m.ps[k][:, t * P:(t + 1) * P], m.X[:, t, k * P:(k + 1) * P], m.ident[:, :])
                last.then_inc(transposed, 1)

        @block.scalar
        def _(act):
            for k in range(0, KD, 2):
                act.wait_ge(transposed, k + 1)
                act.copy(m.XT[:, k, :], m.ps[k][:, :]).then_inc(xt_act, 1)
            act.wait_ge(xt_act, KD // 2)

        @block.vector
        def _(dve):
            for k in range(1, KD, 2):
                dve.wait_ge(transposed, k + 1)
                dve.tensor_copy(m.XT[:, k, :], m.ps[k][:, :]).then_inc(xt_dve, 1)
            dve.wait_ge(xt_dve, KD // 2)


def in_projection(nc, m, layer, mx):
    with stage(nc, "in_projection", "unit_done", "home_act", "home_dve") as (block, (unit_done, home_act, home_dve)):
        units = []
        for c in range(3):
            units.append((0, c * P, P, S, [("copy", slice(0, P), mx.CQ[:, c, :])]))
        units.append((0, 3 * P, P, S, [("copy", slice(0, GR), mx.SC[0:GR, :]), ("rope", slice(64, 128), mx.KRT[64:128, :])]))
        for c in range(6):
            units.append((1 + c // 4, (c % 4) * P, P, S, [("copy", slice(0, P), mx.XB[:, c, 2:2 + S])]))
        for c in range(2):
            units.append((2, (2 + c) * P, P, S, [("copy", slice(0, P), mx.Z[:, c, :])]))
        for c in range(2):
            units.append((3, c * P, P, S, [("copy", slice(0, P), mx.MQ[:, c, :])]))
        for c in range(2):
            units.append((3, (2 + c) * P, P, S, [("scale", slice(0, P), mx.MK[:, c, :])]))
        units.append((4, 4096, GR, GR, [("copy", slice(0, GR), mx.IG[0:GR, :])]))
        for t in range(NT):
            units.append((4, None, t, S, [("v", None, mx.V1[:, t, :, 0:64]), ("copy2", None, mx.O[:, t, :])]))
        engine = [g % 2 if g > 3 else (1 if g in (1, 3) else 0) for g in range(len(units))]

        def evictions(eng, which, done):
            for g, (_, _, _, _, homes) in enumerate(units):
                if engine[g] != which:
                    continue
                bank = m.ps[g % 8]
                eng.wait_ge(unit_done, g + 1)
                for kind, rows, home in homes:
                    if kind == "rope":
                        last = eng.tensor_tensor(home, bank[rows, :], m.TAB[rows, :], ALU.mult)
                        continue
                    if kind == "v":
                        src = bank[:, 0:256].rearrange("p (h d) -> p h d", h=4)
                    elif kind == "copy2":
                        src = bank[:, 256:512]
                    else:
                        src = bank[rows, :]
                    factor = 0.125 if kind == "scale" else None
                    if which == 0:
                        last = eng.mul(home, src, factor) if factor else eng.copy(home, src)
                    else:
                        last = eng.tensor_scalar(home, src, factor, None, ALU.mult) if factor else eng.tensor_copy(home, src)
                last.then_inc(done, 1)
            eng.wait_ge(done, sum(1 for e in engine if e == which))

        @block.sync
        def _(sp):
            sp.wait_ge(unit_done, 4)
            sp.dma_start(m.ring[:, 0, 0:4096], m.d["w_in_t"][bass.ds(layer, 1), 3].rearrange("a p n -> p (a n)")).then_inc(m.ring_in[0], 16)
            sp.wait_ge(unit_done, 8)
            sp.dma_start(m.ring[:, 1, 0:4416], m.d["w_in_n"][bass.ds(layer, 1)].rearrange("a p n -> p (a n)")).then_inc(m.ring_in[1], 16)
            sp.wait_ge(unit_done, 12)
            sp.dma_start(m.ring[:, 2, 0:3072], m.d["w_mla"][bass.ds(layer, 1)].rearrange("a p n -> p (a n)")).then_inc(m.ring_in[2], 16)
            for half, (done, slot) in enumerate(((16, 0), (len(units), 1))):
                sp.wait_ge(unit_done, done)
                sp.dma_start(m.ring[:, slot, 0:4096], m.d["w_out"][bass.ds(layer, 1), half].rearrange("a p n -> p (a n)")).then_inc(m.ring_in[slot], 16)

        @block.tensor
        def _(pe):
            seen = -1
            for g, (load, col, n, width, _) in enumerate(units):
                if load != seen:
                    seen = load
                    pe.wait_ge(m.ring_in[load % RING], 16 * (load // RING + 1))
                if g >= 8:
                    e = engine[g - 8]
                    pe.wait_ge((home_act, home_dve)[e], sum(1 for x in engine[:g - 7] if x == e))
                slot = m.ring[:, load % RING, :]
                for k in range(KD):
                    if col is None:
                        last = pe.matmul(m.ps[g % 8][:, :], m.XT[:, k, n * P:(n + 1) * P], slot[:, k * S:(k + 1) * S],
                                         start=(k == 0), stop=(k == KD - 1))
                    else:
                        at = col + k * width
                        last = pe.matmul(m.ps[g % 8][0:n, :], slot[:, at:at + n], m.XT[:, k, :],
                                         start=(k == 0), stop=(k == KD - 1))
                last.then_inc(unit_done, 1)

        @block.scalar
        def _(act):
            evictions(act, 0, home_act)

        @block.vector
        def _(dve):
            evictions(dve, 1, home_dve)

        @block.gpsimd
        def _(pool):
            pool.memset(mx.XB[:, :, 0:2], 0.0)
            pool.memset(mx.XB[:, :, 2 + S:4 + S], 0.0)
            pool.memset(mx.V1[:, :, :, 64:65], 1.0)


def mla(nc, m, mx, a):
    HH = HEADS // 2
    NU = HH * NT
    names = ("act_step", "dve_step", "squares", "sums", "inv_rms", "normed", "q_done", "q_home", "k_done", "k_home", "v_done",
             "v_home", "kr_done", "scores", "neg_max", "probs", "probs_normed", "probs_t", "probs_t_home", "pv", "head_home")
    with stage(nc, "mla", *names) as (block, sems):
        (act_step, dve_step, squares, sums, inv_rms, normed, q_done, q_home, k_done, k_home, v_done,
         v_home, kr_done, scores, neg_max, probs, probs_normed, probs_t, probs_t_home, pv, head_home) = sems
        w = m.ring[:, 2, :]
        wq = w[:, 0:2048].rearrange("p (k n) -> p k n", k=2)
        wk = w[:, 2048:2560]
        wv = w[:, 2560:3072]

        @block.tensor
        def _(pe):
            pe.wait_ge(m.ring_in[2], 32)
            pe.wait_ge(squares, 1)
            pe.matmul(m.ps[0][:, :], m.ones[:, :], a.SQ[:, 0, :], start=True, stop=False)
            pe.matmul(m.ps[0][:, :], m.ones[:, :], a.SQ[:, 1, :], start=False, stop=True)
            pe.matmul(m.ps[1][:, :], m.ones[:, :], a.SQ[:, 2, :], start=True, stop=True).then_inc(sums, 1)
            pe.matmul(m.ps[2][64:128, :], m.dup[64:128, :], mx.KRT[64:128, :], start=True, stop=True).then_inc(kr_done, 1)
            pe.wait_ge(normed, 1)
            for t in range(NT):
                if t >= 1:
                    pe.wait_ge(v_home, t)
                pe.matmul(m.ps[3][:, :], mx.CQ[:, 2, t * P:(t + 1) * P], wv, start=True, stop=True).then_inc(v_done, 1)
            for half in range(2):
                for hh in range(HH):
                    h = half * HH + hh
                    if h == 0:
                        pe.wait_ge(inv_rms, 2)
                    if h >= 2:
                        pe.wait_ge(q_home, h - 1)
                        pe.wait_ge(k_home, h)
                    elif h == 0:
                        pe.wait_ge(k_home, 1)
                    elif h == 1:
                        pe.wait_ge(v_home, NT)
                    for k in range(2):
                        last = pe.matmul(m.ps[h % 2][:, :], wq[:, k, h * P:(h + 1) * P], mx.CQ[:, k, :], start=(k == 0), stop=(k == 1))
                    last.then_inc(q_done, 1)
                    pe.matmul(m.ps[2 + h % 2][0:64, :], wk[:, h * 64:(h + 1) * 64], mx.CQ[:, 2, :], start=True, stop=True).then_inc(k_done, 1)
                pe.wait_ge(q_home, (half + 1) * HH)
                pe.wait_ge(k_home, 1 + (half + 1) * HH)
                for step in range(NU + 2):
                    if step < NU:
                        i = half * NU + step
                        hh, t = divmod(step, NT)
                        if i >= 2:
                            pe.wait_ge(probs, i - 1)
                        pe.matmul(m.ps[2 + i % 2][:, :], a.QT[:, hh, t * P:(t + 1) * P], a.KT[:, hh, :], start=True, stop=True).then_inc(scores, 1)
                    if 1 <= step <= NU:
                        i = half * NU + step - 1
                        pe.wait_ge(probs_normed, i + 1)
                        if i >= 2:
                            pe.wait_ge(probs_t_home, i - 1)
                        for k in range(NT):
                            last = pe.transpose(m.ps[4 + i % 2][:, k * P:(k + 1) * P], a.PR[:, i % 2, k * P:(k + 1) * P], m.ident[:, :])
                        last.then_inc(probs_t, 1)
                    if step >= 2:
                        i = half * NU + step - 2
                        h, t = divmod(i, NT)
                        pair, rows = h // 2, slice(64 * (h % 2), 64 * (h % 2) + 64)
                        pe.wait_ge(probs_t_home, i + 1)
                        if pair >= 2 and h % 2 == 0 and t == 0:
                            pe.wait_ge(head_home, pair - 1)
                        for k in range(NT):
                            last = pe.matmul(m.ps[6 + pair % 2][rows, t * P:(t + 1) * P], a.V[:, k, h * 64:(h + 1) * 64],
                                             a.PT[:, i % 2, k, :], start=(k == 0), stop=(k == NT - 1))
                        last.then_inc(pv, 1)

        @block.scalar
        def _(act):
            link = Chain(act, act_step)
            act.wait_ge(sums, 1)
            rstd(act, link, a.RS[:, 0, :], m.ps[0][:, :], 1.0 / 256, 1e-6).then_inc(inv_rms, 1)
            rstd(act, link, a.RS[:, 1, :], m.ps[1][:, :], 1.0 / 128, 1e-6).then_inc(inv_rms, 1)
            act.wait_ge(kr_done, 1)
            act.copy(a.KT[64:128, :, :], m.ps[2][64:128, :].rearrange("p (a n) -> p a n", a=1).to_broadcast([64, HH, S])).then_inc(k_home, 1)
            for t in range(NT):
                act.wait_ge(v_done, t + 1)
                act.copy(a.V[:, t, :], m.ps[3][:, :]).then_inc(v_home, 1)
            for half in range(2):
                if half:
                    act.wait_ge(scores, NU)
                for h in range(half * HH, (half + 1) * HH):
                    act.wait_ge(k_done, h + 1)
                    act.copy(a.KT[0:64, h % HH, :], m.ps[2 + h % 2][0:64, :]).then_inc(k_home, 1)
                for step in range(NU + 1):
                    if step < NU:
                        i = half * NU + step
                        act.wait_ge(neg_max, i + 1)
                        if i >= 2:
                            act.wait_ge(probs_t, i - 1)
                        act.activation(a.PR[:, i % 2, :], m.ps[2 + i % 2][:, :], ACT.Exp, bias=a.NM[:, i % 2:i % 2 + 1],
                                       scale=SCALE, accum_out=a.SM[:, i % 2:i % 2 + 1]).then_inc(probs, 1)
                    if step >= 1:
                        i = half * NU + step - 1
                        act.wait_ge(probs_t, i + 1)
                        if i >= 2:
                            act.wait_ge(pv, i - 1)
                        act.copy(a.PT[:, i % 2, :, :].rearrange("p k n -> p (k n)"), m.ps[4 + i % 2][:, :]).then_inc(probs_t_home, 1)

        @block.vector
        def _(dve):
            link = Chain(dve, dve_step)
            cq = mx.CQ[:, :, :].rearrange("p a n -> p (a n)")
            dve.tensor_tensor(a.SQ[:, :, :].rearrange("p a n -> p (a n)"), cq, cq, ALU.mult).then_inc(squares, 1)
            dve.wait_ge(inv_rms, 2)
            for c in range(3):
                last = dve.scalar_tensor_tensor(out=mx.CQ[:, c, :], in0=mx.CQ[:, c, :], scalar=m.CP[:, C_QN + c:C_QN + c + 1],
                                                in1=a.RS[:, c // 2, :], op0=ALU.mult, op1=ALU.mult)
            last.then_inc(normed, 1)
            for half in range(2):
                if half:
                    dve.wait_ge(scores, NU)
                for h in range(half * HH, (half + 1) * HH):
                    dve.wait_ge(q_done, h + 1)
                    dve.tensor_tensor(a.QT[:, h % HH, :], m.ps[h % 2][:, :], m.TAB[:, :], ALU.mult).then_inc(q_home, 1)
                for step in range(NU + 2):
                    if step < NU:
                        i = half * NU + step
                        dve.wait_ge(scores, i + 1)
                        if i >= 2:
                            dve.wait_ge(probs, i - 1)
                        link(dve.reduce_max(a.MX[:, i % 2:i % 2 + 1], m.ps[2 + i % 2][:, :], AX.X))
                        dve.tensor_scalar(a.NM[:, i % 2:i % 2 + 1], a.MX[:, i % 2:i % 2 + 1], -SCALE, None, ALU.mult).then_inc(neg_max, 1)
                    if 1 <= step <= NU:
                        i = half * NU + step - 1
                        dve.wait_ge(probs, i + 1)
                        link(dve.reciprocal(a.RC[:, i % 2:i % 2 + 1], a.SM[:, i % 2:i % 2 + 1]))
                        dve.tensor_scalar(a.PR[:, i % 2, :], a.PR[:, i % 2, :], a.RC[:, i % 2:i % 2 + 1], None, ALU.mult).then_inc(probs_normed, 1)
                    if step >= 2:
                        i = half * NU + step - 2
                        h, t = divmod(i, NT)
                        if h % 2 == 1 and t == NT - 1:
                            dve.wait_ge(pv, i + 1)
                            dve.tensor_copy(m.XT[:, h // 2, :], m.ps[6 + (h // 2) % 2][:, :]).then_inc(head_home, 1)
            dve.wait_ge(head_home, HEADS // 2)


def gates_and_conv(nc, m, mx, g):
    names = ("act_step", "dve_step", "biased", "abs_ready", "log_ready", "coef", "rows_done", "conv_done",
             "silu_done", "gates_t", "x_t", "em_ready")
    with stage(nc, "gates_and_conv", *names) as (block, sems):
        act_step, dve_step, biased, abs_ready, log_ready, coef, rows_done, conv_done, silu_done, gates_t, x_t, em_ready = sems
        R = slice(0, GR)

        @block.scalar
        def _(act):
            link = Chain(act, act_step)
            link(act.activation(g.CO[R, 0:1], m.CP[R, C_AL:C_AL + 1], ACT.Exp))
            link(act.mul(g.CO[R, 0:1], g.CO[R, 0:1], -1.0))
            link(act.activation(g.CO[R, 1:2], m.CP[R, C_SB:C_SB + 1], ACT.Identity, scale=m.CP[R, C_SGN:C_SGN + 1]))
            link(act.activation(mx.SC[R, :], mx.SC[R, :], ACT.Identity, scale=m.CP[R, C_SGN:C_SGN + 1], bias=g.CO[R, 1:2]))
            link(act.activation(mx.IG[R, :], mx.IG[R, :], ACT.Identity, bias=m.CP[R, C_IB:C_IB + 1]))
            act.sem_inc(biased, 1)
            act.wait_ge(abs_ready, 1)
            link(act.activation(g.T1[R, :], g.T1[R, :], ACT.Exp))
            act.activation(g.T1[R, :], g.T1[R, :], ACT.Ln, bias=1.0).then_inc(log_ready, 1)
            act.wait_ge(gates_t, 2)
            act.activation(g.EM[:, :, :], g.GN[:, 1, :, :], ACT.Exp, scale=-1.0).then_inc(em_ready, 1)
            for c in range(6):
                act.wait_ge(conv_done, c + 1)
                act.activation(g.XC[:, c, :], g.XC[:, c, :], ACT.Silu, bias=m.CP[:, C_CB + c:C_CB + c + 1]).then_inc(silu_done, 1)
            act.wait_ge(em_ready, 1)
            for c in range(2):
                act.activation(mx.Z[:, c, :], mx.Z[:, c, :], ACT.Silu).then_inc(silu_done, 1)
            act.activation(mx.O[:, :, :], mx.O[:, :, :], ACT.Sigmoid).then_inc(silu_done, 1)
            act.wait_ge(silu_done, 9)

        @block.vector
        def _(dve):
            link = Chain(dve, dve_step)
            dve.wait_ge(biased, 1)
            dve.scalar_tensor_tensor(out=g.T1[R, :], in0=mx.SC[R, :], scalar=-1.0, in1=mx.SC[R, :], op0=ALU.mult, op1=ALU.min).then_inc(abs_ready, 1)
            dve.wait_ge(log_ready, 1)
            link(dve.scalar_tensor_tensor(out=g.SP[R, :], in0=mx.SC[R, :], scalar=0.0, in1=g.T1[R, :], op0=ALU.max, op1=ALU.add))
            link(dve.tensor_scalar(g.T1[R, :], g.SP[R, :], g.CO[R, 0:1], None, ALU.mult))
            link(dve.memset(g.CS[R, :], 0.0))
            link(dve.tensor_tensor_scan(g.CS[0:8, :], m.zeros[0:8, :], g.T1[0:8, :], 0.0, ALU.add, ALU.add))
            link(dve.tensor_tensor_scan(g.CS[32:40, ::-1], m.zeros[32:40, ::-1], g.T1[32:40, ::-1], 0.0, ALU.add, ALU.add))
            link(dve.tensor_tensor(g.FS[R, :], mx.IG[R, :], g.CS[R, :], ALU.subtract))
            link(dve.memset(g.NM[R, :], 0.0))
            link(dve.tensor_tensor_scan(g.NM[0:8, :], m.zeros[0:8, :], g.FS[0:8, :], -3e38, ALU.add, ALU.max))
            link(dve.tensor_tensor_scan(g.NM[32:40, ::-1], m.zeros[32:40, ::-1], g.FS[32:40, ::-1], -3e38, ALU.add, ALU.max))
            link(dve.tensor_tensor(g.T1[R, :], g.CS[R, :], g.NM[R, :], ALU.add))
            dve.tensor_scalar(g.NM[R, :], g.NM[R, :], -1.0, None, ALU.mult).then_inc(rows_done, 1)
            dve.wait_ge(gates_t, 1)
            dve.tensor_copy(g.GN[:, :, :, :].rearrange("p a t r -> p (a t r)"), m.ps[0][:, 0:12 * GR]).then_inc(gates_t, 1)
            for c in range(6):
                for tap in range(5):
                    w = m.CP[:, C_CW + 5 * c + tap:C_CW + 5 * c + tap + 1]
                    src = mx.XB[:, c, tap:tap + S]
                    if tap == 0:
                        link(dve.tensor_scalar(g.XC[:, c, :], src, w, None, ALU.mult))
                    elif tap < 4:
                        link(dve.scalar_tensor_tensor(out=g.XC[:, c, :], in0=src, scalar=w, in1=g.XC[:, c, :], op0=ALU.mult, op1=ALU.add))
                    else:
                        dve.scalar_tensor_tensor(out=g.XC[:, c, :], in0=src, scalar=w, in1=g.XC[:, c, :],
                                                 op0=ALU.mult, op1=ALU.add).then_inc(conv_done, 1)
            for c in range(2):
                dve.wait_ge(x_t, c + 1)
                link(dve.tensor_copy(g.XN[:, :, c * P:(c + 1) * P], m.ps[1 + c][:, :].rearrange("p (t n) -> p t n", t=NT)))

        @block.tensor
        def _(pe):
            pe.wait_ge(rows_done, 1)
            for n, rows in enumerate((g.FS, g.T1, g.SP)):
                for t in range(NT):
                    at = (n * NT + t) * GR
                    last = pe.transpose(m.ps[0][:, at:at + GR], rows[0:GR, t * P:(t + 1) * P], m.ident[0:GR, 0:GR])
            last.then_inc(gates_t, 1)
            for c in range(2):
                pe.wait_ge(silu_done, c + 1)
                for t in range(NT):
                    last = pe.transpose(m.ps[1 + c][:, t * P:(t + 1) * P], g.XC[:, c, t * P:(t + 1) * P], m.ident[:, :])
                last.then_inc(x_t, 1)


def scans(nc, m, mx, g):
    streams = [("mlstm", h, d, h) for h in range(4) for d in range(2)]
    streams += [("ssd", h, d, 4 + h // 2) for h in range(4) for d in range(2)]
    NS = len(streams)
    last_of_base = {b: max(s for s, x in enumerate(streams) if x[3] == b) for b in range(6)}
    names = ("dve_step", "row_done", "row_masked", "decay", "base_done", "weighted", "applied", "head_out", "y_out")
    with stage(nc, "scans", *names) as (block, sems):
        dve_step, row_done, row_masked, decay, base_done, weighted, applied, head_out, y_out = sems

        def span(d, j):
            return slice(j * P, S) if d == 0 else slice(0, (j + 1) * P)

        def base_operands(b):
            if b < 4:
                rows = slice(64 * (b % 2), 64 * (b % 2) + 64)
                return mx.MK[rows, b // 2, :], mx.MQ[rows, b // 2, :]
            return g.XC[:, 2 + b - 4, :], g.XC[:, 4 + b - 4, :]

        @block.tensor
        def _(pe):
            def row(s):
                kind, h, d, _ = streams[s]
                r = 32 * d + h + (4 if kind == "ssd" else 0)
                if s >= 2:
                    pe.wait_ge(decay, 4 * (s - 1))
                pe.matmul(m.ps[4 + s % 2][:, :], m.ident[0:GR, r:r + 1].to_broadcast([GR, P]), g.NM[0:GR, :],
                          start=True, stop=True).then_inc(row_done, 1)

            def base(b, j):
                k, q = base_operands(b)
                pe.matmul(m.ps[j][:, :], k[:, j * P:(j + 1) * P], q, start=True, stop=True).then_inc(base_done, 1)

            row(0)
            row(1)
            for j in range(NT):
                base(0, j)
            for s, (kind, h, d, b) in enumerate(streams):
                for j in range(NT):
                    pe.wait_ge(weighted, 4 * s + j + 1)
                    w = g.W[:, (4 * s + j) % 4, :]
                    if kind == "mlstm":
                        if j == 0 and h >= 1:
                            pe.wait_ge(head_out, 2 * (h - 1) + d + 1)
                        tiles = range(j, NT) if d == 0 else range(0, j + 1)
                        for t in tiles:
                            last = pe.matmul(m.ps[6 + d][:, t * 65:(t + 1) * 65], w[:, t * P:(t + 1) * P], mx.V1[:, j, h, :],
                                             start=(j == 0 and t == tiles[0]), stop=(j == NT - 1 and t == tiles[-1]), skip_group_check=True)
                    else:
                        if s == 8:
                            pe.wait_ge(head_out, 8)
                        e = h % 2
                        last = pe.matmul(m.ps[6 + h // 2][64 * e:64 * e + 64, span(d, j)], g.XN[:, j, h * 64:(h + 1) * 64], w[:, span(d, j)],
                                         start=(d == 0 and j == 0), stop=(d == 1 and j == NT - 1), skip_group_check=True)
                    last.then_inc(applied, 1)
                    if s == last_of_base[b] and b < 5:
                        base(b + 1, j)
                if s + 2 < NS:
                    row(s + 2)

        @block.scalar
        def _(act):
            for s, (kind, h, d, b) in enumerate(streams):
                r = 32 * d + h + (4 if kind == "ssd" else 0)
                for j in range(NT):
                    i = 4 * s + j
                    if j == 0:
                        act.wait_ge(row_masked, s + 1)
                    if i >= 4:
                        act.wait_ge(weighted, i - 3)
                    diag = slice(j * P, (j + 1) * P)
                    off = slice((j + 1) * P, S) if d == 0 else slice(0, j * P)
                    bias = g.GN[:, 0, j, r:r + 1]
                    last = act.activation(g.E[:, i % 4, diag], g.RM[:, s % 2, diag], ACT.Exp, bias=bias)
                    if off.stop > off.start:
                        last = act.activation(g.E[:, i % 4, off], m.ps[4 + s % 2][:, off], ACT.Exp, bias=bias)
                    last.then_inc(decay, 1)

        @block.vector
        def _(dve):
            link = Chain(dve, dve_step)

            def mask_row(s):
                dve.wait_ge(row_done, s + 1)
                if s >= 2:
                    dve.wait_ge(decay, 4 * (s - 1))
                dve.tensor_tensor(blocks(g.RM[:, s % 2, :]), blocks(m.ps[4 + s % 2][:, :]), every_block(m.mask[:, streams[s][2], :]), ALU.add).then_inc(row_masked, 1)

            mask_row(0)
            for s, (kind, h, d, b) in enumerate(streams):
                if s + 1 < NS:
                    mask_row(s + 1)
                r = 32 * d + h + (4 if kind == "ssd" else 0)
                for j in range(NT):
                    i = 4 * s + j
                    dve.wait_ge(decay, i + 1)
                    dve.wait_ge(base_done, 4 * b + j + 1)
                    if i >= 4:
                        dve.wait_ge(applied, i - 3)
                    at = span(d, j)
                    if kind == "mlstm":
                        ins = dve.tensor_tensor(g.W[:, i % 4, at], g.E[:, i % 4, at], m.ps[j][:, at], ALU.mult)
                    else:
                        ins = dve.scalar_tensor_tensor(out=g.W[:, i % 4, at], in0=g.E[:, i % 4, at], scalar=g.GN[:, 2, j, r:r + 1],
                                                       in1=m.ps[j][:, at], op0=ALU.mult, op1=ALU.mult)
                    ins.then_inc(weighted, 1)
                if kind == "mlstm":
                    dve.wait_ge(applied, 4 * s + 4)
                    nd = m.ps[6 + d][:, 0:NT * 65].rearrange("p (t n) -> p t n", t=NT)
                    den = g.DN[:, d, :].rearrange("p (t a) -> p t a", a=1)
                    link(dve.tensor_scalar(g.DT[:, d, :].rearrange("p (t a) -> p t a", a=1), nd[:, :, 64:65], -1.0, None, ALU.mult))
                    link(dve.tensor_tensor(den, g.DT[:, d, :].rearrange("p (t a) -> p t a", a=1), nd[:, :, 64:65], ALU.max))
                    link(dve.tensor_tensor(den, den, g.EM[:, :, r:r + 1], ALU.max))
                    link(dve.reciprocal(g.DN[:, d, :], g.DN[:, d, :]))
                    dst = g.H[:, :, h, :] if d == 0 else g.HB[:, :, :]
                    ins = dve.tensor_tensor(dst, nd[:, :, 0:64], den.to_broadcast([P, NT, 64]), ALU.mult)
                    ins.then_inc(head_out, 1)
                    dve.wait_ge(head_out, 2 * h + d + 1)
                    if d == 1:
                        link(dve.tensor_tensor(g.H[:, :, h, :], g.H[:, :, h, :], g.HB[:, :, :], ALU.add))
                elif h % 2 == 1 and d == 1:
                    dve.wait_ge(applied, 4 * s + 4)
                    c = h // 2
                    dve.scalar_tensor_tensor(out=m.XT[:, 6 + c, :], in0=g.XC[:, c, :], scalar=m.CP[:, C_DS + c:C_DS + c + 1], in1=m.ps[6 + c][:, :],
                                             op0=ALU.mult, op1=ALU.add).then_inc(y_out, 1)
            dve.wait_ge(y_out, 2)


def mixer_norms(nc, m, mx, g):
    names = ("act_step", "dve_step", "y_squares", "y_sums", "y_inv", "h_squares", "h_var", "h_inv", "h_ready", "h_t")
    with stage(nc, "mixer_norms", *names) as (block, sems):
        act_step, dve_step, y_squares, y_sums, y_inv, h_squares, h_var, h_inv, h_ready, h_t = sems
        H = g.H[:, :, :, :].rearrange("p t h d -> p (t h) d")
        Hf = g.H[:, :, :, :].rearrange("p t h d -> p (t h d)")
        H2 = g.E[:, 0:2, :].rearrange("p a n -> p (a n)")
        mean = g.MEAN[:, 0, :]
        var = g.MEAN[:, 1, :]

        @block.vector
        def _(dve):
            link = Chain(dve, dve_step)
            Y = m.XT[:, 6:8, :].rearrange("p a n -> p (a n)")
            link(dve.tensor_tensor(Y, Y, mx.Z[:, :, :].rearrange("p a n -> p (a n)"), ALU.mult))
            dve.tensor_tensor(g.W[:, 0:2, :].rearrange("p a n -> p (a n)"), Y, Y, ALU.mult).then_inc(y_squares, 1)
            link(dve.reduce_sum(mean, H, AX.X))
            link(dve.tensor_scalar(mean, mean, 1.0 / 64, None, ALU.mult))
            link(dve.tensor_tensor(H, H, mean.rearrange("p (n a) -> p n a", a=1).to_broadcast([P, 16, 64]), ALU.subtract))
            link(dve.tensor_tensor(H2, Hf, Hf, ALU.mult))
            dve.reduce_sum(var, H2.rearrange("p (n d) -> p n d", d=64), AX.X).then_inc(h_var, 1)
            dve.wait_ge(y_inv, 2)
            for c in range(2):
                link(dve.scalar_tensor_tensor(out=m.XT[:, 6 + c, :], in0=m.XT[:, 6 + c, :], scalar=m.CP[:, C_SN + c:C_SN + c + 1],
                                              in1=g.RM[:, c, :], op0=ALU.mult, op1=ALU.mult))
            dve.wait_ge(h_inv, 1)
            link(dve.tensor_tensor(H, H, var.rearrange("p (n a) -> p n a", a=1).to_broadcast([P, 16, 64]), ALU.mult))
            H3 = g.H[:, :, :, :].rearrange("p t h d -> p t (h d)")
            link(dve.tensor_tensor(H3, H3, m.RP[:, R_MN:R_MN + 256].rearrange("p (a n) -> p a n", a=1).to_broadcast([P, NT, 256]), ALU.mult))
            dve.tensor_tensor(Hf, Hf, mx.O[:, :, :].rearrange("p t n -> p (t n)"), ALU.mult).then_inc(h_ready, 1)
            for c in range(2):
                dve.wait_ge(h_t, c + 1)
                link(dve.tensor_copy(m.XT[:, 4 + c, :], m.ps[2 + c][:, :]))

        @block.tensor
        def _(pe):
            pe.wait_ge(y_squares, 1)
            for c in range(2):
                pe.matmul(m.ps[c][:, :], m.ones[:, :], g.W[:, c, :], start=True, stop=True).then_inc(y_sums, 1)
            pe.wait_ge(h_ready, 1)
            H3 = g.H[:, :, :, :].rearrange("p t h d -> p t (h d)")
            for c in range(2):
                for t in range(NT):
                    last = pe.transpose(m.ps[2 + c][:, t * P:(t + 1) * P], H3[:, t, c * P:(c + 1) * P], m.ident[:, :])
                last.then_inc(h_t, 1)

        @block.scalar
        def _(act):
            link = Chain(act, act_step)
            for c in range(2):
                act.wait_ge(y_sums, c + 1)
                rstd(act, link, g.RM[:, c, :], m.ps[c][:, :], 1.0 / 128, 1e-6).then_inc(y_inv, 1)
            act.wait_ge(h_var, 1)
            rstd(act, link, var, var, 1.0 / 64, 1e-5).then_inc(h_inv, 1)


def norm_stage(nc, m, ln, which, layer, product=None):
    names = ("rows_in", "tile_done", "summed", "act_step", "dve_step", "var_ready", "inv_ready", "scaled", "pool_step")
    with stage(nc, "norm_stage", *names) as (block, sems):
        rows_in, tile_done, summed, act_step, dve_step, var_ready, inv_ready, scaled, pool_step = sems
        at = (R_L1, R_L2)[which]

        @block.sync
        def _(sp):
            sp.dma_start(ln.GB[:, :], m.d["rows"][bass.ds(layer, 1), at:at + 2 * D].to_broadcast([P, 2 * D])).then_inc(rows_in, 16)
            sp.wait_ge(rows_in, 16)

        @block.tensor
        def _(pe):
            if product:
                for half in range(2):
                    pe.wait_ge(m.ring_in[half], 48)
                for t in range(NT):
                    for half in range(2):
                        for k in range(KD):
                            last = pe.matmul(m.ps[2 * t + half][:, :], m.XT[:, k, t * P:(t + 1) * P],
                                             m.ring[:, half, k * S:(k + 1) * S], start=(k == 0), stop=(k == KD - 1))
                        last.then_inc(tile_done, 1)

        @block.vector
        def _(dve):
            link = Chain(dve, dve_step)
            for t in range(NT):
                for half in range(2):
                    cols = slice(half * S, (half + 1) * S)
                    if product:
                        dve.wait_ge(tile_done, 2 * t + half + 1)
                        y = m.ps[2 * t + half][:, :]
                    else:
                        y = ln.Y[:, t, cols]
                    link(dve.scalar_tensor_tensor(out=m.X[:, t, cols], in0=m.X[:, t, cols], scalar=ALPHA, in1=y, op0=ALU.mult, op1=ALU.add))
                    link(dve.bn_stats(ln.ST[:, t, half, :], m.X[:, t, cols]))
                link(dve.bn_aggr(ln.MV[:, t, :], ln.ST[:, t, :, :]))
                dve.sem_inc(var_ready, 1)
                dve.wait_ge(inv_ready, t + 1)
                link(dve.tensor_scalar(m.X[:, t, :], m.X[:, t, :], ln.MV[:, t, 0:1], ln.IV[:, t:t + 1], ALU.subtract, ALU.mult))
                if t == 0:
                    dve.wait_ge(rows_in, 16)
                link(dve.tensor_tensor(m.X[:, t, :], m.X[:, t, :], ln.GB[:, 0:D], ALU.mult))
                dve.sem_inc(scaled, 1)

        @block.scalar
        def _(act):
            link = Chain(act, act_step)
            for t in range(NT):
                act.wait_ge(var_ready, t + 1)
                rstd(act, link, ln.IV[:, t:t + 1], ln.MV[:, t, 1:2], 1.0, 1e-5).then_inc(inv_ready, 1)

        @block.gpsimd
        def _(pool):
            link = Chain(pool, pool_step)
            pool.wait_ge(rows_in, 16)
            for t in range(NT):
                pool.wait_ge(scaled, t + 1)
                link(pool.tensor_tensor(m.X[:, t, :], m.X[:, t, :], ln.GB[:, D:2 * D], ALU.add))


def router(nc, m, r):
    with stage(nc, "router", "logits_done", "dve_step", "exp_in", "exp_done") as (block, (logits_done, dve_step, exp_in, exp_done)):

        @block.tensor
        def _(pe):
            for t in range(NT):
                for k in range(KD):
                    last = pe.matmul(m.ps[0][:, t * 20:(t + 1) * 20], m.XT[:, k, t * P:(t + 1) * P], m.WR[:, k, :],
                                     start=(k == 0), stop=(k == KD - 1))
            last.then_inc(logits_done, 1)

        @block.vector
        def _(dve):
            link = Chain(dve, dve_step)

            def wide(x, n=4):
                return x.rearrange("p (t a) -> p t a", a=1).to_broadcast([P, NT, n])

            def first_max(hot, top, x):
                link(dve.reduce_max(top, x, AX.X))
                link(dve.tensor_tensor(hot, x, wide(top), ALU.is_equal))
                link(dve.tensor_tensor(hot, hot, m.CC[:, 4:8].rearrange("p (a n) -> p a n", a=1).to_broadcast([P, NT, 4]), ALU.mult))
                link(dve.reduce_max(r.t1[:, :], hot, AX.X))
                link(dve.tensor_tensor(hot, hot, wide(r.t1[:, :]), ALU.is_equal))

            lg = r.LG
            dve.wait_ge(logits_done, 1)
            link(dve.tensor_tensor(lg[:, :, :], m.ps[0][:, 0:80].rearrange("p (t n) -> p t n", t=NT),
                                   m.RP[:, R_RB:R_RB + 20].rearrange("p (a n) -> p a n", a=1).to_broadcast([P, NT, 20]), ALU.add))
            first_max(r.hg[:, :, :], r.gm[:, :], lg[:, :, 0:4])
            link(dve.tensor_tensor(r.e4[:, :, :], lg[:, :, 0:4], wide(r.gm[:, :]), ALU.subtract))
            for g in range(NGR):
                hot = r.hg[:, :, g:g + 1].to_broadcast([P, NT, 4])
                part = lg[:, :, 4 + 4 * g:8 + 4 * g]
                if g == 0:
                    link(dve.tensor_tensor(r.el[:, :, :], part, hot, ALU.mult))
                else:
                    link(dve.tensor_tensor(r.h2[:, :, :], part, hot, ALU.mult))
                    link(dve.tensor_tensor(r.el[:, :, :], r.el[:, :, :], r.h2[:, :, :], ALU.add))
            first_max(r.h1[:, :, :], r.m1[:, :], r.el[:, :, :])
            link(dve.scalar_tensor_tensor(out=r.el[:, :, :], in0=r.h1[:, :, :], scalar=NEG, in1=r.el[:, :, :], op0=ALU.mult, op1=ALU.add))
            first_max(r.h2[:, :, :], r.m2[:, :], r.el[:, :, :])
            link(dve.tensor_tensor(r.m2[:, :], r.m2[:, :], r.m1[:, :], ALU.subtract))
            dve.sem_inc(exp_in, 1)
            dve.wait_ge(exp_done, 2)
            link(dve.tensor_tensor(r.el[:, :, :], r.h1[:, :, :], r.h2[:, :, :], ALU.add))
            for g in range(NGR):
                link(dve.tensor_tensor(r.OH[:, :, 4 * g:4 * g + 4], r.el[:, :, :], r.hg[:, :, g:g + 1].to_broadcast([P, NT, 4]), ALU.mult))
            link(dve.reduce_sum(r.gm[:, :], r.e4[:, :, :], AX.X))
            link(dve.tensor_scalar(r.m1[:, :], r.m2[:, :], 1.0, None, ALU.add))
            link(dve.tensor_tensor(r.gm[:, :], r.gm[:, :], r.m1[:, :], ALU.mult))
            link(dve.reciprocal(r.gm[:, :], r.gm[:, :]))
            link(dve.tensor_tensor(r.m2[:, :], r.gm[:, :], r.m2[:, :], ALU.mult))
            link(dve.tensor_tensor(r.h1[:, :, :], r.h1[:, :, :], wide(r.gm[:, :]), ALU.mult))
            link(dve.tensor_tensor(r.h2[:, :, :], r.h2[:, :, :], wide(r.m2[:, :]), ALU.mult))
            link(dve.tensor_tensor(r.h1[:, :, :], r.h1[:, :, :], r.h2[:, :, :], ALU.add))
            for g in range(NGR):
                link(dve.tensor_tensor(r.COMB[:, :, 4 * g:4 * g + 4], r.h1[:, :, :], r.hg[:, :, g:g + 1].to_broadcast([P, NT, 4]), ALU.mult))

        @block.scalar
        def _(act):
            act.wait_ge(exp_in, 1)
            act.activation(r.e4[:, :, :], r.e4[:, :, :], ACT.Exp).then_inc(exp_done, 1)
            act.activation(r.m2[:, :], r.m2[:, :], ACT.Exp).then_inc(exp_done, 1)
            act.wait_ge(exp_done, 2)


def dispatch(nc, m, r):
    names = ("pe_rank", "pe_total", "dve_step", "x_hi", "x_lo", "act_step", "passes_out")
    with stage(nc, "dispatch", *names) as (block, (pe_rank, pe_total, dve_step, x_hi, x_lo, act_step, passes_out)):

        @block.tensor
        def _(pe):
            for t in range(NT):
                for u in range(t):
                    pe.matmul(m.ps[0][:, t * NE:(t + 1) * NE], m.ones[:, :], r.OH[:, u, :], start=(u == 0), stop=False)
                last = pe.matmul(m.ps[0][:, t * NE:(t + 1) * NE], r.TRI[:, :], r.OH[:, t, :], start=(t == 0), stop=True)
            last.then_inc(pe_rank, 1)
            for t in range(NT):
                last = pe.matmul(m.ps[1][:, 0:NE], m.ones[:, :], r.OH[:, t, :], start=(t == 0), stop=(t == NT - 1))
            last.then_inc(pe_total, 1)

        @block.vector
        def _(dve):
            link = Chain(dve, dve_step)
            dve.wait_ge(pe_rank, 1)
            link(dve.tensor_scalar(r.POS[:, :, :], r.OH[:, :, :], 10000.0, -10000.0, ALU.mult, ALU.add))
            link(dve.tensor_tensor(r.POS[:, :, :], r.POS[:, :, :], m.ps[0][:, 0:NT * NE].rearrange("p (t e) -> p t e", t=NT), ALU.add))
            dve.wait_ge(pe_total, 1)
            link(dve.reduce_max(r.NP[:, 0:1], m.ps[1][:, 0:NE], AX.X))
            link(dve.tensor_scalar(r.NP[:, 1:2], r.NP[:, 0:1], 128.0, 1.0, ALU.is_gt, ALU.add))
            for n in (256.0, 384.0):
                link(dve.tensor_scalar(r.NP[:, 2:3], r.NP[:, 0:1], n, None, ALU.is_gt))
                link(dve.tensor_tensor(r.NP[:, 1:2], r.NP[:, 1:2], r.NP[:, 2:3], ALU.add))
            link(dve.tensor_copy(r.NPI[:, :], r.NP[:, 1:2]))
            link(dve.tensor_copy(r.CW[:, :, :, 0], r.COMB[:, :, :]))
            link(dve.tensor_tensor(r.CW[:, :, :, 1], r.COMB[:, :, :], r.CW[:, :, :, 0].bitcast(F32), ALU.subtract))
            link(dve.memset(r.Y[:, :, :], 0.0))
            for t in range(2, NT):
                dve.wait_ge(x_hi, t + 1)
                link(dve.tensor_tensor(r.XL[:, t, :], m.X[:, t, :], r.XH[:, t, :].bitcast(F32), ALU.subtract))

        @block.scalar
        def _(act):
            for t in range(NT):
                act.copy(r.XH[:, t, :], m.X[:, t, :]).then_inc(x_hi, 1)

        @block.gpsimd
        def _(pool):
            for t in range(2):
                pool.wait_ge(x_hi, t + 1)
                pool.tensor_tensor(r.XL[:, t, :], m.X[:, t, :], r.XH[:, t, :].bitcast(F32), ALU.subtract).then_inc(x_lo, 1)
            pool.wait_ge(x_lo, 2)


def experts(nc, m, r, layer):
    GE = NE // NGR
    names = ("w_in0", "w_in1", "sel_ready", "sel_free", "gathered", "xe_act", "xe_dve", "weights_done", "dve_step", "selt_done", "selt_home",
             "gate_up", "silu_done", "hidden", "ht_done", "ht_home", "down", "ye_hi", "ye_home", "scattered", "added")
    with stage(nc, "experts", *names) as (block, sems):
        (w_in0, w_in1, sel_ready, sel_free, gathered, xe_act, xe_dve, weights_done, dve_step, selt_done, selt_home,
         gate_up, silu_done, hidden, ht_done, ht_home, down, ye_hi, ye_home, scattered, added) = sems
        w_in = (w_in0, w_in1)
        XE = m.XT

        def load(sp, n, b):
            sp.dma_start(m.ring[:, b, :], m.d["w_exp"][bass.ds(layer, 1), bass.ds(n, 1)].rearrange("a b p n -> p (a b n)")).then_inc(w_in[b], 16)

        @block.sync
        def _(sp):
            load(sp, 0, 0)
            load(sp, 1, 1)
            with sp.Fori(0, NE // 2 - 1) as i:
                for b in range(2):
                    sp.wait_ge(down, i * 4 + 2 * (b + 1))
                    load(sp, i * 2 + (b + 2), b)

        @block.tensor
        def _(pe):
            with pe.Fori(0, NGR) as g:

                def gate_up_of(e):
                    pe.wait_ge(w_in[e % 2], g * 32 + 16 * (e // 2 + 1))
                    if e >= 2:
                        pe.wait_ge(hidden, g * GE + e - 1)
                    for k in range(KD):
                        last = pe.matmul(m.ps[4 + e % 2][:, :], XE[:, k, e * P:(e + 1) * P], m.ring[:, e % 2, k * S:(k + 1) * S],
                                         start=(k == 0), stop=(k == KD - 1))
                    last.then_inc(gate_up, 1)

                def down_of(e):
                    pe.wait_ge(hidden, g * GE + e + 1)
                    for f in range(2):
                        last = pe.transpose(m.ps[6][:, f * P:(f + 1) * P], r.H[:, e % 2, f * P:(f + 1) * P], m.ident[:, :])
                    last.then_inc(ht_done, 1)
                    pe.wait_ge(ht_home, g * GE + e + 1)
                    if e == 0:
                        pe.wait_ge(selt_home, g * GE + GE)
                    for half in range(2):
                        if e:
                            pe.wait_ge(ye_home, g * 8 + 2 * (e - 1) + half + 1)
                        for f in range(2):
                            at = 4096 + f * D + half * S
                            last = pe.matmul(m.ps[2 + half][:, :], r.HT[:, f * P:(f + 1) * P], m.ring[:, e % 2, at:at + S], start=(f == 0), stop=(f == 1))
                        last.then_inc(down, 1)

                def scatter(pair):
                    pe.wait_ge(ye_home, g * 8 + 4 * (pair + 1))
                    for v in range(2 * NT):
                        t, half = divmod(v, 2)
                        pe.wait_ge(added, g * 16 + 8 * pair + v + 1)
                        n = 0
                        for e in range(2):
                            for part in range(2):
                                last = pe.matmul(m.ps[v % 2][:, :], r.SELT[:, 2 * pair + e, t * P:(t + 1) * P],
                                                 r.YE[:, part, e, half * S:(half + 1) * S], start=(n == 0), stop=(n == 3))
                                n += 1
                        last.then_inc(scattered, 1)

                pe.wait_ge(sel_ready, g * NT + NT)
                for k in range(KD):
                    if k < 2:
                        pe.wait_ge(added, g * 16 + k + 1)
                    else:
                        pe.wait_ge((xe_act, xe_dve)[k % 2], g * 4 + k // 2)
                    n = 0
                    for t in range(NT):
                        for part in (r.XH, r.XL):
                            last = pe.matmul(m.ps[k % 2][:, :], part[:, t, k * P:(k + 1) * P], r.SEL[:, t, :], start=(n == 0), stop=(n == 7))
                            n += 1
                    last.then_inc(gathered, 1)
                for e in range(GE):
                    for t in range(NT):
                        last = pe.matmul(m.ps[7][:, 2 * e:2 * e + 2], r.SEL[:, t, e * P:(e + 1) * P],
                                         r.CW[:, t, bass.ds(g * GE + e, 1), :].rearrange("p a b -> p (a b)"), start=(t == 0), stop=(t == NT - 1))
                last.then_inc(weights_done, 1)
                for e in range(GE):
                    if e >= 2:
                        pe.wait_ge(selt_home, g * GE + e - 1)
                    for t in range(NT):
                        last = pe.transpose(m.ps[2 + e % 2][:, t * P:(t + 1) * P], r.SEL[:, t, e * P:(e + 1) * P].bitcast(F32), m.ident[:, :])
                    last.then_inc(selt_done, 1)
                pe.wait_ge(xe_act, g * 4 + 4)
                pe.wait_ge(xe_dve, g * 4 + 4)
                gate_up_of(0)
                gate_up_of(1)
                down_of(0)
                gate_up_of(2)
                down_of(1)
                gate_up_of(3)
                scatter(0)
                down_of(2)
                down_of(3)
                scatter(1)

        @block.scalar
        def _(act):
            with act.Fori(0, NGR) as g:

                def silu(e):
                    act.wait_ge(gate_up, g * GE + e + 1)
                    act.activation(r.SG[:, e % 2, :], m.ps[4 + e % 2][:, 0:FE], ACT.Silu).then_inc(silu_done, 1)

                def home(e):
                    act.wait_ge(ht_done, g * GE + e + 1)
                    act.copy(r.HT[:, :], m.ps[6][:, 0:2 * P]).then_inc(ht_home, 1)
                    for half in range(2):
                        act.wait_ge(down, g * 8 + 2 * e + half + 1)
                        act.copy(r.YE[:, 0, e % 2, half * S:(half + 1) * S], m.ps[2 + half][:, :]).then_inc(ye_hi, 1)

                for k in range(0, KD, 2):
                    act.wait_ge(gathered, g * KD + k + 1)
                    act.copy(XE[:, k, :], m.ps[0][:, :]).then_inc(xe_act, 1)
                for e in range(GE):
                    act.wait_ge(selt_done, g * GE + e + 1)
                    if e == GE - 1:
                        act.sem_inc(sel_free, 1)
                    act.copy(r.SELT[:, e, :], m.ps[2 + e % 2][:, :]).then_inc(selt_home, 1)
                silu(0)
                silu(1)
                home(0)
                silu(2)
                home(1)
                silu(3)
                home(2)
                home(3)

        @block.vector
        def _(dve):
            dve.sem_inc(added, 2)
            dve.sem_inc(sel_free, 1)
            with dve.Fori(0, NGR) as g:

                def hidden_of(e):
                    dve.wait_ge(silu_done, g * GE + e + 1)
                    dve.scalar_tensor_tensor(out=r.H[:, e % 2, :], in0=m.ps[4 + e % 2][:, FE:2 * FE], scalar=r.WS[:, e:e + 1],
                                             in1=r.SG[:, e % 2, :], op0=ALU.mult, op1=ALU.mult).then_inc(hidden, 1)

                def low_part(e):
                    for half in range(2):
                        cols = slice(half * S, (half + 1) * S)
                        dve.wait_ge(ye_hi, g * 8 + 2 * e + half + 1)
                        dve.tensor_tensor(r.YE[:, 1, e % 2, cols], m.ps[2 + half][:, :], r.YE[:, 0, e % 2, cols].bitcast(F32),
                                          ALU.subtract).then_inc(ye_home, 1)

                def add(pair):
                    for v in range(2 * NT):
                        t, cols = v // 2, slice((v % 2) * S, (v % 2 + 1) * S)
                        dve.wait_ge(scattered, g * 16 + 8 * pair + v + 1)
                        dve.wait_ge(added, g * 16 + 8 * pair + v + 2)
                        dve.tensor_tensor(r.Y[:, t, cols], r.Y[:, t, cols], m.ps[v % 2][:, :], ALU.add).then_inc(added, 1)

                dve.wait_ge(sel_free, g + 1)
                for t in range(NT):
                    for e in range(GE):
                        last = dve.tensor_scalar(r.SEL[:, t, e * P:(e + 1) * P], r.IOTA[:, :], r.POS[:, t, bass.ds(g * GE + e, 1)], None, ALU.is_equal)
                    last.then_inc(sel_ready, 1)
                for k in range(1, KD, 2):
                    dve.wait_ge(gathered, g * KD + k + 1)
                    dve.tensor_copy(XE[:, k, :], m.ps[1][:, :]).then_inc(xe_dve, 1)
                dve.wait_ge(weights_done, g + 1)
                dve.reduce_sum(r.WS[:, :], m.ps[7][:, 0:2 * GE].rearrange("p (e a) -> p e a", a=2), AX.X).then_inc(dve_step, 1)
                dve.wait_ge(dve_step, g + 1)
                hidden_of(0)
                hidden_of(1)
                low_part(0)
                hidden_of(2)
                low_part(1)
                hidden_of(3)
                add(0)
                low_part(2)
                low_part(3)
                add(1)


def next_pass(nc, r):
    with stage(nc, "next_pass", "moved") as (block, (moved,)):

        @block.vector
        def _(dve):
            dve.tensor_scalar(r.POS[:, :, :], r.POS[:, :, :], -float(P), None, ALU.add).then_inc(moved, 1)
            dve.wait_ge(moved, 1)


GH, GD = 4, 128
FF = 4096
K_NM, K_NP, K_GC, K_LC, K_LB, K_AB, K_XB, K_AP, K_GN, K_AL, K_DB, K_N = 0, 8, 16, 64, 80, 84, 88, 92, 96, 97, 98, 99


def rms_transpose(nc, m, n, gain, extra=None):
    names = ("squared", "inv", "act_step", "dve_step", "normed", "transposed", "xt_act", "xt_dve", "param_in")
    with stage(nc, "rms_transpose", *names) as (block, (squared, inv, act_step, dve_step, normed, transposed, xt_act, xt_dve, param_in)):

        @block.sync
        def _(sp):
            if extra:
                sp.wait_ge(param_in, 16 * extra(sp, param_in))

        @block.scalar
        def _(act):
            link = Chain(act, act_step)
            for t in range(NT):
                link(act.activation(n.XN[:, t, :], m.X[:, t, :], ACT.Square, accum_out=n.SS[:, t:t + 1]))
            rstd(act, link, n.SS[:, :], n.SS[:, :], 1.0 / D, 1e-6).then_inc(inv, 1)
            if extra:
                act.wait_ge(param_in, 16)
            for k in range(0, KD, 2):
                act.wait_ge(transposed, k + 1)
                act.activation(m.XT[:, k, :], m.ps[k][:, :], ACT.Copy, scale=m.CP[:, gain + k:gain + k + 1]).then_inc(xt_act, 1)
            act.wait_ge(xt_act, KD // 2)

        @block.vector
        def _(dve):
            dve.wait_ge(inv, 1)
            for t in range(NT):
                dve.tensor_scalar(n.XN[:, t, :], m.X[:, t, :], n.SS[:, t:t + 1], None, ALU.mult).then_inc(normed, 1)
            if extra:
                dve.wait_ge(param_in, 16)
            for k in range(1, KD, 2):
                dve.wait_ge(transposed, k + 1)
                dve.tensor_scalar(m.XT[:, k, :], m.ps[k][:, :], m.CP[:, gain + k:gain + k + 1], None, ALU.mult).then_inc(xt_dve, 1)
            dve.wait_ge(xt_dve, KD // 2)

        @block.tensor
        def _(pe):
            for k in range(KD):
                for t in range(NT):
                    if k == 0:
                        pe.wait_ge(normed, t + 1)
                    last = pe.transpose(m.ps[k][:, t * P:(t + 1) * P], n.XN[:, t, k * P:(k + 1) * P], m.ident[:, :])
                last.then_inc(transposed, 1)


def in_projection_2(nc, m, b, q):
    names = ("unit_done", "home_act", "home_dve", "w_in0", "w_in1", "w_in2")
    with stage(nc, "in_projection_2", *names) as (block, (unit_done, home_act, home_dve, *ring_in)):
        homes = [q.QB[:, c, 3:3 + S] for c in range(12)] + [b.Z[:, c, :] for c in range(4)]
        homes += [b.LX[:, c, 3:3 + S] for c in range(4)] + [b.LG[:, c, :] for c in range(4)]
        NU = len(homes) + 1

        @block.sync
        def _(sp):
            for i in range(6):
                if i >= RING:
                    sp.wait_ge(unit_done, 4 * (i - RING + 1))
                n = 4416 if i == 5 else 4096
                sp.dma_start(q.ring[:, i % RING, 0:n], m.d["w_in_2"][i, :, 0:n]).then_inc(ring_in[i % RING], 16)

        @block.tensor
        def _(pe):
            for u in range(NU):
                load = min(u // 4, 5)
                if u % 4 == 0 and u < 24:
                    pe.wait_ge(ring_in[load % RING], 16 * (load // RING + 1))
                if u >= 8:
                    pe.wait_ge((home_act, home_dve)[u % 2], (u - 8) // 2 + 1)
                for k in range(KD):
                    at, n = ((u % 4) * P + k * S, P) if u < 24 else (4096 + k * GR, GR)
                    last = pe.matmul(m.ps[u % 8][0:n, :], q.ring[:, load % RING, at:at + n], m.XT[:, k, :], start=(k == 0), stop=(k == KD - 1))
                last.then_inc(unit_done, 1)

        @block.scalar
        def _(act):
            for u in range(0, NU, 2):
                act.wait_ge(unit_done, u + 1)
                if u < 24:
                    act.copy(homes[u], m.ps[u % 8][:, :]).then_inc(home_act, 1)
                else:
                    act.copy(b.GR[0:GR, :], m.ps[u % 8][0:GR, :]).then_inc(home_act, 1)
            act.wait_ge(home_act, (NU + 1) // 2)

        @block.vector
        def _(dve):
            for u in range(1, NU, 2):
                dve.wait_ge(unit_done, u + 1)
                dve.tensor_copy(homes[u], m.ps[u % 8][:, :]).then_inc(home_dve, 1)
            dve.wait_ge(home_dve, NU // 2)

        @block.gpsimd
        def _(pool):
            pool.memset(q.QB[:, :, 0:3], 0.0)
            pool.memset(b.LX[:, :, 0:3], 0.0)


def gdn_prepare(nc, m, b, q):
    names = ("act_step", "dve_step", "conv_done", "silu_done", "squares", "sums", "inv", "biased", "abs_ready", "log_ready",
             "rows_a", "rows_b", "rows_c", "rows_t")
    with stage(nc, "gdn_prepare", *names) as (block, sems):
        act_step, dve_step, conv_done, silu_done, squares, sums, inv, biased, abs_ready, log_ready, rows_a, rows_b, rows_c, rows_t = sems
        R = slice(0, GH)

        @block.vector
        def _(dve):
            link = Chain(dve, dve_step)
            dve.wait_ge(biased, 1)
            dve.scalar_tensor_tensor(out=b.G1[R, :], in0=b.GR[R, :], scalar=-1.0, in1=b.GR[R, :], op0=ALU.mult, op1=ALU.min).then_inc(abs_ready, 1)
            dve.wait_ge(log_ready, 1)
            link(dve.scalar_tensor_tensor(out=b.G1[R, :], in0=b.GR[R, :], scalar=0.0, in1=b.G1[R, :], op0=ALU.max, op1=ALU.add))
            link(dve.tensor_scalar(b.G1[R, :], b.G1[R, :], b.CO[R, 0:1], None, ALU.mult))
            for c in range(NT):
                at = slice(c * P, (c + 1) * P)
                link(dve.tensor_tensor_scan(b.GC[R, at], m.zeros[R, at], b.G1[R, at], 0.0, ALU.add, ALU.add))
            link(dve.tensor_scalar(b.GM[R, :], b.GC[R, :], -1.0, None, ALU.mult))
            last_of_chunk = b.GC[R, :].rearrange("p (c n) -> p c n", c=NT)[:, :, P - 1:P].to_broadcast([GH, NT, P])
            link(dve.tensor_tensor(b.G1[R, :].rearrange("p (c n) -> p c n", c=NT), last_of_chunk,
                                   b.GC[R, :].rearrange("p (c n) -> p c n", c=NT), ALU.subtract))
            dve.sem_inc(rows_a, 1)
            dve.wait_ge(rows_b, 1)
            link(dve.tensor_tensor(b.BE[R, :], b.BT[R, :], b.EG[R, :], ALU.mult))
            dve.sem_inc(rows_c, 1)
            for c in range(12):
                for tap in range(4):
                    w = m.CP[:, K_GC + 4 * c + tap:K_GC + 4 * c + tap + 1]
                    src = q.QB[:, c, tap:tap + S]
                    if tap == 0:
                        link(dve.tensor_scalar(b.XC[:, c, :], src, w, None, ALU.mult))
                    else:
                        link(dve.scalar_tensor_tensor(out=b.XC[:, c, :], in0=src, scalar=w, in1=b.XC[:, c, :], op0=ALU.mult, op1=ALU.add))
                dve.sem_inc(conv_done, 1)
                if c == 0:
                    dve.wait_ge(rows_t, 1)
                    link(dve.tensor_copy(b.GN[:, :], m.ps[7][:, 0:64]))
            for c in range(8):
                if c >= 2:
                    dve.wait_ge(sums, c - 1)
                dve.wait_ge(silu_done, c + 1)
                dve.tensor_tensor(q.SQ[:, c % 2, :], b.XC[:, c, :], b.XC[:, c, :], ALU.mult).then_inc(squares, 1)
            for c in range(8):
                dve.wait_ge(inv, c + 1)
                link(dve.scalar_tensor_tensor(out=b.XC[:, c, :], in0=b.XC[:, c, :], scalar=(GD ** -0.5 if c < 4 else 1.0),
                                              in1=q.RS[:, c, :], op0=ALU.mult, op1=ALU.mult))

        @block.scalar
        def _(act):
            link = Chain(act, act_step)
            link(act.activation(b.BT[R, :], b.GR[32:32 + GH, :], ACT.Sigmoid))
            link(act.activation(b.CO[R, 0:1], m.CP[R, K_AL:K_AL + 1], ACT.Exp))
            link(act.mul(b.CO[R, 0:1], b.CO[R, 0:1], -1.0))
            link(act.activation(b.GR[R, :], b.GR[R, :], ACT.Identity, bias=m.CP[R, K_DB:K_DB + 1]))
            act.sem_inc(biased, 1)
            act.wait_ge(abs_ready, 1)
            link(act.activation(b.G1[R, :], b.G1[R, :], ACT.Exp))
            act.activation(b.G1[R, :], b.G1[R, :], ACT.Ln, bias=1.0).then_inc(log_ready, 1)
            act.wait_ge(rows_a, 1)
            link(act.activation(b.EG[R, :], b.GC[R, :], ACT.Exp))
            link(act.activation(b.DK[R, :], b.G1[R, :], ACT.Exp))
            act.sem_inc(rows_b, 1)
            for c in range(12):
                act.wait_ge(conv_done, c + 1)
                act.activation(b.XC[:, c, :], b.XC[:, c, :], ACT.Silu).then_inc(silu_done, 1)
            for c in range(8):
                act.wait_ge(sums, c + 1)
                rstd(act, link, q.RS[:, c, :], m.ps[c % 2][:, :], 1.0, 1e-6).then_inc(inv, 1)
            act.wait_ge(silu_done, 12)

        @block.tensor
        def _(pe):
            pe.wait_ge(rows_c, 1)
            for n, rows in enumerate((b.GM, b.BT, b.BE, b.DK)):
                for t in range(NT):
                    at = (n * NT + t) * GH
                    last = pe.transpose(m.ps[7][:, at:at + GH], rows[R, t * P:(t + 1) * P], m.ident[0:GH, 0:GH])
            last.then_inc(rows_t, 1)
            for c in range(8):
                pe.wait_ge(squares, c + 1)
                if c >= 2:
                    pe.wait_ge(inv, c - 1)
                pe.matmul(m.ps[c % 2][:, :], m.ones[:, :], q.SQ[:, c % 2, :], start=True, stop=True).then_inc(sums, 1)


def gdn_matrices(nc, m, b, w):
    names = ("dve_step", "nat_done", "nat_home", "row_done", "row_used", "masked", "decay", "tri_done", "tri_home", "ready")
    with stage(nc, "gdn_matrices", *names) as (block, sems):
        dve_step, nat_done, nat_home, row_done, row_used, masked, decay, tri_done, tri_home, ready = sems
        rows = [b.GC, b.BT, b.EG]

        @block.sync
        def _(sp):
            sp.dma_start(w.LM[:, :, :], m.d["level_masks"]).then_inc(ready, 16)
            sp.wait_ge(ready, 16)

        @block.tensor
        def _(pe):
            for c in range(NT):
                for x in range(2):
                    if c >= 2:
                        pe.wait_ge(nat_home, 2 * (c - 2) + x + 1)
                    for h in range(GH):
                        last = pe.transpose(m.ps[2 * x + c % 2][:, h * P:(h + 1) * P], b.XC[:, 4 * (x + 1) + h, c * P:(c + 1) * P], m.ident[:, :])
                    last.then_inc(nat_done, 1)
            for h in range(GH):
                for n in range(3):
                    i = 3 * h + n
                    if i >= 4:
                        pe.wait_ge(row_used, i - 3)
                    pe.matmul(m.ps[4 + i % 4][:, :], m.ident[0:GH, h:h + 1].to_broadcast([GH, P]), rows[n][0:GH, :], start=True, stop=True).then_inc(row_done, 1)
            pe.wait_ge(row_used, 12)
            pe.wait_ge(nat_home, 8)
            for c in range(NT):
                at = slice(c * P, (c + 1) * P)
                for x, right in enumerate((w.KB, None)):
                    i = 2 * c + x
                    if i >= 4:
                        pe.wait_ge(tri_home, i - 3)
                    for h in range(GH):
                        rhs = w.KB[:, h, at] if x == 0 else b.XC[:, h, at]
                        last = pe.matmul(m.ps[i % 4][:, h * P:(h + 1) * P], b.XC[:, 4 + h, at], rhs, start=True, stop=True)
                    last.then_inc(tri_done, 1)

        @block.vector
        def _(dve):
            link = Chain(dve, dve_step)

            def per_head(kind, c):
                at = (kind * NT + c) * GH
                return b.GN[:, at:at + GH].rearrange("p (h a) -> p h a", a=1).to_broadcast([P, GH, P])

            for c in range(NT):
                dve.wait_ge(nat_done, 2 * c + 1)
                k = m.ps[c % 2][:, :].rearrange("p (h n) -> p h n", h=GH)
                link(dve.tensor_tensor(w.KE[:, c, :, :], k, per_head(2, c), ALU.mult))
                dve.tensor_tensor(w.KD[:, c, :, :], k, per_head(3, c), ALU.mult).then_inc(nat_home, 1)
                dve.wait_ge(nat_done, 2 * c + 2)
                v = m.ps[2 + c % 2][:, :].rearrange("p (h n) -> p h n", h=GH)
                dve.tensor_tensor(w.VB[:, c, :, :], v, per_head(1, c), ALU.mult).then_inc(nat_home, 1)
            for h in range(GH):
                i = 3 * h
                dve.wait_ge(row_done, i + 1)
                dve.tensor_tensor(blocks(w.RM[:, h, :]), blocks(m.ps[4 + i % 4][:, :]), every_block(m.mask[:, 0, :]), ALU.add).then_inc(row_used, 1)
                dve.wait_ge(row_done, i + 2)
                dve.tensor_tensor(w.KB[:, h, :], m.ps[4 + (i + 1) % 4][:, :], b.XC[:, 4 + h, :], ALU.mult).then_inc(row_used, 1)
                dve.wait_ge(row_done, i + 3)
                link(dve.tensor_tensor(w.QE[:, h, :], m.ps[4 + (i + 2) % 4][:, :], b.XC[:, h, :], ALU.mult))
                dve.tensor_copy(w.GL[:, h, :], m.ps[4 + (i + 2) % 4][:, P - 1:S:P]).then_inc(row_used, 1)
            for c in range(NT):
                dve.wait_ge(decay, GH * NT)
                for x, out in enumerate((w.AT, w.AQ)):
                    dve.wait_ge(tri_done, 2 * c + x + 1)
                    dve.tensor_tensor(out[:, c, :, :].rearrange("p h n -> p (h n)"), m.ps[(2 * c + x) % 4][:, :],
                                      w.E[:, c, :, :].rearrange("p h n -> p (h n)"), ALU.mult).then_inc(tri_home, 1)
            for c in range(NT):
                for out in (w.T, w.U):
                    link(dve.tensor_copy(out[:, c, :, :], m.ident[:, :].rearrange("p (a n) -> p a n", a=1).to_broadcast([P, GH, P])))
            dve.wait_ge(tri_home, 8)

        @block.scalar
        def _(act):
            for h in range(GH):
                act.wait_ge(row_used, 3 * h + 1)
                for c in range(NT):
                    act.activation(w.E[:, c, h, :], w.RM[:, h, c * P:(c + 1) * P], ACT.Exp, bias=b.GN[:, c * GH + h:c * GH + h + 1]).then_inc(decay, 1)


def gdn_inverse(nc, m, w):
    LEVELS = 7
    with stage(nc, "gdn_inverse", "z_done", "z_home", "t_done", "u_done", "tu_home") as (block, (z_done, z_home, t_done, u_done, tu_home)):

        @block.tensor
        def _(pe):
            with pe.Fori(0, LEVELS) as level:
                for c in range(NT):
                    pe.wait_ge(tu_home, level * 8 + 2 * c + 2)
                    for h in range(GH):
                        last = pe.matmul(m.ps[c][:, h * P:(h + 1) * P], w.AT[:, c, h, :], w.T[:, c, h, :], start=True, stop=True)
                    last.then_inc(z_done, 1)
                for c in range(NT):
                    pe.wait_ge(z_home, level * NT + c + 1)
                    for h in range(GH):
                        last = pe.matmul(m.ps[4 + c][:, h * P:(h + 1) * P], w.U[:, c, h, :], w.Z[:, c, h, :], start=True, stop=True)
                    last.then_inc(t_done, 1)
                    for h in range(GH):
                        last = pe.matmul(m.ps[c][:, h * P:(h + 1) * P], w.Z[:, c, h, :], w.U[:, c, h, :], start=True, stop=True)
                    last.then_inc(u_done, 1)

        @block.vector
        def _(dve):
            dve.sem_inc(tu_home, 8)
            with dve.Fori(0, LEVELS) as level:
                for c in range(NT):
                    dve.wait_ge(z_done, level * NT + c + 1)
                    mask = w.LM[:, bass.ds(level, 1), :].to_broadcast([P, GH, P])
                    dve.tensor_tensor(w.Z[:, c, :, :], m.ps[c][:, :].rearrange("p (h n) -> p h n", h=GH), mask, ALU.mult).then_inc(z_home, 1)
                for c in range(NT):
                    for x, (done, bank, out) in enumerate(((t_done, 4 + c, w.T), (u_done, c, w.U))):
                        dve.wait_ge(u_done, level * NT + c + 1)
                        flat = out[:, c, :, :].rearrange("p h n -> p (h n)")
                        dve.tensor_tensor(flat, flat, m.ps[bank][:, :], ALU.add).then_inc(tu_home, 1)


def gdn_sequence(nc, m, b, w):
    with stage(nc, "gdn_sequence", "w_done", "w_home", "v_done", "v_home", "o_done", "o_home", "s_done", "s_home", "dve_step") as (block, sems):
        w_done, w_home, v_done, v_home, o_done, o_home, s_done, s_home, dve_step = sems

        @block.tensor
        def _(pe):
            for c in range(1, NT):
                for h in range(GH):
                    last = pe.matmul(m.ps[c][:, h * P:(h + 1) * P], w.KE[:, c, h, :], w.U[:, c, h, :], start=True, stop=True)
                last.then_inc(w_done, 1)
            for c in range(NT):
                at = slice(c * P, (c + 1) * P)
                if c:
                    pe.wait_ge(w_home, c)
                    pe.wait_ge(s_home, c)
                    pe.wait_ge(v_home, c)
                for h in range(GH):
                    last = pe.matmul(m.ps[4][:, h * P:(h + 1) * P], w.U[:, c, h, :], w.VB[:, c, h, :], start=True, stop=(c == 0))
                    if c:
                        last = pe.matmul(m.ps[4][:, h * P:(h + 1) * P], w.NW[:, c, h, :], w.S[:, h, :], start=False, stop=True)
                last.then_inc(v_done, 1)
                pe.wait_ge(v_home, c + 1)
                if c:
                    pe.wait_ge(o_home, c)
                for h in range(GH):
                    if c:
                        pe.matmul(m.ps[5][:, h * P:(h + 1) * P], w.S[:, h, :], w.QE[:, h, at], start=True, stop=False)
                    last = pe.matmul(m.ps[5][:, h * P:(h + 1) * P], w.VN[:, h, :], w.AQ[:, c, h, :], start=(c == 0), stop=True)
                last.then_inc(o_done, 1)
                if c < NT - 1:
                    for h in range(GH):
                        last = pe.matmul(m.ps[6][:, h * P:(h + 1) * P], w.KD[:, c, h, :], w.VN[:, h, :], start=True, stop=True)
                    last.then_inc(s_done, 1)

        @block.vector
        def _(dve):
            link = Chain(dve, dve_step)
            for c in range(NT):
                dve.wait_ge(v_done, c + 1)
                if c:
                    dve.wait_ge(s_done, c)
                dve.tensor_copy(w.VN[:, :, :].rearrange("p h n -> p (h n)"), m.ps[4][:, :]).then_inc(v_home, 1)
                if c < NT - 1:
                    S_ = w.S[:, :, :].rearrange("p h n -> p (h n)")
                    dve.wait_ge(s_done, c + 1)
                    if c == 0:
                        dve.tensor_copy(S_, m.ps[6][:, :]).then_inc(s_home, 1)
                        dve.wait_ge(s_home, 1)
                    else:
                        link(dve.tensor_tensor(w.S[:, :, :], w.S[:, :, :], w.GL[:, :, c:c + 1].to_broadcast([P, GH, P]), ALU.mult))
                        dve.tensor_tensor(S_, S_, m.ps[6][:, :], ALU.add).then_inc(s_home, 1)
                        dve.wait_ge(s_home, c + 1)

        @block.scalar
        def _(act):
            for c in range(1, NT):
                act.wait_ge(w_done, c)
                act.mul(w.NW[:, c, :, :].rearrange("p h n -> p (h n)"), m.ps[c][:, :], -1.0).then_inc(w_home, 1)
            for c in range(NT):
                act.wait_ge(o_done, c + 1)
                act.copy(w.OT[:, :, c * P:(c + 1) * P], m.ps[5][:, :].rearrange("p (h n) -> p h n", h=GH)).then_inc(o_home, 1)
            act.wait_ge(o_home, NT)


def gdn_norm(nc, m, b, w):
    with stage(nc, "gdn_norm", "act_step", "dve_step", "squares", "sums", "inv", "silu_done") as (block, sems):
        act_step, dve_step, squares, sums, inv, silu_done = sems

        @block.vector
        def _(dve):
            link = Chain(dve, dve_step)
            for h in range(GH):
                dve.tensor_tensor(w.KB[:, h, :], w.OT[:, h, :], w.OT[:, h, :], ALU.mult).then_inc(squares, 1)
            for h in range(GH):
                dve.wait_ge(inv, h + 1)
                dve.wait_ge(silu_done, h + 1)
                link(dve.scalar_tensor_tensor(out=w.OT[:, h, :], in0=w.OT[:, h, :], scalar=m.CP[:, K_GN:K_GN + 1], in1=w.QE[:, h, :],
                                              op0=ALU.mult, op1=ALU.mult))
                link(dve.tensor_tensor(m.XT[:, h, :], w.OT[:, h, :], b.Z[:, h, :], ALU.mult))

        @block.tensor
        def _(pe):
            for h in range(GH):
                pe.wait_ge(squares, h + 1)
                pe.matmul(m.ps[h][:, :], m.ones[:, :], w.KB[:, h, :], start=True, stop=True).then_inc(sums, 1)

        @block.scalar
        def _(act):
            link = Chain(act, act_step)
            for h in range(GH):
                act.activation(b.Z[:, h, :], b.Z[:, h, :], ACT.Silu).then_inc(silu_done, 1)
            for h in range(GH):
                act.wait_ge(sums, h + 1)
                rstd(act, link, w.QE[:, h, :], m.ps[h][:, :], 1.0 / GD, 1e-6).then_inc(inv, 1)


def lru(nc, m, b, u):
    names = ("act_step", "dve_step", "gate_w_in", "conv_done", "gates_done", "gates_home", "decay_arg", "decay_done", "root_arg", "root_done", "gelu_done")
    with stage(nc, "lru", *names) as (block, sems):
        act_step, dve_step, gate_w_in, conv_done, gates_done, gates_home, decay_arg, decay_done, root_arg, root_done, gelu_done = sems

        @block.sync
        def _(sp):
            sp.dma_start(u.WA[:, :, :], m.d["lru_w"]).then_inc(gate_w_in, 16)
            sp.wait_ge(gate_w_in, 16)

        @block.vector
        def _(dve):
            link = Chain(dve, dve_step)
            for c in range(4):
                for tap in range(4):
                    w = m.CP[:, K_LC + 4 * c + tap:K_LC + 4 * c + tap + 1]
                    src = b.LX[:, c, tap:tap + S]
                    if tap == 0:
                        link(dve.tensor_scalar(u.XR[:, c, :], src, w, m.CP[:, K_LB + c:K_LB + c + 1], ALU.mult, ALU.add))
                    else:
                        link(dve.scalar_tensor_tensor(out=u.XR[:, c, :], in0=src, scalar=w, in1=u.XR[:, c, :], op0=ALU.mult, op1=ALU.add))
                dve.sem_inc(conv_done, 1)
            for c in range(4):
                dve.wait_ge(gates_home, 2 * c + 3)
                dve.tensor_scalar(u.RG[:, c, :], u.RG[:, c, :], u.SPA[:, c:c + 1], None, ALU.mult).then_inc(decay_arg, 1)
            for c in range(4):
                dve.wait_ge(decay_done, 2 * c + 2)
                link(dve.tensor_scalar(u.TH[:, 1, :], u.RT[:, c, :], 1.0, None, ALU.add))
                link(dve.reciprocal(u.TH[:, 1, :], u.TH[:, 1, :]))
                dve.scalar_tensor_tensor(out=u.RT[:, c, :], in0=u.RT[:, c, :], scalar=2.0, in1=u.TH[:, 1, :], op0=ALU.mult, op1=ALU.mult).then_inc(root_arg, 1)
                link(dve.tensor_tensor(u.XR[:, c, :], u.XR[:, c, :], u.IG[:, c, :], ALU.mult))
            for c in range(4):
                dve.wait_ge(root_done, c + 1)
                link(dve.tensor_tensor(u.XR[:, c, :], u.XR[:, c, :], u.RT[:, c, :], ALU.mult))
                link(dve.tensor_tensor_scan(u.RT[:, c, :], u.RG[:, c, :], u.XR[:, c, :], 0.0, ALU.mult, ALU.add))
                dve.wait_ge(gelu_done, c + 1)
                link(dve.tensor_tensor(m.XT[:, 4 + c, :], u.RT[:, c, :], b.LG[:, c, :], ALU.mult))

        @block.tensor
        def _(pe):
            pe.wait_ge(gate_w_in, 16)
            for c in range(4):
                pe.wait_ge(conv_done, c + 1)
                for x in range(2):
                    for half in range(2):
                        rows = slice(64 * half, 64 * half + 64)
                        last = pe.matmul(m.ps[2 * c + x][rows, :], u.WA[rows, 2 * c + x, :], u.XR[rows, c, :], start=True, stop=True)
                    last.then_inc(gates_done, 1)

        @block.scalar
        def _(act):
            link = Chain(act, act_step)
            a = m.CP[:, K_AP:K_AP + 4]
            link(act.activation(u.AB[:, 0:4], a, ACT.Abs))
            link(act.activation(u.AB[:, 0:4], u.AB[:, 0:4], ACT.Exp, scale=-1.0))
            link(act.activation(u.AB[:, 0:4], u.AB[:, 0:4], ACT.Ln, bias=1.0))
            link(act.activation(u.AB[:, 4:8], a, ACT.Relu, scale=-1.0))
            for c in range(4):
                link(act.activation(u.AB[:, c:c + 1], u.AB[:, c:c + 1], ACT.Identity, bias=u.AB[:, 4 + c:5 + c]))
            act.activation(u.SPA[:, :], u.AB[:, 0:4], ACT.Copy, scale=8.0).then_inc(gates_home, 1)
            for c in range(4):
                for x, out in enumerate((u.RG, u.IG)):
                    act.wait_ge(gates_done, 2 * c + x + 1)
                    at = (K_AB, K_XB)[x] + c
                    act.activation(out[:, c, :], m.ps[2 * c + x][:, :], ACT.Sigmoid, bias=m.CP[:, at:at + 1]).then_inc(gates_home, 1)
            for c in range(4):
                act.wait_ge(decay_arg, c + 1)
                act.activation(u.RT[:, c, :], u.RG[:, c, :], ACT.Tanh).then_inc(decay_done, 1)
                act.wait_ge(decay_done, 2 * c + 1)
                act.activation(u.RG[:, c, :], u.RG[:, c, :], ACT.Exp, scale=-1.0).then_inc(decay_done, 1)
            for c in range(4):
                act.wait_ge(root_arg, c + 1)
                act.activation(u.RT[:, c, :], u.RT[:, c, :], ACT.Sqrt).then_inc(root_done, 1)
            for c in range(4):
                act.activation(b.LG[:, c, :], b.LG[:, c, :], ACT.Gelu_apprx_tanh).then_inc(gelu_done, 1)


def out_projection_2(nc, m, f):
    with stage(nc, "out_projection_2", "w_arrived", "tile_done", "summed") as (block, (w_arrived, tile_done, summed)):

        @block.sync
        def _(sp):
            for half in range(2):
                sp.dma_start(f.ring[:, half, :], m.d["w_out_2"][half]).then_inc(w_arrived, 16)
            sp.wait_ge(w_arrived, 32)

        @block.tensor
        def _(pe):
            pe.wait_ge(w_arrived, 32)
            for t in range(NT):
                for half in range(2):
                    for k in range(KD):
                        last = pe.matmul(m.ps[2 * t + half][:, :], m.XT[:, k, t * P:(t + 1) * P], f.ring[:, half, k * S:(k + 1) * S],
                                         start=(k == 0), stop=(k == KD - 1))
                    last.then_inc(tile_done, 1)

        @block.vector
        def _(dve):
            for q in range(2 * NT):
                t, cols = q // 2, slice((q % 2) * S, (q % 2 + 1) * S)
                dve.wait_ge(tile_done, q + 1)
                dve.tensor_tensor(m.X[:, t, cols], m.X[:, t, cols], m.ps[q][:, :], ALU.add).then_inc(summed, 1)
            dve.wait_ge(summed, 2 * NT)


def feed_forward(nc, m, f):
    names = ("w0", "w1", "w2", "w3", "ff_done", "relu_done", "squared", "half_done", "summed")
    with stage(nc, "feed_forward", *names) as (block, sems):
        w_in, (ff_done, relu_done, squared, half_done, summed) = sems[:4], sems[4:]

        @block.sync
        def _(sp):
            for i in range(16):
                if i >= 4:
                    j = i - 4
                    sp.wait_ge(ff_done, 4 * (j + 1) if j < 8 else 32 + (j - 7))
                src = m.d["w_ff1"][i] if i < 8 else m.d["w_ff2"][i - 8]
                sp.dma_start(f.ring[:, i % 4, :], src).then_inc(w_in[i % 4], 16)

        @block.tensor
        def _(pe):
            for i in range(8):
                pe.wait_ge(w_in[i % 4], 16 * (i // 4 + 1))
                for c in range(4):
                    u = 4 * i + c
                    if u >= 4:
                        pe.wait_ge(relu_done, u - 3)
                    for k in range(KD):
                        last = pe.matmul(m.ps[u % 4][:, :], f.ring[:, i % 4, k * S + c * P:k * S + (c + 1) * P], m.XT[:, k, :],
                                         start=(k == 0), stop=(k == KD - 1))
                    last.then_inc(ff_done, 1)
            for i in range(8):
                half, part = divmod(i, 4)
                pe.wait_ge(w_in[i % 4], 16 * (i // 4 + 3))
                if half == 0:
                    pe.wait_ge(squared, 8 * (part + 1))
                for t in range(NT):
                    bank = m.ps[(4 if half == 0 else 0) + t]
                    for k in range(8):
                        last = pe.matmul(bank[:, :], f.U2[:, 8 * part + k, t * P:(t + 1) * P], f.ring[:, i % 4, k * S:(k + 1) * S],
                                         start=(part == 0 and k == 0), stop=(part == 3 and k == 7))
                    if part == 3 and t < NT - 1:
                        last.then_inc(half_done, 1)
                last.then_inc(ff_done, 1)

        @block.scalar
        def _(act):
            for u in range(32):
                act.wait_ge(ff_done, u + 1)
                act.activation(f.U2[:, u, :], m.ps[u % 4][:, :], ACT.Relu).then_inc(relu_done, 1)

        @block.vector
        def _(dve):
            for u in range(32):
                dve.wait_ge(relu_done, u + 1)
                dve.tensor_tensor(f.U2[:, u, :], f.U2[:, u, :], f.U2[:, u, :], ALU.mult).then_inc(squared, 1)
            for half in range(2):
                for t in range(NT):
                    if t < NT - 1:
                        dve.wait_ge(half_done, half * 3 + t + 1)
                    else:
                        dve.wait_ge(ff_done, 32 + 4 * (half + 1))
                    cols = slice(half * S, (half + 1) * S)
                    dve.tensor_tensor(m.X[:, t, cols], m.X[:, t, cols], m.ps[(4 if half == 0 else 0) + t][:, :], ALU.add).then_inc(summed, 1)
            dve.wait_ge(summed, 8)


def final_norm(nc, m, n, out):
    names = ("row_in", "act_step", "inv", "dve_step", "finished", "out_done")
    with stage(nc, "final_norm", *names) as (block, (row_in, act_step, inv, dve_step, finished, out_done)):

        @block.sync
        def _(sp):
            sp.dma_start(n.FN[:, :], m.d["final_norm"].to_broadcast([P, D])).then_inc(row_in, 16)
            for t in range(NT):
                sp.wait_ge(finished, t + 1)
                sp.dma_start(out.rearrange("(t p) d -> t p d", p=P)[t], m.X[:, t, :]).then_inc(out_done, 16)
            sp.wait_ge(out_done, 16 * NT)

        @block.scalar
        def _(act):
            link = Chain(act, act_step)
            for t in range(NT):
                link(act.activation(n.XN[:, t, :], m.X[:, t, :], ACT.Square, accum_out=n.SS[:, t:t + 1]))
            rstd(act, link, n.SS[:, :], n.SS[:, :], 1.0 / D, 1e-6).then_inc(inv, 1)

        @block.vector
        def _(dve):
            dve.wait_ge(row_in, 16)
            dve.wait_ge(inv, 1)
            for t in range(NT):
                dve.scalar_tensor_tensor(out=m.X[:, t, :], in0=m.X[:, t, :], scalar=n.SS[:, t:t + 1], in1=n.FN[:, :],
                                         op0=ALU.mult, op1=ALU.mult).then_inc(finished, 1)


class Bag:
    pass


def sb(nc, ctx, name, *shape):
    return ctx.enter_context(nc.sbuf_tensor(f"{name}_{nc.next_id()}", list(shape), F32))


def sbr(nc, ctx, name, *shape):
    return ctx.enter_context(nc.sbuf_tensor(f"{name}_{nc.next_id()}", list(shape), F32R))


def build(nc, d, out):
    with ExitStack() as ctx:
        m = Bag()
        m.X = sb(nc, ctx, "X", P, NT, D)
        m.XT = sb(nc, ctx, "XT", P, KD, S)
        m.ident = sb(nc, ctx, "ident", P, P)
        m.ones = sb(nc, ctx, "ones", P, P)
        m.zeros = sb(nc, ctx, "zeros", P, S)
        m.mask = sb(nc, ctx, "mask", P, 2, P)
        m.TRI = sb(nc, ctx, "TRI", P, P)
        m.IOTA = sb(nc, ctx, "IOTA", P, P)
        m.TAB = sb(nc, ctx, "TAB", P, S)
        m.dup = sb(nc, ctx, "dup", P, 64)
        m.CC = sb(nc, ctx, "CC", P, 8)
        m.CP = sb(nc, ctx, "CP", P, K_N)
        m.RP = sb(nc, ctx, "RP", P, 276)
        m.WR = sb(nc, ctx, "WR", P, KD, 20)
        m.d = d
        m.x_dram, m.dup_dram = d["x"], d["dup"]
        m.ps = [ctx.enter_context(nc.psum_tensor(f"bank{i}", [P, S], F32)) for i in range(8)]
        m.ring_in = [ctx.enter_context(nc.semaphore(f"ring_in{i}")) for i in range(RING)]
        with ExitStack() as c0:
            m.ang = sb(nc, c0, "ang", P, S)
            m.kk = sb(nc, c0, "kk", P, S)
            m.posi = c0.enter_context(nc.sbuf_tensor("posi", [P, S], I32))
            constants(nc, m, d["consts"], d["positions"])

        with ExitStack() as c1:
            m.ring = sb(nc, c1, "ring", P, RING, SLOT)
            with nc.Fori(0, DEPTH) as layer:
                one = bass.ds(layer, 1)

                def first_loads(sp):
                    for i in range(RING):
                        sp.dma_start(m.ring[:, i, 0:4096], d["w_in_t"][one, i].rearrange("a p n -> p (a n)")).then_inc(m.ring_in[i], 16)

                def layer_params(sp, sem):
                    sp.dma_start(m.CP[:, 0:C_N], d["cols"][one].rearrange("a p n -> p (a n)")).then_inc(sem, 16)
                    sp.dma_start(m.RP[:, :], d["rows"][one, 0:276].to_broadcast([P, 276])).then_inc(sem, 16)
                    sp.dma_start(m.WR[:, :, :].rearrange("p k n -> p (k n)"), d["w_router"][one].rearrange("a p n -> p (a n)")).then_inc(sem, 16)
                    return 3

                transpose_stage(nc, m, first_loads, layer_params)
                with ExitStack() as c2:
                    mx = Bag()
                    mx.V1 = sb(nc, c2, "V1", P, NT, 4, 65)
                    mx.O = sb(nc, c2, "O", P, NT, 256)
                    mx.MQ = sb(nc, c2, "MQ", P, 2, S)
                    mx.MK = sb(nc, c2, "MK", P, 2, S)
                    mx.Z = sb(nc, c2, "Z", P, 2, S)
                    mx.XB = sb(nc, c2, "XB", P, 6, S + 4)
                    mx.SC = sb(nc, c2, "SC", P, S)
                    mx.IG = sb(nc, c2, "IG", P, S)
                    with ExitStack() as c3:
                        mx.CQ = sb(nc, c3, "CQ", P, 3, S)
                        mx.KRT = sb(nc, c3, "KRT", P, S)
                        in_projection(nc, m, layer, mx)
                        a = Bag()
                        a.QT = sb(nc, c3, "QT", P, 4, S)
                        a.KT = sb(nc, c3, "KT", P, 4, S)
                        a.V = sb(nc, c3, "V", P, NT, S)
                        a.PR = sb(nc, c3, "PR", P, 2, S)
                        a.PT = sb(nc, c3, "PT", P, 2, NT, P)
                        a.SQ = sb(nc, c3, "SQ", P, 3, S)
                        a.RS = sb(nc, c3, "RS", P, 2, S)
                        a.MX = sb(nc, c3, "MX", P, 2)
                        a.NM = sb(nc, c3, "NM", P, 2)
                        a.SM = sb(nc, c3, "SM", P, 2)
                        a.RC = sb(nc, c3, "RC", P, 2)
                        mla(nc, m, mx, a)
                    with ExitStack() as c3:
                        g = Bag()
                        g.T1 = sb(nc, c3, "T1", P, S)
                        g.SP = sb(nc, c3, "SP", P, S)
                        g.CS = sb(nc, c3, "CS", P, S)
                        g.FS = sb(nc, c3, "FS", P, S)
                        g.NM = sb(nc, c3, "NM", P, S)
                        g.CO = sb(nc, c3, "CO", P, 2)
                        g.GN = sb(nc, c3, "GN", P, 3, NT, GR)
                        g.EM = sb(nc, c3, "EM", P, NT, GR)
                        g.XC = sb(nc, c3, "XC", P, 6, S)
                        g.XN = sb(nc, c3, "XN", P, NT, 256)
                        g.E = sb(nc, c3, "E", P, 4, S)
                        g.W = sb(nc, c3, "W", P, 4, S)
                        g.RM = sb(nc, c3, "RM", P, 2, S)
                        g.H = sb(nc, c3, "H", P, NT, 4, 64)
                        g.HB = sb(nc, c3, "HB", P, NT, 64)
                        g.DN = sb(nc, c3, "DN", P, 2, NT)
                        g.DT = sb(nc, c3, "DT", P, 2, NT)
                        g.MEAN = sb(nc, c3, "MEAN", P, 2, 16)
                        gates_and_conv(nc, m, mx, g)
                        scans(nc, m, mx, g)
                        mixer_norms(nc, m, mx, g)
                with ExitStack() as c2:
                    ln = Bag()
                    ln.Y = sb(nc, c2, "Y", P, NT, D)
                    ln.GB = m.ring[:, 2, 0:2 * D]
                    ln.ST = sb(nc, c2, "ST", P, NT, 2, 6)
                    ln.MV = sb(nc, c2, "MV", P, NT, 2)
                    ln.IV = sb(nc, c2, "IV", P, NT)
                    norm_stage(nc, m, ln, 0, layer, product=True)
                    transpose_stage(nc, m)
                    with ExitStack() as c3:
                        r = Bag()
                        r.LG = sb(nc, c3, "LG", P, NT, 20)
                        r.hg = sb(nc, c3, "hg", P, NT, 4)
                        r.h1 = sb(nc, c3, "h1", P, NT, 4)
                        r.h2 = sb(nc, c3, "h2", P, NT, 4)
                        r.e4 = sb(nc, c3, "e4", P, NT, 4)
                        r.el = sb(nc, c3, "el", P, NT, 4)
                        r.gm = sb(nc, c3, "gm", P, NT)
                        r.m1 = sb(nc, c3, "m1", P, NT)
                        r.m2 = sb(nc, c3, "m2", P, NT)
                        r.t1 = sb(nc, c3, "t1", P, NT)
                        r.COMB = sb(nc, c3, "COMB", P, NT, NE)
                        r.OH = sb(nc, c3, "OH", P, NT, NE)
                        r.POS = sb(nc, c3, "POS", P, NT, NE)
                        r.NP = sb(nc, c3, "NP", P, 3)
                        r.NPI = c3.enter_context(nc.sbuf_tensor("passes", [P, 1], I32))
                        r.CW = sbr(nc, c3, "CW", P, NT, NE, 2)
                        r.XH = sbr(nc, c3, "XH", P, NT, D)
                        r.XL = sbr(nc, c3, "XL", P, NT, D)
                        r.SEL = sbr(nc, c3, "SEL", P, NT, 4 * P)
                        r.SELT = sbr(nc, c3, "SELT", P, 4, S)
                        r.YE = sbr(nc, c3, "YE", P, 2, 2, D)
                        r.WS = sb(nc, c3, "WS", P, 4)
                        r.H = sb(nc, c3, "H", P, 2, FE)
                        r.HT = sb(nc, c3, "HT", P, 2 * P)
                        r.SG = sb(nc, c3, "SG", P, 2, FE)
                        r.TRI, r.IOTA = m.TRI, m.IOTA
                        r.Y = ln.Y
                        router(nc, m, r)
                        dispatch(nc, m, r)
                        passes = nc.values_load(r.NPI[0:1, 0:1], min_val=1, max_val=4,
                                                skip_runtime_bounds_check_because="it is one plus three comparisons' results")
                        with nc.Fori(0, passes):
                            experts(nc, m, r, layer)
                            next_pass(nc, r)
                    norm_stage(nc, m, ln, 1, layer)
                nums = [s.num for s in m.ring_in]
                nc.all_engine_barrier(sems_to_clear=range(min(nums), max(nums) + 1))

        with ExitStack() as c1:
            b = Bag()
            b.Z = sb(nc, c1, "Z", P, 4, S)
            b.LG = sb(nc, c1, "LG", P, 4, S)
            b.LX = sb(nc, c1, "LX", P, 4, S + 3)
            b.XC = sb(nc, c1, "XC", P, 12, S)
            b.GR = sb(nc, c1, "GR", P, S)
            b.G1 = sb(nc, c1, "G1", P, S)
            b.GC = sb(nc, c1, "GC", P, S)
            b.GM = sb(nc, c1, "GM", P, S)
            b.BT = sb(nc, c1, "BT", P, S)
            b.EG = sb(nc, c1, "EG", P, S)
            b.DK = sb(nc, c1, "DK", P, S)
            b.BE = sb(nc, c1, "BE", P, S)
            b.CO = sb(nc, c1, "CO", P, 1)
            b.GN = sb(nc, c1, "GN", P, 64)
            with ExitStack() as c2:
                q = Bag()
                q.QB = sb(nc, c2, "QB", P, 12, S + 3)

                def params(sp, sem):
                    sp.dma_start(m.CP[:, 0:K_N], d["cols_2"]).then_inc(sem, 16)
                    return 1

                with ExitStack() as c3:
                    n = Bag()
                    n.XN = sb(nc, c3, "XN", P, NT, D)
                    n.SS = sb(nc, c3, "SS", P, NT)
                    rms_transpose(nc, m, n, K_NM, params)
                with ExitStack() as c3:
                    q.ring = sb(nc, c3, "ring", P, RING, 4416)
                    in_projection_2(nc, m, b, q)
                q.SQ = sb(nc, c2, "SQ", P, 2, S)
                q.RS = sb(nc, c2, "RS", P, 8, S)
                gdn_prepare(nc, m, b, q)
            with ExitStack() as c2:
                hd = (P, GH, S)
                ch = (P, NT, GH, P)
                w = Bag()
                w.LM = sb(nc, c2, "LM", P, 7, P)
                w.KB = sb(nc, c2, "KB", *hd)
                w.QE = sb(nc, c2, "QE", *hd)
                w.GL = sb(nc, c2, "GL", P, GH, NT)
                w.AT = sb(nc, c2, "AT", *ch)
                w.AQ = sb(nc, c2, "AQ", *ch)
                w.T = sb(nc, c2, "T", *ch)
                w.U = sb(nc, c2, "U", *ch)
                w.KE = sb(nc, c2, "KE", *ch)
                w.KD = sb(nc, c2, "KD", *ch)
                w.VB = sb(nc, c2, "VB", *ch)
                w.VN = sb(nc, c2, "VN", P, GH, P)
                w.S = sb(nc, c2, "S", P, GH, P)
                with ExitStack() as c3:
                    w.E = sb(nc, c3, "E", *ch)
                    w.RM = sb(nc, c3, "RM", *hd)
                    gdn_matrices(nc, m, b, w)
                with ExitStack() as c3:
                    w.Z = sb(nc, c3, "Z", *ch)
                    gdn_inverse(nc, m, w)
                w.NW = sb(nc, c2, "NW", *ch)
                w.OT = sb(nc, c2, "OT", *hd)
                gdn_sequence(nc, m, b, w)
                gdn_norm(nc, m, b, w)
            with ExitStack() as c2:
                u = Bag()
                u.XR = sb(nc, c2, "XR", *hd)
                u.RG = sb(nc, c2, "RG", *hd)
                u.IG = sb(nc, c2, "IG", *hd)
                u.RT = sb(nc, c2, "RT", *hd)
                u.TH = sb(nc, c2, "TH", P, 2, S)
                u.WA = sb(nc, c2, "WA", P, 8, 64)
                u.AB = sb(nc, c2, "AB", P, 8)
                u.SPA = sb(nc, c2, "SPA", P, 4)
                lru(nc, m, b, u)
        with ExitStack() as c1:
            f = Bag()
            f.ring = sb(nc, c1, "ring", P, 4, 4096)
            out_projection_2(nc, m, f)
            with ExitStack() as c2:
                n = Bag()
                n.XN = sb(nc, c2, "XN", P, NT, D)
                n.SS = sb(nc, c2, "SS", P, NT)
                n.FN = sb(nc, c2, "FN", P, D)
                rms_transpose(nc, m, n, K_NP)
            with ExitStack() as c2:
                f.U2 = sb(nc, c2, "U2", P, 32, S)
                feed_forward(nc, m, f)
            with ExitStack() as c2:
                n = Bag()
                n.XN = sb(nc, c2, "XN", P, NT, D)
                n.SS = sb(nc, c2, "SS", P, NT)
                n.FN = sb(nc, c2, "FN", P, D)
                final_norm(nc, m, n, out)


def rows_to_tiles(w, cols):
    w = w[:, cols] if cols is not None else w
    return np.ascontiguousarray(w.reshape(-1, P, w.shape[1]).transpose(1, 0, 2).reshape(P, -1))


def layer_arrays(i):
    w_in, L = i["w_in"], DEPTH
    z = np.zeros((L, D, 1), np.float32)

    def take(cols):
        idx = np.array([2488 if c is None else c for c in cols])
        return np.concatenate([w_in, z], -1)[:, :, idx]

    none = [None]
    kr = list(range(384, 416))
    krs = kr[16:] + kr[:16]
    g = lambda j: list(range(1440 + 4 * j, 1444 + 4 * j))
    dt = lambda j: list(range(2480 + 4 * j, 2484 + 4 * j))
    sc = g(1) + dt(0) + none * 24 + g(3) + dt(1)
    ig = g(0) + none * 28 + g(2) + none * 4
    xbc = list(range(1712, 2480))
    block0 = list(range(0, 384)) + sc + none * 24 + kr + krs
    block1 = xbc[:512]
    block2 = xbc[512:] + list(range(1456, 1712))
    block3 = list(range(416, 928))
    vo = list(range(928, 1440))
    tiles = lambda a: np.stack([rows_to_tiles(x, None) for x in a])
    w_t = np.stack([tiles(take(b)) for b in (block0, block1, block2, block3)], 1)
    w_n = np.concatenate([tiles(take(vo)), tiles(take(ig))], -1)

    uq = i["mla_w_uq"].reshape(L, 256, HEADS, NOPE + ROPE)
    swapped = np.concatenate([uq[..., 80:96], uq[..., 64:80]], -1)
    uq = np.concatenate([uq, swapped], -1).reshape(L, 256, HEADS * P)
    ukv = i["mla_w_ukv"].reshape(L, P, HEADS, NOPE + VD)
    w_mla = np.concatenate([tiles(uq), ukv[..., :NOPE].reshape(L, P, 512), ukv[..., NOPE:].reshape(L, P, 512)], -1)

    halves = lambda a: np.stack([rows_to_tiles(a, slice(0, S)), rows_to_tiles(a, slice(S, D))])
    w_out = np.stack([halves(a) for a in i["w_out"]])
    gu = np.concatenate([i["expert_w_gate"], i["expert_w_up"]], -1)
    w_exp = np.concatenate([gu.reshape(L, NE, KD, P, 2 * FE).transpose(0, 1, 3, 2, 4).reshape(L, NE, P, -1),
                            i["expert_w_down"].reshape(L, NE, 2, P, D).transpose(0, 1, 3, 2, 4).reshape(L, NE, P, -1)], -1)
    we = i["router_expert_w"].transpose(0, 2, 1, 3).reshape(L, D, NE)
    w_router = tiles(np.concatenate([i["router_group_w"], we], -1))

    cols = np.zeros((L, P, C_N), np.float32)
    cols[:, :, C_QN:C_QN + 2] = i["mla_q_norm"].reshape(L, 2, P).transpose(0, 2, 1)
    cols[:, :, C_KVN] = i["mla_kv_norm"]
    cols[:, :, C_CW:C_CW + 30] = i["ssd_conv_w"].reshape(L, 5, 6, P).transpose(0, 3, 2, 1).reshape(L, P, 30)
    cols[:, :, C_CB:C_CB + 6] = i["ssd_conv_b"].reshape(L, 6, P).transpose(0, 2, 1)
    cols[:, :, C_DS:C_DS + 2] = np.repeat(i["ssd_d"].reshape(L, 2, 2), 64, axis=2).transpose(0, 2, 1)
    cols[:, :, C_SN:C_SN + 2] = i["ssd_norm"].reshape(L, 2, P).transpose(0, 2, 1)
    for d in range(2):
        lf, dtr = slice(32 * d, 32 * d + 4), slice(32 * d + 4, 32 * d + 8)
        cols[:, lf, C_SGN], cols[:, dtr, C_SGN] = -1.0, 1.0
        cols[:, dtr, C_SB] = i["ssd_dt_bias"][:, d]
        cols[:, lf, C_SB] = i["mlstm_gate_bias"][:, 2 * d + 1]
        cols[:, dtr, C_AL] = i["ssd_a_log"][:, d]
        cols[:, lf, C_IB] = i["mlstm_gate_bias"][:, 2 * d]
    rows = np.concatenate([i["mlstm_norm"], i["router_group_b"], i["router_expert_b"].reshape(L, NE),
                           i["ln1_g"], i["ln1_b"], i["ln2_g"], i["ln2_b"]], -1)
    return {"w_in_t": w_t, "w_in_n": w_n, "w_mla": w_mla, "w_out": w_out, "w_exp": w_exp, "w_router": w_router, "cols": cols, "rows": rows}


def second_arrays(i):
    w = i["w_in_2"][0]
    perm = list(range(0, 1536)) + list(range(1536, 2048)) + list(range(2056, 3080))
    blocks = [rows_to_tiles(w, np.array(perm[512 * n:512 * (n + 1)])) for n in range(6)]
    gate = np.zeros((D, GR), np.float32)
    gate[:, 0:4], gate[:, 32:36] = w[:, 2052:2056], w[:, 2048:2052]
    gate = rows_to_tiles(gate, None)
    w_in_2 = np.stack([np.concatenate([x, gate], -1) for x in blocks])
    cols = np.zeros((P, K_N), np.float32)
    per = lambda v, n: v.reshape(n, P).T
    cols[:, K_NM:K_NM + 8] = per(i["norm_mix_w_2"][0], 8)
    cols[:, K_NP:K_NP + 8] = per(i["norm_mlp_w_2"][0], 8)
    cols[:, K_GC:K_GC + 48] = i["gdn_conv_w_2"][0].reshape(4, 12, P).transpose(2, 1, 0).reshape(P, 48)
    cols[:, K_LC:K_LC + 16] = i["lru_conv_w_2"][0].reshape(4, 4, P).transpose(2, 1, 0).reshape(P, 16)
    cols[:, K_LB:K_LB + 4] = per(i["lru_conv_b_2"][0], 4)
    cols[:, K_AB:K_AB + 4] = per(i["lru_gate_a_b_2"][0], 4)
    cols[:, K_XB:K_XB + 4] = per(i["lru_gate_x_b_2"][0], 4)
    cols[:, K_AP:K_AP + 4] = per(i["lru_a_param_2"][0], 4)
    cols[:, K_GN] = i["gdn_norm_w_2"][0]
    cols[0:4, K_AL] = i["gdn_A_log_2"][0]
    cols[0:4, K_DB] = i["gdn_dt_bias_2"][0]
    gates = np.stack([i["lru_gate_a_w_2"][0], i["lru_gate_x_w_2"][0]], 1).reshape(4, 2, 2, 64, 64)
    lru_w = np.ascontiguousarray(gates.transpose(1, 3, 0, 2, 4).reshape(P, 8, 64))
    halves = lambda a: np.stack([rows_to_tiles(a, slice(0, S)), rows_to_tiles(a, slice(S, D))])
    w_ff1 = np.stack([rows_to_tiles(i["w_ff1_2"][0], slice(S * n, S * (n + 1))) for n in range(8)])
    w_ff2 = np.stack([rows_to_tiles(i["w_ff2_2"][0][D * part:D * (part + 1)], slice(S * half, S * (half + 1)))
                      for half in range(2) for part in range(4)])
    return {"w_in_2": w_in_2, "cols_2": cols, "lru_w": lru_w, "w_out_2": halves(i["w_out_2"][0]), "w_ff1": w_ff1, "w_ff2": w_ff2,
            "final_norm": i["final_norm_w_2"].reshape(1, D)}


def shape_constants():
    consts = np.zeros((P, 8), np.float32)
    freq = np.float32(10000.0) ** (-np.arange(0, ROPE, 2, dtype=np.float32) / np.float32(ROPE))
    consts[64:128, 0] = np.tile(freq, 4)
    consts[64:96, 1] = 0.25
    consts[64:96, 2] = math.pi / 2
    consts[64:96, 3], consts[96:112, 3], consts[112:128, 3] = 1.0, -1.0, 1.0
    consts[:, 4:8] = [4.0, 3.0, 2.0, 1.0]
    dup = np.zeros((P, 64), np.float32)
    for r in range(64):
        dup[64 + r, r % 32], dup[64 + r, 32 + r % 32] = 1.0, 1.0
    i, j = np.arange(P)[:, None], np.arange(P)[None, :]
    masks = [-((i // (2 * n) == j // (2 * n)) & (i // n > j // n)).astype(np.float32) for n in (1, 2, 4, 8, 16, 32, 64)]
    return {"consts": consts, "dup": dup, "level_masks": np.ascontiguousarray(np.stack(masks, 1))}


def kernel(**inputs):
    import concourse.bacc as bacc
    from concourse.bass_utils import run_bass_kernel_spmd as run

    i = {k: np.asarray(v) for k, v in inputs.items()}
    arrays = {"x": i["x"].reshape(S, D), "positions": i["positions"].reshape(1, S)}
    arrays.update(shape_constants())
    arrays.update(layer_arrays(i))
    arrays.update(second_arrays(i))
    arrays = {k: np.ascontiguousarray(v) for k, v in arrays.items()}
    nc = bacc.Bacc("TRN2", target_bir_lowering=False, num_devices=1)
    d = {k: nc.dram_tensor(f"in_{k}", v.shape, mybir.dt.from_np(v.dtype), kind="ExternalInput").ap() for k, v in arrays.items()}
    out = nc.dram_tensor("out", (S, D), F32, kind="ExternalOutput").ap()
    build(nc, d, out)
    r = run(nc, [{f"in_{k}": v for k, v in arrays.items()}], core_ids=[0])
    return r.results[0]["out"].reshape(1, S, D)
```

```python
import math
from contextlib import ExitStack, contextmanager

import numpy as np

import concourse.bass as bass
from concourse import mybir

F32 = mybir.dt.float32
F32R = mybir.dt.float32r
I32 = mybir.dt.int32
ALU = mybir.AluOpType
ACT = mybir.ActivationFunctionType
AX = mybir.AxisListType

P = 128
S = 512
NT = S // P
D = 1024
KD = D // P
DEPTH = 2
ALPHA = (2 * DEPTH) ** 0.25
NEG = -1e30

HEADS, NOPE, ROPE, VD = 8, 64, 32, 64
SCALE = (NOPE + ROPE) ** -0.5
RING, SLOT = 3, 6144
NE, FE = 16, 256
NGR = 4

C_QN, C_KVN, C_CW, C_CB, C_DS, C_SN, C_SGN, C_SB, C_AL, C_IB, C_N = 0, 2, 3, 33, 39, 41, 43, 44, 45, 46, 47
R_MN, R_RB, R_L1, R_L2, R_N = 0, 256, 276, 276 + 2 * D, 276 + 4 * D
GR = 40
TERMS = ((0, 0), (0, 1), (1, 0))


class Chain:

    def __init__(self, eng, sem):
        self.eng, self.sem, self.n = eng, sem, 0

    def __call__(self, ins):
        ins.then_inc(self.sem, 1)
        self.n += 1
        self.eng.wait_ge(self.sem, self.n)


@contextmanager
def stage(nc, name, *names):
    with ExitStack() as ctx:
        sems = [ctx.enter_context(nc.semaphore(n)) for n in names]
        with nc.Block(f"{name}_{nc.next_id()}", no_gpsimd_drain=True) as block:
            yield block, sems
        nums = [s.num for s in sems]
        nc.all_engine_barrier(sems_to_clear=range(min(nums), max(nums) + 1))


def rstd(act, link, out, var, scale, eps):
    link(act.activation(out, var, ACT.Ln, scale=scale, bias=eps))
    return act.activation(out, out, ACT.Exp, scale=-0.5)


def blocks(x):
    return x.rearrange("p (b n) -> p b n", b=NT)


def every_block(x):
    return x.rearrange("p (a n) -> p a n", a=1).to_broadcast([P, NT, P])


def constants(nc, m, consts_dram, pos_dram):
    with stage(nc, "constants", "pool_step", "const_in", "pos_in", "dve_step", "angle", "sine") as (block, sems):
        pool_step, const_in, pos_in, dve_step, angle, sine = sems

        @block.sync
        def _(sp):
            sp.dma_start(m.X[:, :, :], m.x_dram.rearrange("(t p) d -> p t d", p=P)).then_inc(const_in, 16)
            sp.dma_start(m.CC[:, :], consts_dram).then_inc(const_in, 16)
            sp.dma_start(m.dup[:, :], m.dup_dram).then_inc(const_in, 16)
            sp.wait_ge(const_in, 48)

        @block.gpsimd
        def _(pool):
            link = Chain(pool, pool_step)
            link(pool.memset(m.ident[:, :], 0.0))
            link(pool.affine_select(out=m.ident[:, :], in_=m.ident[:, :], compare_op=ALU.not_equal, fill=1.0,
                                    base=0, pattern=[[-1, P]], channel_multiplier=1))
            link(pool.memset(m.ones[:, :], 1.0))
            link(pool.memset(m.zeros[:, :], 0.0))
            for d, sign in ((0, 1), (1, -1)):
                link(pool.affine_select(out=m.mask[:, d, :], in_=m.zeros[:, 0:P], compare_op=ALU.is_ge, fill=NEG, base=0,
                                        pattern=[[sign, P]], channel_multiplier=-sign))
            link(pool.affine_select(out=m.TRI[:, :], in_=m.ones[:, :], compare_op=ALU.is_gt, fill=0.0, base=0, pattern=[[1, P]], channel_multiplier=-1))
            link(pool.iota(m.IOTA[:, :], pattern=[[1, P]], base=0, channel_multiplier=0, allow_small_or_imprecise_dtypes=True))

        @block.vector
        def _(dve):
            link = Chain(dve, dve_step)
            dve.wait_ge(pos_in, 16)
            dve.wait_ge(const_in, 48)
            r = slice(64, 128)
            ang, k = m.ang[r, :], m.kk[r, :]
            link(dve.memset(m.TAB[0:64, :], 1.0))
            link(dve.tensor_copy(ang, m.posi[r, :]))
            link(dve.tensor_scalar(ang, ang, m.CC[r, 0:1], None, ALU.mult))
            link(dve.tensor_scalar(k, ang, 1.0 / (2 * math.pi), m.CC[r, 1:2], ALU.mult, ALU.add))
            link(dve.tensor_scalar(k, k, 12582912.0, None, ALU.add))
            link(dve.tensor_scalar(k, k, -12582912.0, None, ALU.add))
            for c in (6.28125, 0.0019350051879882812, 3.0199159819567e-07):
                link(dve.scalar_tensor_tensor(out=ang, in0=k, scalar=-c, in1=ang, op0=ALU.mult, op1=ALU.add))
            link(dve.tensor_scalar(ang, ang, m.CC[r, 2:3], None, ALU.add))
            link(dve.tensor_scalar(ang, ang, 3.1415925, -3.1415925, ALU.min, ALU.max))
            dve.sem_inc(angle, 1)
            dve.wait_ge(sine, 1)
            link(dve.tensor_scalar(m.TAB[r, :], k, m.CC[r, 3:4], None, ALU.mult))

        @block.scalar
        def _(act):
            act.dma_start(m.posi[:, :], pos_dram.to_broadcast([P, S])).then_inc(pos_in, 16)
            act.wait_ge(angle, 1)
            act.activation(m.kk[64:128, :], m.ang[64:128, :], ACT.Sin).then_inc(sine, 1)


def transpose_stage(nc, m, loads=None, params=None):
    with stage(nc, "transpose_stage", "transposed", "xt_act", "xt_dve", "param_in") as (block, (transposed, xt_act, xt_dve, param_in)):

        @block.sync
        def _(sp):
            if loads:
                loads(sp)
            if params:
                n = params(sp, param_in)
                sp.wait_ge(param_in, 16 * n)

        @block.tensor
        def _(pe):
            for k in range(KD):
                for t in range(NT):
                    last = pe.transpose(m.ps[k][:, t * P:(t + 1) * P], m.X[:, t, k * P:(k + 1) * P], m.ident[:, :])
                last.then_inc(transposed, 1)

        @block.scalar
        def _(act):
            for k in range(0, KD, 2):
                act.wait_ge(transposed, k + 1)
                act.copy(m.XT[:, k, :], m.ps[k][:, :]).then_inc(xt_act, 1)
            act.wait_ge(xt_act, KD // 2)

        @block.vector
        def _(dve):
            for k in range(1, KD, 2):
                dve.wait_ge(transposed, k + 1)
                dve.tensor_copy(m.XT[:, k, :], m.ps[k][:, :]).then_inc(xt_dve, 1)
            dve.wait_ge(xt_dve, KD // 2)


def in_projection(nc, m, layer, mx):
    with stage(nc, "in_projection", "unit_done", "home_act", "home_dve") as (block, (unit_done, home_act, home_dve)):
        units = []
        for c in range(3):
            units.append((0, c * P, P, S, [("copy", slice(0, P), mx.CQ[:, c, :])]))
        units.append((0, 3 * P, P, S, [("copy", slice(0, GR), mx.SC[0:GR, :]), ("rope", slice(64, 128), mx.KRT[64:128, :])]))
        for c in range(6):
            units.append((1 + c // 4, (c % 4) * P, P, S, [("copy", slice(0, P), mx.XB[:, c, 2:2 + S])]))
        for c in range(2):
            units.append((2, (2 + c) * P, P, S, [("copy", slice(0, P), mx.Z[:, c, :])]))
        for c in range(2):
            units.append((3, c * P, P, S, [("copy", slice(0, P), mx.MQ[:, c, :])]))
        for c in range(2):
            units.append((3, (2 + c) * P, P, S, [("scale", slice(0, P), mx.MK[:, c, :])]))
        units.append((4, 4096, GR, GR, [("copy", slice(0, GR), mx.IG[0:GR, :])]))
        for t in range(NT):
            units.append((4, None, t, S, [("v", None, mx.V1[:, t, :, 0:64]), ("copy2", None, mx.O[:, t, :])]))
        engine = [g % 2 if g > 3 else (1 if g in (1, 3) else 0) for g in range(len(units))]

        def evictions(eng, which, done):
            for g, (_, _, _, _, homes) in enumerate(units):
                if engine[g] != which:
                    continue
                bank = m.ps[g % 8]
                eng.wait_ge(unit_done, g + 1)
                for kind, rows, home in homes:
                    if kind == "rope":
                        last = eng.tensor_tensor(home, bank[rows, :], m.TAB[rows, :], ALU.mult)
                        continue
                    if kind == "v":
                        src = bank[:, 0:256].rearrange("p (h d) -> p h d", h=4)
                    elif kind == "copy2":
                        src = bank[:, 256:512]
                    else:
                        src = bank[rows, :]
                    factor = 0.125 if kind == "scale" else None
                    if which == 0:
                        last = eng.mul(home, src, factor) if factor else eng.copy(home, src)
                    else:
                        last = eng.tensor_scalar(home, src, factor, None, ALU.mult) if factor else eng.tensor_copy(home, src)
                last.then_inc(done, 1)
            eng.wait_ge(done, sum(1 for e in engine if e == which))

        @block.sync
        def _(sp):
            sp.wait_ge(unit_done, 4)
            sp.dma_start(m.ring[:, 0, 0:4096], m.d["w_in_t"][bass.ds(layer, 1), 3].rearrange("a p n -> p (a n)")).then_inc(m.ring_in[0], 16)
            sp.wait_ge(unit_done, 8)
            sp.dma_start(m.ring[:, 1, 0:4416], m.d["w_in_n"][bass.ds(layer, 1)].rearrange("a p n -> p (a n)")).then_inc(m.ring_in[1], 16)
            sp.wait_ge(unit_done, 12)
            sp.dma_start(m.ring[:, 2, 0:3072], m.d["w_mla"][bass.ds(layer, 1)].rearrange("a p n -> p (a n)")).then_inc(m.ring_in[2], 16)
            for half, (done, slot) in enumerate(((16, 0), (len(units), 1))):
                sp.wait_ge(unit_done, done)
                sp.dma_start(m.ring[:, slot, 0:4096], m.d["w_out"][bass.ds(layer, 1), half].rearrange("a p n -> p (a n)")).then_inc(m.ring_in[slot], 16)

        @block.tensor
        def _(pe):
            seen = -1
            for g, (load, col, n, width, _) in enumerate(units):
                if load != seen:
                    seen = load
                    pe.wait_ge(m.ring_in[load % RING], 16 * (load // RING + 1))
                if g >= 8:
                    e = engine[g - 8]
                    pe.wait_ge((home_act, home_dve)[e], sum(1 for x in engine[:g - 7] if x == e))
                slot = m.ring[:, load % RING, :]
                for k in range(KD):
                    if col is None:
                        last = pe.matmul(m.ps[g % 8][:, :], m.XT[:, k, n * P:(n + 1) * P], slot[:, k * S:(k + 1) * S],
                                         start=(k == 0), stop=(k == KD - 1))
                    else:
                        at = col + k * width
                        last = pe.matmul(m.ps[g % 8][0:n, :], slot[:, at:at + n], m.XT[:, k, :],
                                         start=(k == 0), stop=(k == KD - 1))
                last.then_inc(unit_done, 1)

        @block.scalar
        def _(act):
            evictions(act, 0, home_act)

        @block.vector
        def _(dve):
            evictions(dve, 1, home_dve)

        @block.gpsimd
        def _(pool):
            pool.memset(mx.XB[:, :, 0:2], 0.0)
            pool.memset(mx.XB[:, :, 2 + S:4 + S], 0.0)
            pool.memset(mx.V1[:, :, :, 64:65], 1.0)


def mla(nc, m, mx, a):
    HH = HEADS // 2
    NU = HH * NT
    names = ("act_step", "dve_step", "squares", "sums", "inv_rms", "normed", "q_done", "q_home", "k_done", "k_home", "v_done",
             "v_home", "kr_done", "scores", "neg_max", "probs", "probs_normed", "probs_t", "probs_t_home", "pv", "head_home")
    with stage(nc, "mla", *names) as (block, sems):
        (act_step, dve_step, squares, sums, inv_rms, normed, q_done, q_home, k_done, k_home, v_done,
         v_home, kr_done, scores, neg_max, probs, probs_normed, probs_t, probs_t_home, pv, head_home) = sems
        w = m.ring[:, 2, :]
        wq = w[:, 0:2048].rearrange("p (k n) -> p k n", k=2)
        wk = w[:, 2048:2560]
        wv = w[:, 2560:3072]

        @block.tensor
        def _(pe):
            pe.wait_ge(m.ring_in[2], 32)
            pe.wait_ge(squares, 1)
            pe.matmul(m.ps[0][:, :], m.ones[:, :], a.SQ[:, 0, :], start=True, stop=False)
            pe.matmul(m.ps[0][:, :], m.ones[:, :], a.SQ[:, 1, :], start=False, stop=True)
            pe.matmul(m.ps[1][:, :], m.ones[:, :], a.SQ[:, 2, :], start=True, stop=True).then_inc(sums, 1)
            pe.matmul(m.ps[2][64:128, :], m.dup[64:128, :], mx.KRT[64:128, :], start=True, stop=True).then_inc(kr_done, 1)
            pe.wait_ge(normed, 1)
            for t in range(NT):
                if t >= 1:
                    pe.wait_ge(v_home, t)
                pe.matmul(m.ps[3][:, :], mx.CQ[:, 2, t * P:(t + 1) * P], wv, start=True, stop=True).then_inc(v_done, 1)
            for half in range(2):
                for hh in range(HH):
                    h = half * HH + hh
                    if h == 0:
                        pe.wait_ge(inv_rms, 2)
                    if h >= 2:
                        pe.wait_ge(q_home, h - 1)
                        pe.wait_ge(k_home, h)
                    elif h == 0:
                        pe.wait_ge(k_home, 1)
                    elif h == 1:
                        pe.wait_ge(v_home, NT)
                    for k in range(2):
                        last = pe.matmul(m.ps[h % 2][:, :], wq[:, k, h * P:(h + 1) * P], mx.CQ[:, k, :], start=(k == 0), stop=(k == 1))
                    last.then_inc(q_done, 1)
                    pe.matmul(m.ps[2 + h % 2][0:64, :], wk[:, h * 64:(h + 1) * 64], mx.CQ[:, 2, :], start=True, stop=True).then_inc(k_done, 1)
                pe.wait_ge(q_home, (half + 1) * HH)
                pe.wait_ge(k_home, 1 + (half + 1) * HH)
                for step in range(NU + 3):
                    if step < NU:
                        i = half * NU + step
                        hh, t = divmod(step, NT)
                        if i >= 4:
                            pe.wait_ge(probs, i - 3)
                        pe.matmul(m.ps[i % 4][:, :], a.QT[:, hh, t * P:(t + 1) * P], a.KT[:, hh, :], start=True, stop=True).then_inc(scores, 1)
                    if 2 <= step < NU + 2:
                        i = half * NU + step - 2
                        pe.wait_ge(probs_normed, i + 1)
                        if i >= 2:
                            pe.wait_ge(probs_t_home, i - 1)
                        for k in range(NT):
                            last = pe.transpose(m.ps[4 + i % 2][:, k * P:(k + 1) * P], a.PR[:, i % 4, k * P:(k + 1) * P], m.ident[:, :])
                        last.then_inc(probs_t, 1)
                    if step >= 3:
                        i = half * NU + step - 3
                        h, t = divmod(i, NT)
                        pair, rows = h // 2, slice(64 * (h % 2), 64 * (h % 2) + 64)
                        pe.wait_ge(probs_t_home, i + 1)
                        if pair >= 2 and h % 2 == 0 and t == 0:
                            pe.wait_ge(head_home, pair - 1)
                        for k in range(NT):
                            last = pe.matmul(m.ps[6 + pair % 2][rows, t * P:(t + 1) * P], a.V[:, k, h * 64:(h + 1) * 64],
                                             a.PT[:, i % 2, k, :], start=(k == 0), stop=(k == NT - 1))
                        last.then_inc(pv, 1)

        @block.scalar
        def _(act):
            link = Chain(act, act_step)
            act.wait_ge(sums, 1)
            rstd(act, link, a.RS[:, 0, :], m.ps[0][:, :], 1.0 / 256, 1e-6).then_inc(inv_rms, 1)
            rstd(act, link, a.RS[:, 1, :], m.ps[1][:, :], 1.0 / 128, 1e-6).then_inc(inv_rms, 1)
            act.wait_ge(kr_done, 1)
            act.copy(a.KT[64:128, :, :], m.ps[2][64:128, :].rearrange("p (a n) -> p a n", a=1).to_broadcast([64, HH, S])).then_inc(k_home, 1)
            for t in range(NT):
                act.wait_ge(v_done, t + 1)
                act.copy(a.V[:, t, :], m.ps[3][:, :]).then_inc(v_home, 1)
            for half in range(2):
                if half:
                    act.wait_ge(scores, NU)
                for h in range(half * HH, (half + 1) * HH):
                    act.wait_ge(k_done, h + 1)
                    act.copy(a.KT[0:64, h % HH, :], m.ps[2 + h % 2][0:64, :]).then_inc(k_home, 1)
                for step in range(NU + 2):
                    if step < NU:
                        i = half * NU + step
                        act.wait_ge(neg_max, i + 1)
                        if i >= 4:
                            act.wait_ge(probs_t, i - 3)
                        act.activation(a.PR[:, i % 4, :], m.ps[i % 4][:, :], ACT.Exp, bias=a.NM[:, i % 4:i % 4 + 1],
                                       scale=SCALE, accum_out=a.SM[:, i % 4:i % 4 + 1]).then_inc(probs, 1)
                    if step >= 2:
                        i = half * NU + step - 2
                        act.wait_ge(probs_t, i + 1)
                        if i >= 2:
                            act.wait_ge(pv, i - 1)
                        act.copy(a.PT[:, i % 2, :, :].rearrange("p k n -> p (k n)"), m.ps[4 + i % 2][:, :]).then_inc(probs_t_home, 1)

        @block.vector
        def _(dve):
            link = Chain(dve, dve_step)
            cq = mx.CQ[:, :, :].rearrange("p a n -> p (a n)")
            dve.tensor_tensor(a.SQ[:, :, :].rearrange("p a n -> p (a n)"), cq, cq, ALU.mult).then_inc(squares, 1)
            dve.wait_ge(inv_rms, 2)
            for c in range(3):
                last = dve.scalar_tensor_tensor(out=mx.CQ[:, c, :], in0=mx.CQ[:, c, :], scalar=m.CP[:, C_QN + c:C_QN + c + 1],
                                                in1=a.RS[:, c // 2, :], op0=ALU.mult, op1=ALU.mult)
            last.then_inc(normed, 1)
            for half in range(2):
                if half:
                    dve.wait_ge(scores, NU)
                for h in range(half * HH, (half + 1) * HH):
                    dve.wait_ge(q_done, h + 1)
                    dve.tensor_tensor(a.QT[:, h % HH, :], m.ps[h % 2][:, :], m.TAB[:, :], ALU.mult).then_inc(q_home, 1)
                for step in range(NU + 2):
                    if step < NU:
                        i = half * NU + step
                        dve.wait_ge(scores, i + 1)
                        if i >= 4:
                            dve.wait_ge(probs, i - 3)
                        link(dve.reduce_max(a.MX[:, i % 4:i % 4 + 1], m.ps[i % 4][:, :], AX.X))
                        dve.tensor_scalar(a.NM[:, i % 4:i % 4 + 1], a.MX[:, i % 4:i % 4 + 1], -SCALE, None, ALU.mult).then_inc(neg_max, 1)
                    if 1 <= step <= NU:
                        i = half * NU + step - 1
                        dve.wait_ge(probs, i + 1)
                        link(dve.reciprocal(a.RC[:, i % 4:i % 4 + 1], a.SM[:, i % 4:i % 4 + 1]))
                        dve.tensor_scalar(a.PR[:, i % 4, :], a.PR[:, i % 4, :], a.RC[:, i % 4:i % 4 + 1], None, ALU.mult).then_inc(probs_normed, 1)
                    if step >= 2:
                        i = half * NU + step - 2
                        h, t = divmod(i, NT)
                        if h % 2 == 1 and t == NT - 1:
                            dve.wait_ge(pv, i + 1)
                            dve.tensor_copy(m.XT[:, h // 2, :], m.ps[6 + (h // 2) % 2][:, :]).then_inc(head_home, 1)
            dve.wait_ge(head_home, HEADS // 2)


def gates_and_conv(nc, m, mx, g):
    names = ("act_step", "dve_step", "biased", "abs_ready", "log_ready", "coef", "rows_done", "conv_done",
             "silu_done", "gates_t", "x_t", "em_ready")
    with stage(nc, "gates_and_conv", *names) as (block, sems):
        act_step, dve_step, biased, abs_ready, log_ready, coef, rows_done, conv_done, silu_done, gates_t, x_t, em_ready = sems
        R = slice(0, GR)

        @block.scalar
        def _(act):
            link = Chain(act, act_step)
            link(act.activation(g.CO[R, 0:1], m.CP[R, C_AL:C_AL + 1], ACT.Exp))
            link(act.mul(g.CO[R, 0:1], g.CO[R, 0:1], -1.0))
            link(act.activation(g.CO[R, 1:2], m.CP[R, C_SB:C_SB + 1], ACT.Identity, scale=m.CP[R, C_SGN:C_SGN + 1]))
            link(act.activation(mx.SC[R, :], mx.SC[R, :], ACT.Identity, scale=m.CP[R, C_SGN:C_SGN + 1], bias=g.CO[R, 1:2]))
            link(act.activation(mx.IG[R, :], mx.IG[R, :], ACT.Identity, bias=m.CP[R, C_IB:C_IB + 1]))
            act.sem_inc(biased, 1)
            act.wait_ge(abs_ready, 1)
            link(act.activation(g.T1[R, :], g.T1[R, :], ACT.Exp))
            act.activation(g.T1[R, :], g.T1[R, :], ACT.Ln, bias=1.0).then_inc(log_ready, 1)
            act.wait_ge(gates_t, 2)
            act.activation(g.EM[:, :, :], g.GN[:, 1, :, :], ACT.Exp, scale=-1.0).then_inc(em_ready, 1)
            for c in range(6):
                act.wait_ge(conv_done, c + 1)
                act.activation(g.XC[:, c, :], g.XC[:, c, :], ACT.Silu, bias=m.CP[:, C_CB + c:C_CB + c + 1]).then_inc(silu_done, 1)
            act.wait_ge(em_ready, 1)
            for c in range(2):
                act.activation(mx.Z[:, c, :], mx.Z[:, c, :], ACT.Silu).then_inc(silu_done, 1)
            act.activation(mx.O[:, :, :], mx.O[:, :, :], ACT.Sigmoid).then_inc(silu_done, 1)
            act.wait_ge(silu_done, 9)

        @block.vector
        def _(dve):
            link = Chain(dve, dve_step)
            dve.wait_ge(biased, 1)
            dve.scalar_tensor_tensor(out=g.T1[R, :], in0=mx.SC[R, :], scalar=-1.0, in1=mx.SC[R, :], op0=ALU.mult, op1=ALU.min).then_inc(abs_ready, 1)
            dve.wait_ge(log_ready, 1)
            link(dve.scalar_tensor_tensor(out=g.SP[R, :], in0=mx.SC[R, :], scalar=0.0, in1=g.T1[R, :], op0=ALU.max, op1=ALU.add))
            link(dve.tensor_scalar(g.T1[R, :], g.SP[R, :], g.CO[R, 0:1], None, ALU.mult))
            link(dve.memset(g.CS[R, :], 0.0))
            link(dve.tensor_tensor_scan(g.CS[0:8, :], m.zeros[0:8, :], g.T1[0:8, :], 0.0, ALU.add, ALU.add))
            link(dve.tensor_tensor_scan(g.CS[32:40, ::-1], m.zeros[32:40, ::-1], g.T1[32:40, ::-1], 0.0, ALU.add, ALU.add))
            link(dve.tensor_tensor(g.FS[R, :], mx.IG[R, :], g.CS[R, :], ALU.subtract))
            link(dve.memset(g.NM[R, :], 0.0))
            link(dve.tensor_tensor_scan(g.NM[0:8, :], m.zeros[0:8, :], g.FS[0:8, :], -3e38, ALU.add, ALU.max))
            link(dve.tensor_tensor_scan(g.NM[32:40, ::-1], m.zeros[32:40, ::-1], g.FS[32:40, ::-1], -3e38, ALU.add, ALU.max))
            link(dve.tensor_tensor(g.T1[R, :], g.CS[R, :], g.NM[R, :], ALU.add))
            dve.tensor_scalar(g.NM[R, :], g.NM[R, :], -1.0, None, ALU.mult).then_inc(rows_done, 1)
            dve.wait_ge(gates_t, 1)
            dve.tensor_copy(g.GN[:, :, :, :].rearrange("p a t r -> p (a t r)"), m.ps[0][:, 0:12 * GR]).then_inc(gates_t, 1)
            for c in range(6):
                for tap in range(5):
                    w = m.CP[:, C_CW + 5 * c + tap:C_CW + 5 * c + tap + 1]
                    src = mx.XB[:, c, tap:tap + S]
                    if tap == 0:
                        link(dve.tensor_scalar(g.XC[:, c, :], src, w, None, ALU.mult))
                    elif tap < 4:
                        link(dve.scalar_tensor_tensor(out=g.XC[:, c, :], in0=src, scalar=w, in1=g.XC[:, c, :], op0=ALU.mult, op1=ALU.add))
                    else:
                        dve.scalar_tensor_tensor(out=g.XC[:, c, :], in0=src, scalar=w, in1=g.XC[:, c, :],
                                                 op0=ALU.mult, op1=ALU.add).then_inc(conv_done, 1)
            for c in range(2):
                dve.wait_ge(x_t, c + 1)
                link(dve.tensor_copy(g.XN[:, :, c * P:(c + 1) * P], m.ps[1 + c][:, :].rearrange("p (t n) -> p t n", t=NT)))

        @block.tensor
        def _(pe):
            pe.wait_ge(rows_done, 1)
            for n, rows in enumerate((g.FS, g.T1, g.SP)):
                for t in range(NT):
                    at = (n * NT + t) * GR
                    last = pe.transpose(m.ps[0][:, at:at + GR], rows[0:GR, t * P:(t + 1) * P], m.ident[0:GR, 0:GR])
            last.then_inc(gates_t, 1)
            for c in range(2):
                pe.wait_ge(silu_done, c + 1)
                for t in range(NT):
                    last = pe.transpose(m.ps[1 + c][:, t * P:(t + 1) * P], g.XC[:, c, t * P:(t + 1) * P], m.ident[:, :])
                last.then_inc(x_t, 1)


def scans(nc, m, mx, g):
    streams = [("mlstm", h, d, h) for h in range(4) for d in range(2)]
    streams += [("ssd", h, d, 4 + h // 2) for h in range(4) for d in range(2)]
    NS = len(streams)
    last_of_base = {b: max(s for s, x in enumerate(streams) if x[3] == b) for b in range(6)}
    names = ("dve_step", "row_done", "row_masked", "decay", "base_done", "weighted", "applied", "head_out", "y_out")
    with stage(nc, "scans", *names) as (block, sems):
        dve_step, row_done, row_masked, decay, base_done, weighted, applied, head_out, y_out = sems

        def span(d, j):
            return slice(j * P, S) if d == 0 else slice(0, (j + 1) * P)

        def base_operands(b):
            if b < 4:
                rows = slice(64 * (b % 2), 64 * (b % 2) + 64)
                return mx.MK[rows, b // 2, :], mx.MQ[rows, b // 2, :]
            return g.XC[:, 2 + b - 4, :], g.XC[:, 4 + b - 4, :]

        @block.tensor
        def _(pe):
            def row(s):
                kind, h, d, _ = streams[s]
                r = 32 * d + h + (4 if kind == "ssd" else 0)
                if s >= 2:
                    pe.wait_ge(decay, 4 * (s - 1))
                pe.matmul(m.ps[4 + s % 2][:, :], m.ident[0:GR, r:r + 1].to_broadcast([GR, P]), g.NM[0:GR, :],
                          start=True, stop=True).then_inc(row_done, 1)

            def base(b, j):
                k, q = base_operands(b)
                pe.matmul(m.ps[j][:, :], k[:, j * P:(j + 1) * P], q, start=True, stop=True).then_inc(base_done, 1)

            row(0)
            row(1)
            for j in range(NT):
                base(0, j)
            for s, (kind, h, d, b) in enumerate(streams):
                for j in range(NT):
                    pe.wait_ge(weighted, 4 * s + j + 1)
                    w = g.W[:, (4 * s + j) % 4, :]
                    if kind == "mlstm":
                        if j == 0 and h >= 1:
                            pe.wait_ge(head_out, 2 * (h - 1) + d + 1)
                        tiles = range(j, NT) if d == 0 else range(0, j + 1)
                        for t in tiles:
                            last = pe.matmul(m.ps[6 + d][:, t * 65:(t + 1) * 65], w[:, t * P:(t + 1) * P], mx.V1[:, j, h, :],
                                             start=(j == 0 and t == tiles[0]), stop=(j == NT - 1 and t == tiles[-1]), skip_group_check=True)
                    else:
                        if s == 8:
                            pe.wait_ge(head_out, 8)
                        e = h % 2
                        last = pe.matmul(m.ps[6 + h // 2][64 * e:64 * e + 64, span(d, j)], g.XN[:, j, h * 64:(h + 1) * 64], w[:, span(d, j)],
                                         start=(d == 0 and j == 0), stop=(d == 1 and j == NT - 1), skip_group_check=True)
                    last.then_inc(applied, 1)
                    if s == last_of_base[b] and b < 5:
                        base(b + 1, j)
                if s + 2 < NS:
                    row(s + 2)

        @block.scalar
        def _(act):
            for s, (kind, h, d, b) in enumerate(streams):
                r = 32 * d + h + (4 if kind == "ssd" else 0)
                for j in range(NT):
                    i = 4 * s + j
                    if j == 0:
                        act.wait_ge(row_masked, s + 1)
                    if i >= 4:
                        act.wait_ge(weighted, i - 3)
                    diag = slice(j * P, (j + 1) * P)
                    off = slice((j + 1) * P, S) if d == 0 else slice(0, j * P)
                    bias = g.GN[:, 0, j, r:r + 1]
                    last = act.activation(g.E[:, i % 4, diag], g.RM[:, s % 2, diag], ACT.Exp, bias=bias)
                    if off.stop > off.start:
                        last = act.activation(g.E[:, i % 4, off], m.ps[4 + s % 2][:, off], ACT.Exp, bias=bias)
                    last.then_inc(decay, 1)

        @block.vector
        def _(dve):
            link = Chain(dve, dve_step)

            def mask_row(s):
                dve.wait_ge(row_done, s + 1)
                if s >= 2:
                    dve.wait_ge(decay, 4 * (s - 1))
                dve.tensor_tensor(blocks(g.RM[:, s % 2, :]), blocks(m.ps[4 + s % 2][:, :]), every_block(m.mask[:, streams[s][2], :]), ALU.add).then_inc(row_masked, 1)

            def outputs(s):
                kind, h, d, b = streams[s]
                r = 32 * d + h
                if kind == "mlstm":
                    dve.wait_ge(applied, 4 * s + 4)
                    nd = m.ps[6 + d][:, 0:NT * 65].rearrange("p (t n) -> p t n", t=NT)
                    den = g.DN[:, d, :].rearrange("p (t a) -> p t a", a=1)
                    link(dve.tensor_scalar(g.DT[:, d, :].rearrange("p (t a) -> p t a", a=1), nd[:, :, 64:65], -1.0, None, ALU.mult))
                    link(dve.tensor_tensor(den, g.DT[:, d, :].rearrange("p (t a) -> p t a", a=1), nd[:, :, 64:65], ALU.max))
                    link(dve.tensor_tensor(den, den, g.EM[:, :, r:r + 1], ALU.max))
                    link(dve.reciprocal(g.DN[:, d, :], g.DN[:, d, :]))
                    dst = g.H[:, :, h, :] if d == 0 else g.HB[:, :, :]
                    dve.tensor_tensor(dst, nd[:, :, 0:64], den.to_broadcast([P, NT, 64]), ALU.mult).then_inc(head_out, 1)
                    if d == 1:
                        dve.wait_ge(head_out, 2 * h + d + 1)
                        link(dve.tensor_tensor(g.H[:, :, h, :], g.H[:, :, h, :], g.HB[:, :, :], ALU.add))
                elif h % 2 == 1 and d == 1:
                    dve.wait_ge(applied, 4 * s + 4)
                    c = h // 2
                    dve.scalar_tensor_tensor(out=m.XT[:, 6 + c, :], in0=g.XC[:, c, :], scalar=m.CP[:, C_DS + c:C_DS + c + 1], in1=m.ps[6 + c][:, :],
                                             op0=ALU.mult, op1=ALU.add).then_inc(y_out, 1)

            mask_row(0)
            for s, (kind, h, d, b) in enumerate(streams):
                if s + 1 < NS:
                    mask_row(s + 1)
                r = 32 * d + h + (4 if kind == "ssd" else 0)
                for j in range(NT):
                    i = 4 * s + j
                    dve.wait_ge(decay, i + 1)
                    dve.wait_ge(base_done, 4 * b + j + 1)
                    if i >= 4:
                        dve.wait_ge(applied, i - 3)
                    at = span(d, j)
                    if kind == "mlstm":
                        ins = dve.tensor_tensor(g.W[:, i % 4, at], g.E[:, i % 4, at], m.ps[j][:, at], ALU.mult)
                    else:
                        ins = dve.scalar_tensor_tensor(out=g.W[:, i % 4, at], in0=g.E[:, i % 4, at], scalar=g.GN[:, 2, j, r:r + 1],
                                                       in1=m.ps[j][:, at], op0=ALU.mult, op1=ALU.mult)
                    ins.then_inc(weighted, 1)
                    if j == 1 and s:
                        outputs(s - 1)
            outputs(NS - 1)
            dve.wait_ge(y_out, 2)


def mixer_norms(nc, m, mx, g):
    names = ("act_step", "dve_step", "y_squares", "y_sums", "y_inv", "h_squares", "h_var", "h_inv", "h_ready", "h_t")
    with stage(nc, "mixer_norms", *names) as (block, sems):
        act_step, dve_step, y_squares, y_sums, y_inv, h_squares, h_var, h_inv, h_ready, h_t = sems
        H = g.H[:, :, :, :].rearrange("p t h d -> p (t h) d")
        Hf = g.H[:, :, :, :].rearrange("p t h d -> p (t h d)")
        H2 = g.E[:, 0:2, :].rearrange("p a n -> p (a n)")
        mean = g.MEAN[:, 0, :]
        var = g.MEAN[:, 1, :]

        @block.vector
        def _(dve):
            link = Chain(dve, dve_step)
            Y = m.XT[:, 6:8, :].rearrange("p a n -> p (a n)")
            link(dve.tensor_tensor(Y, Y, mx.Z[:, :, :].rearrange("p a n -> p (a n)"), ALU.mult))
            dve.tensor_tensor(g.W[:, 0:2, :].rearrange("p a n -> p (a n)"), Y, Y, ALU.mult).then_inc(y_squares, 1)
            link(dve.reduce_sum(mean, H, AX.X))
            link(dve.tensor_scalar(mean, mean, 1.0 / 64, None, ALU.mult))
            link(dve.tensor_tensor(H, H, mean.rearrange("p (n a) -> p n a", a=1).to_broadcast([P, 16, 64]), ALU.subtract))
            link(dve.tensor_tensor(H2, Hf, Hf, ALU.mult))
            dve.reduce_sum(var, H2.rearrange("p (n d) -> p n d", d=64), AX.X).then_inc(h_var, 1)
            dve.wait_ge(y_inv, 2)
            for c in range(2):
                link(dve.scalar_tensor_tensor(out=m.XT[:, 6 + c, :], in0=m.XT[:, 6 + c, :], scalar=m.CP[:, C_SN + c:C_SN + c + 1],
                                              in1=g.RM[:, c, :], op0=ALU.mult, op1=ALU.mult))
            dve.wait_ge(h_inv, 1)
            link(dve.tensor_tensor(H, H, var.rearrange("p (n a) -> p n a", a=1).to_broadcast([P, 16, 64]), ALU.mult))
            H3 = g.H[:, :, :, :].rearrange("p t h d -> p t (h d)")
            link(dve.tensor_tensor(H3, H3, m.RP[:, R_MN:R_MN + 256].rearrange("p (a n) -> p a n", a=1).to_broadcast([P, NT, 256]), ALU.mult))
            dve.tensor_tensor(Hf, Hf, mx.O[:, :, :].rearrange("p t n -> p (t n)"), ALU.mult).then_inc(h_ready, 1)
            for c in range(2):
                dve.wait_ge(h_t, c + 1)
                link(dve.tensor_copy(m.XT[:, 4 + c, :], m.ps[2 + c][:, :]))

        @block.tensor
        def _(pe):
            pe.wait_ge(y_squares, 1)
            for c in range(2):
                pe.matmul(m.ps[c][:, :], m.ones[:, :], g.W[:, c, :], start=True, stop=True).then_inc(y_sums, 1)
            pe.wait_ge(h_ready, 1)
            H3 = g.H[:, :, :, :].rearrange("p t h d -> p t (h d)")
            for c in range(2):
                for t in range(NT):
                    last = pe.transpose(m.ps[2 + c][:, t * P:(t + 1) * P], H3[:, t, c * P:(c + 1) * P], m.ident[:, :])
                last.then_inc(h_t, 1)

        @block.scalar
        def _(act):
            link = Chain(act, act_step)
            for c in range(2):
                act.wait_ge(y_sums, c + 1)
                rstd(act, link, g.RM[:, c, :], m.ps[c][:, :], 1.0 / 128, 1e-6).then_inc(y_inv, 1)
            act.wait_ge(h_var, 1)
            rstd(act, link, var, var, 1.0 / 64, 1e-5).then_inc(h_inv, 1)


def norm_stage(nc, m, ln, which, layer, product=None):
    names = ("rows_in", "tile_done", "summed", "act_step", "dve_step", "var_ready", "inv_ready", "scaled", "pool_step")
    with stage(nc, "norm_stage", *names) as (block, sems):
        rows_in, tile_done, summed, act_step, dve_step, var_ready, inv_ready, scaled, pool_step = sems
        at = (R_L1, R_L2)[which]

        @block.sync
        def _(sp):
            sp.dma_start(ln.GB[:, :], m.d["rows"][bass.ds(layer, 1), at:at + 2 * D].to_broadcast([P, 2 * D])).then_inc(rows_in, 16)
            sp.wait_ge(rows_in, 16)

        @block.tensor
        def _(pe):
            if product:
                for half in range(2):
                    pe.wait_ge(m.ring_in[half], 48)
                for t in range(NT):
                    for half in range(2):
                        for k in range(KD):
                            last = pe.matmul(m.ps[2 * t + half][:, :], m.XT[:, k, t * P:(t + 1) * P],
                                             m.ring[:, half, k * S:(k + 1) * S], start=(k == 0), stop=(k == KD - 1))
                        last.then_inc(tile_done, 1)

        @block.vector
        def _(dve):
            link = Chain(dve, dve_step)
            for t in range(NT):
                for half in range(2):
                    cols = slice(half * S, (half + 1) * S)
                    if product:
                        dve.wait_ge(tile_done, 2 * t + half + 1)
                        y = m.ps[2 * t + half][:, :]
                    else:
                        y = ln.Y[:, t, cols]
                    link(dve.scalar_tensor_tensor(out=m.X[:, t, cols], in0=m.X[:, t, cols], scalar=ALPHA, in1=y, op0=ALU.mult, op1=ALU.add))
                    link(dve.bn_stats(ln.ST[:, t, half, :], m.X[:, t, cols]))
                link(dve.bn_aggr(ln.MV[:, t, :], ln.ST[:, t, :, :]))
                dve.sem_inc(var_ready, 1)
                dve.wait_ge(inv_ready, t + 1)
                link(dve.tensor_scalar(m.X[:, t, :], m.X[:, t, :], ln.MV[:, t, 0:1], ln.IV[:, t:t + 1], ALU.subtract, ALU.mult))
                if t == 0:
                    dve.wait_ge(rows_in, 16)
                link(dve.tensor_tensor(m.X[:, t, :], m.X[:, t, :], ln.GB[:, 0:D], ALU.mult))
                dve.sem_inc(scaled, 1)

        @block.scalar
        def _(act):
            link = Chain(act, act_step)
            for t in range(NT):
                act.wait_ge(var_ready, t + 1)
                rstd(act, link, ln.IV[:, t:t + 1], ln.MV[:, t, 1:2], 1.0, 1e-5).then_inc(inv_ready, 1)

        @block.gpsimd
        def _(pool):
            link = Chain(pool, pool_step)
            pool.wait_ge(rows_in, 16)
            for t in range(NT):
                pool.wait_ge(scaled, t + 1)
                link(pool.tensor_tensor(m.X[:, t, :], m.X[:, t, :], ln.GB[:, D:2 * D], ALU.add))


def router(nc, m, r):
    with stage(nc, "router", "logits_done", "dve_step", "exp_in", "exp_done") as (block, (logits_done, dve_step, exp_in, exp_done)):

        @block.tensor
        def _(pe):
            for t in range(NT):
                for k in range(KD):
                    last = pe.matmul(m.ps[0][:, t * 20:(t + 1) * 20], m.XT[:, k, t * P:(t + 1) * P], m.WR[:, k, :],
                                     start=(k == 0), stop=(k == KD - 1))
            last.then_inc(logits_done, 1)

        @block.vector
        def _(dve):
            link = Chain(dve, dve_step)

            def wide(x, n=4):
                return x.rearrange("p (t a) -> p t a", a=1).to_broadcast([P, NT, n])

            def first_max(hot, top, x):
                link(dve.reduce_max(top, x, AX.X))
                link(dve.tensor_tensor(hot, x, wide(top), ALU.is_equal))
                link(dve.tensor_tensor(hot, hot, m.CC[:, 4:8].rearrange("p (a n) -> p a n", a=1).to_broadcast([P, NT, 4]), ALU.mult))
                link(dve.reduce_max(r.t1[:, :], hot, AX.X))
                link(dve.tensor_tensor(hot, hot, wide(r.t1[:, :]), ALU.is_equal))

            lg = r.LG
            dve.wait_ge(logits_done, 1)
            link(dve.tensor_tensor(lg[:, :, :], m.ps[0][:, 0:80].rearrange("p (t n) -> p t n", t=NT),
                                   m.RP[:, R_RB:R_RB + 20].rearrange("p (a n) -> p a n", a=1).to_broadcast([P, NT, 20]), ALU.add))
            first_max(r.hg[:, :, :], r.gm[:, :], lg[:, :, 0:4])
            link(dve.tensor_tensor(r.e4[:, :, :], lg[:, :, 0:4], wide(r.gm[:, :]), ALU.subtract))
            for g in range(NGR):
                hot = r.hg[:, :, g:g + 1].to_broadcast([P, NT, 4])
                part = lg[:, :, 4 + 4 * g:8 + 4 * g]
                if g == 0:
                    link(dve.tensor_tensor(r.el[:, :, :], part, hot, ALU.mult))
                else:
                    link(dve.tensor_tensor(r.h2[:, :, :], part, hot, ALU.mult))
                    link(dve.tensor_tensor(r.el[:, :, :], r.el[:, :, :], r.h2[:, :, :], ALU.add))
            first_max(r.h1[:, :, :], r.m1[:, :], r.el[:, :, :])
            link(dve.scalar_tensor_tensor(out=r.el[:, :, :], in0=r.h1[:, :, :], scalar=NEG, in1=r.el[:, :, :], op0=ALU.mult, op1=ALU.add))
            first_max(r.h2[:, :, :], r.m2[:, :], r.el[:, :, :])
            link(dve.tensor_tensor(r.m2[:, :], r.m2[:, :], r.m1[:, :], ALU.subtract))
            dve.sem_inc(exp_in, 1)
            dve.wait_ge(exp_done, 2)
            link(dve.tensor_tensor(r.el[:, :, :], r.h1[:, :, :], r.h2[:, :, :], ALU.add))
            for g in range(NGR):
                link(dve.tensor_tensor(r.OH[:, :, 4 * g:4 * g + 4], r.el[:, :, :], r.hg[:, :, g:g + 1].to_broadcast([P, NT, 4]), ALU.mult))
            link(dve.reduce_sum(r.gm[:, :], r.e4[:, :, :], AX.X))
            link(dve.tensor_scalar(r.m1[:, :], r.m2[:, :], 1.0, None, ALU.add))
            link(dve.tensor_tensor(r.gm[:, :], r.gm[:, :], r.m1[:, :], ALU.mult))
            link(dve.reciprocal(r.gm[:, :], r.gm[:, :]))
            link(dve.tensor_tensor(r.m2[:, :], r.gm[:, :], r.m2[:, :], ALU.mult))
            link(dve.tensor_tensor(r.h1[:, :, :], r.h1[:, :, :], wide(r.gm[:, :]), ALU.mult))
            link(dve.tensor_tensor(r.h2[:, :, :], r.h2[:, :, :], wide(r.m2[:, :]), ALU.mult))
            link(dve.tensor_tensor(r.h1[:, :, :], r.h1[:, :, :], r.h2[:, :, :], ALU.add))
            for g in range(NGR):
                link(dve.tensor_tensor(r.COMB[:, :, 4 * g:4 * g + 4], r.h1[:, :, :], r.hg[:, :, g:g + 1].to_broadcast([P, NT, 4]), ALU.mult))

        @block.scalar
        def _(act):
            act.wait_ge(exp_in, 1)
            act.activation(r.e4[:, :, :], r.e4[:, :, :], ACT.Exp).then_inc(exp_done, 1)
            act.activation(r.m2[:, :], r.m2[:, :], ACT.Exp).then_inc(exp_done, 1)
            act.wait_ge(exp_done, 2)


def dispatch(nc, m, r):
    names = ("pe_rank", "pe_total", "dve_step", "x_hi", "x_lo", "act_step", "passes_out")
    with stage(nc, "dispatch", *names) as (block, (pe_rank, pe_total, dve_step, x_hi, x_lo, act_step, passes_out)):

        @block.tensor
        def _(pe):
            for t in range(NT):
                for u in range(t):
                    pe.matmul(m.ps[0][:, t * NE:(t + 1) * NE], m.ones[:, :], r.OH[:, u, :], start=(u == 0), stop=False)
                last = pe.matmul(m.ps[0][:, t * NE:(t + 1) * NE], r.TRI[:, :], r.OH[:, t, :], start=(t == 0), stop=True)
            last.then_inc(pe_rank, 1)
            for t in range(NT):
                last = pe.matmul(m.ps[1][:, 0:NE], m.ones[:, :], r.OH[:, t, :], start=(t == 0), stop=(t == NT - 1))
            last.then_inc(pe_total, 1)

        @block.vector
        def _(dve):
            link = Chain(dve, dve_step)
            dve.memset(r.POS[:, :, NE:], -10000.0)
            dve.wait_ge(pe_rank, 1)
            link(dve.tensor_scalar(r.POS[:, :, 0:NE], r.OH[:, :, :], 10000.0, -10000.0, ALU.mult, ALU.add))
            link(dve.tensor_tensor(r.POS[:, :, 0:NE], r.POS[:, :, 0:NE], m.ps[0][:, 0:NT * NE].rearrange("p (t e) -> p t e", t=NT), ALU.add))
            dve.wait_ge(pe_total, 1)
            link(dve.reduce_max(r.NP[:, 0:1], m.ps[1][:, 0:NE], AX.X))
            link(dve.tensor_scalar(r.NP[:, 1:2], r.NP[:, 0:1], 128.0, 1.0, ALU.is_gt, ALU.add))
            for n in (256.0, 384.0):
                link(dve.tensor_scalar(r.NP[:, 2:3], r.NP[:, 0:1], n, None, ALU.is_gt))
                link(dve.tensor_tensor(r.NP[:, 1:2], r.NP[:, 1:2], r.NP[:, 2:3], ALU.add))
            link(dve.tensor_copy(r.NPI[:, :], r.NP[:, 1:2]))
            link(dve.tensor_copy(r.CW[:, :, :, 0], r.COMB[:, :, :]))
            link(dve.tensor_tensor(r.CW[:, :, :, 1], r.COMB[:, :, :], r.CW[:, :, :, 0].bitcast(F32), ALU.subtract))
            link(dve.memset(r.Y[:, :, :], 0.0))
            for t in range(2, NT):
                dve.wait_ge(x_hi, t + 1)
                link(dve.tensor_tensor(r.XL[:, t, :], m.X[:, t, :], r.XH[:, t, :].bitcast(F32), ALU.subtract))

        @block.scalar
        def _(act):
            for t in range(NT):
                act.copy(r.XH[:, t, :], m.X[:, t, :]).then_inc(x_hi, 1)

        @block.gpsimd
        def _(pool):
            for t in range(2):
                pool.wait_ge(x_hi, t + 1)
                pool.tensor_tensor(r.XL[:, t, :], m.X[:, t, :], r.XH[:, t, :].bitcast(F32), ALU.subtract).then_inc(x_lo, 1)
            pool.wait_ge(x_lo, 2)


def experts(nc, m, r, layer):
    GE = NE // NGR
    names = ("gu_in0", "gu_in1", "dn_in0", "dn_in1", "sel_ready", "sel_free", "gathered", "xe_act", "xe_dve", "weights_done", "dve_step", "selt_done", "selt_home",
             "gate_up", "silu_done", "hidden", "ht_done", "ht_home", "down", "ye_hi", "ye_home", "scattered", "added")
    with stage(nc, "experts", *names) as (block, sems):
        (gu_in0, gu_in1, dn_in0, dn_in1, sel_ready, sel_free, gathered, xe_act, xe_dve, weights_done, dve_step, selt_done, selt_home,
         gate_up, silu_done, hidden, ht_done, ht_home, down, ye_hi, ye_home, scattered, added) = sems
        gu_in, dn_in = (gu_in0, gu_in1), (dn_in0, dn_in1)
        GU = KD * S
        XE = m.XT

        def load(sp, n, b, cols, arrived):
            sp.dma_start(m.ring[:, b, cols], m.d["w_exp"][bass.ds(layer, 1), bass.ds(n, 1), :, cols].rearrange("a b p n -> p (a b n)")).then_inc(arrived[b], 16)

        @block.sync
        def _(sp):
            for cols, arrived in ((slice(0, GU), gu_in), (slice(GU, SLOT), dn_in)):
                for b in range(2):
                    load(sp, b, b, cols, arrived)
            with sp.Fori(0, NE // 2 - 1) as i:
                for b in range(2):
                    sp.wait_ge(gate_up, i * 2 + b + 1)
                    load(sp, i * 2 + (b + 2), b, slice(0, GU), gu_in)
                    sp.wait_ge(down, i * 4 + 2 * (b + 1))
                    load(sp, i * 2 + (b + 2), b, slice(GU, SLOT), dn_in)

        @block.tensor
        def _(pe):
            with pe.Fori(0, NGR) as g:

                def gate_up_of(e):
                    pe.wait_ge(gu_in[e % 2], g * 32 + 16 * (e // 2 + 1))
                    if e >= 2:
                        pe.wait_ge(hidden, g * GE + e - 1)
                    for k in range(KD):
                        last = pe.matmul(m.ps[4 + e % 2][:, :], XE[:, k, e * P:(e + 1) * P], m.ring[:, e % 2, k * S:(k + 1) * S],
                                         start=(k == 0), stop=(k == KD - 1))
                    last.then_inc(gate_up, 1)

                def hidden_t(e):
                    pe.wait_ge(hidden, g * GE + e + 1)
                    for f in range(2):
                        last = pe.transpose(m.ps[6 + e % 2][:, f * P:(f + 1) * P], r.H[:, e % 2, f * P:(f + 1) * P], m.ident[:, :])
                    last.then_inc(ht_done, 1)

                def sel_t(e):
                    if e >= 2:
                        pe.wait_ge(selt_home, g * GE + e - 1)
                    for t in range(NT):
                        last = pe.transpose(m.ps[2 + e % 2][:, t * P:(t + 1) * P], r.SEL[:, t, e * P:(e + 1) * P].bitcast(F32), m.ident[:, :])
                    last.then_inc(selt_done, 1)

                def down_of(e):
                    pe.wait_ge(dn_in[e % 2], g * 32 + 16 * (e // 2 + 1))
                    pe.wait_ge(ht_home, g * GE + e + 1)
                    if e == 0:
                        pe.wait_ge(selt_home, g * GE + GE)
                    for half in range(2):
                        if e:
                            pe.wait_ge(ye_home, g * 8 + 2 * (e - 1) + half + 1)
                        for f in range(2):
                            at = 4096 + f * D + half * S
                            last = pe.matmul(m.ps[2 + half][:, :], r.HT[:, e % 2, f * P:(f + 1) * P], m.ring[:, e % 2, at:at + S], start=(f == 0), stop=(f == 1))
                        last.then_inc(down, 1)

                def scatter(pair):
                    pe.wait_ge(ye_home, g * 8 + 4 * (pair + 1))
                    for v in range(2 * NT):
                        t, half = divmod(v, 2)
                        pe.wait_ge(added, g * 16 + 8 * pair + v + 1)
                        n = 0
                        for e in range(2):
                            for part in range(2):
                                last = pe.matmul(m.ps[v % 2][:, :], r.SELT[:, 2 * pair + e, t * P:(t + 1) * P],
                                                 r.YE[:, part, e, half * S:(half + 1) * S], start=(n == 0), stop=(n == 3))
                                n += 1
                        last.then_inc(scattered, 1)

                pe.wait_ge(sel_ready, g * NT + NT)
                for k in range(KD):
                    if k < 2:
                        pe.wait_ge(added, g * 16 + k + 1)
                    else:
                        pe.wait_ge((xe_act, xe_dve)[k % 2], g * 4 + k // 2)
                    n = 0
                    for t in range(NT):
                        for part in (r.XH, r.XL):
                            last = pe.matmul(m.ps[k % 2][:, :], part[:, t, k * P:(k + 1) * P], r.SEL[:, t, :], start=(n == 0), stop=(n == 7))
                            n += 1
                    last.then_inc(gathered, 1)
                for e in range(GE):
                    for t in range(NT):
                        last = pe.matmul(m.ps[7][:, 2 * e:2 * e + 2], r.SEL[:, t, e * P:(e + 1) * P],
                                         r.CW[:, t, bass.ds(g * GE + e, 1), :].rearrange("p a b -> p (a b)"), start=(t == 0), stop=(t == NT - 1))
                last.then_inc(weights_done, 1)
                sel_t(0)
                sel_t(1)
                pe.wait_ge(xe_act, g * 4 + 4)
                pe.wait_ge(xe_dve, g * 4 + 4)
                gate_up_of(0)
                sel_t(2)
                gate_up_of(1)
                hidden_t(0)
                sel_t(3)
                down_of(0)
                hidden_t(1)
                gate_up_of(2)
                down_of(1)
                gate_up_of(3)
                hidden_t(2)
                scatter(0)
                hidden_t(3)
                down_of(2)
                down_of(3)
                scatter(1)

        @block.scalar
        def _(act):
            with act.Fori(0, NGR) as g:

                def silu(e):
                    act.wait_ge(gate_up, g * GE + e + 1)
                    act.activation(r.SG[:, e % 2, :], m.ps[4 + e % 2][:, 0:FE], ACT.Silu).then_inc(silu_done, 1)

                def sel_home(e):
                    act.wait_ge(selt_done, g * GE + e + 1)
                    if e == GE - 1:
                        act.sem_inc(sel_free, 1)
                    act.copy(r.SELT[:, e, :], m.ps[2 + e % 2][:, :]).then_inc(selt_home, 1)

                def hidden_home(e):
                    act.wait_ge(ht_done, g * GE + e + 1)
                    act.copy(r.HT[:, e % 2, :], m.ps[6 + e % 2][:, 0:2 * P]).then_inc(ht_home, 1)

                def high_part(e):
                    for half in range(2):
                        act.wait_ge(down, g * 8 + 2 * e + half + 1)
                        act.copy(r.YE[:, 0, e % 2, half * S:(half + 1) * S], m.ps[2 + half][:, :]).then_inc(ye_hi, 1)

                for k in range(0, KD, 2):
                    act.wait_ge(gathered, g * KD + k + 1)
                    act.copy(XE[:, k, :], m.ps[0][:, :]).then_inc(xe_act, 1)
                sel_home(0)
                sel_home(1)
                silu(0)
                sel_home(2)
                silu(1)
                hidden_home(0)
                sel_home(3)
                high_part(0)
                hidden_home(1)
                silu(2)
                high_part(1)
                silu(3)
                hidden_home(2)
                hidden_home(3)
                high_part(2)
                high_part(3)

        @block.vector
        def _(dve):
            dve.sem_inc(added, 2)

            def select(turn):
                for t in range(NT):
                    for e in range(GE):
                        at = r.POS[:, t, e:e + 1] if turn is None else r.POS[:, t, bass.ds(turn * GE + (GE + e), 1)]
                        last = dve.tensor_scalar(r.SEL[:, t, e * P:(e + 1) * P], r.IOTA[:, :], at, None, ALU.is_equal)
                    last.then_inc(sel_ready, 1)

            select(None)
            with dve.Fori(0, NGR) as g:

                def hidden_of(e):
                    dve.wait_ge(silu_done, g * GE + e + 1)
                    dve.scalar_tensor_tensor(out=r.H[:, e % 2, :], in0=m.ps[4 + e % 2][:, FE:2 * FE], scalar=r.WS[:, e:e + 1],
                                             in1=r.SG[:, e % 2, :], op0=ALU.mult, op1=ALU.mult).then_inc(hidden, 1)

                def low_part(e):
                    for half in range(2):
                        cols = slice(half * S, (half + 1) * S)
                        dve.wait_ge(ye_hi, g * 8 + 2 * e + half + 1)
                        dve.tensor_tensor(r.YE[:, 1, e % 2, cols], m.ps[2 + half][:, :], r.YE[:, 0, e % 2, cols].bitcast(F32),
                                          ALU.subtract).then_inc(ye_home, 1)

                def add(pair):
                    for v in range(2 * NT):
                        t, cols = v // 2, slice((v % 2) * S, (v % 2 + 1) * S)
                        dve.wait_ge(scattered, g * 16 + 8 * pair + v + 1)
                        dve.wait_ge(added, g * 16 + 8 * pair + v + 2)
                        dve.tensor_tensor(r.Y[:, t, cols], r.Y[:, t, cols], m.ps[v % 2][:, :], ALU.add).then_inc(added, 1)

                for k in range(1, KD, 2):
                    dve.wait_ge(gathered, g * KD + k + 1)
                    dve.tensor_copy(XE[:, k, :], m.ps[1][:, :]).then_inc(xe_dve, 1)
                dve.wait_ge(weights_done, g + 1)
                dve.reduce_sum(r.WS[:, :], m.ps[7][:, 0:2 * GE].rearrange("p (e a) -> p e a", a=2), AX.X).then_inc(dve_step, 1)
                dve.wait_ge(dve_step, g + 1)
                hidden_of(0)
                hidden_of(1)
                low_part(0)
                dve.wait_ge(sel_free, g + 1)
                select(g)
                hidden_of(2)
                low_part(1)
                hidden_of(3)
                add(0)
                low_part(2)
                low_part(3)
                add(1)


def next_pass(nc, r):
    with stage(nc, "next_pass", "moved") as (block, (moved,)):

        @block.vector
        def _(dve):
            dve.tensor_scalar(r.POS[:, :, :], r.POS[:, :, :], -float(P), None, ALU.add).then_inc(moved, 1)
            dve.wait_ge(moved, 1)


GH, GD = 4, 128
FF = 4096
K_NM, K_NP, K_GC, K_LC, K_LB, K_AB, K_XB, K_AP, K_GN, K_AL, K_DB, K_N = 0, 8, 16, 64, 80, 84, 88, 92, 96, 97, 98, 99


def rms_transpose(nc, m, n, XS, gain, extra=None):
    names = ("squared", "inv", "act_step", "dve_step", "normed", "transposed", "xt_act", "xt_dve", "param_in")
    with stage(nc, "rms_transpose", *names) as (block, (squared, inv, act_step, dve_step, normed, transposed, xt_act, xt_dve, param_in)):

        @block.sync
        def _(sp):
            if extra:
                sp.wait_ge(param_in, 16 * extra(sp, param_in))

        @block.scalar
        def _(act):
            link = Chain(act, act_step)
            for t in range(NT):
                link(act.activation(n.XN[:, t, :], m.X[:, t, :], ACT.Square, accum_out=n.SS[:, t:t + 1]))
            rstd(act, link, n.SS[:, :], n.SS[:, :], 1.0 / D, 1e-6).then_inc(inv, 1)
            if extra:
                act.wait_ge(param_in, 16)
            for k in range(KD):
                act.wait_ge(transposed, k + 1)
                act.activation(XS[:, 0, k, :], m.ps[k][:, :], ACT.Copy, scale=m.CP[:, gain + k:gain + k + 1]).then_inc(xt_act, 1)
            act.wait_ge(xt_act, KD)

        @block.vector
        def _(dve):
            dve.wait_ge(inv, 1)
            for t in range(NT):
                dve.tensor_scalar(n.XN[:, t, :], m.X[:, t, :], n.SS[:, t:t + 1], None, ALU.mult).then_inc(normed, 1)
            if extra:
                dve.wait_ge(param_in, 16)
            for k in range(KD):
                dve.wait_ge(xt_act, k + 1)
                dve.scalar_tensor_tensor(out=XS[:, 1, k, :], in0=m.ps[k][:, :], scalar=m.CP[:, gain + k:gain + k + 1],
                                         in1=XS[:, 0, k, :].bitcast(F32), op0=ALU.mult, op1=ALU.subtract).then_inc(xt_dve, 1)
            dve.wait_ge(xt_dve, KD)

        @block.tensor
        def _(pe):
            for k in range(KD):
                for t in range(NT):
                    if k == 0:
                        pe.wait_ge(normed, t + 1)
                    last = pe.transpose(m.ps[k][:, t * P:(t + 1) * P], n.XN[:, t, k * P:(k + 1) * P], m.ident[:, :])
                last.then_inc(transposed, 1)


def in_projection_2(nc, m, b, q):
    names = ("unit_done", "home_act", "home_dve", "w_high", "w_low", "raw0", "raw1", "raw2", "raw3")
    with stage(nc, "in_projection_2", *names) as (block, (unit_done, home_act, home_dve, w_high, w_low, *raw)):
        homes = [q.QB[:, c, 3:3 + S] for c in range(12)] + [b.Z[:, c, :] for c in range(4)]
        homes += [b.LX[:, c, 3:3 + S] for c in range(4)] + [b.LG[:, c, :] for c in range(4)]
        NU = len(homes) + 1
        NB = NU // 2 + 1
        sizes = [KD * 256] * (NB - 1) + [KD * GR]

        @block.sync
        def _(sp):
            for i in range(NB):
                if i >= 4:
                    sp.wait_ge(w_low, i - 3)
                src = m.d["w_in_2"][i] if i < NB - 1 else m.d["w_gates_2"]
                sp.dma_start(q.ring[:, i % 4, 0:sizes[i]], src).then_inc(raw[i % 4], 16)

        @block.tensor
        def _(pe):
            for u in range(NU):
                i, c = divmod(u, 2)
                if c == 0:
                    pe.wait_ge(w_low, i + 1)
                if u >= 8:
                    pe.wait_ge((home_act, home_dve)[u % 2], (u - 8) // 2 + 1)
                width, n = (GR, GR) if u == NU - 1 else (256, P)
                step = 0
                for k in range(KD):
                    for hw, hx in TERMS:
                        at = k * width + c * P
                        last = pe.matmul(m.ps[u % 8][0:n, :], q.WS[:, i % 2, hw, at:at + n], b.XS[:, hx, k, :], start=(step == 0), stop=(step == 3 * KD - 1))
                        step += 1
                last.then_inc(unit_done, 1)

        @block.scalar
        def _(act):
            for i in range(NB):
                act.wait_ge(raw[i % 4], 16 * (i // 4 + 1))
                if i >= 2:
                    act.wait_ge(unit_done, 2 * (i - 1))
                act.copy(q.WS[:, i % 2, 0, 0:sizes[i]], q.ring[:, i % 4, 0:sizes[i]]).then_inc(w_high, 1)
                if i:
                    u = 2 * i - 2
                    act.wait_ge(unit_done, u + 1)
                    act.copy(homes[u], m.ps[u % 8][:, :]).then_inc(home_act, 1)
            act.wait_ge(unit_done, NU)
            act.copy(b.GR[0:GR, :], m.ps[(NU - 1) % 8][0:GR, :]).then_inc(home_act, 1)
            act.wait_ge(home_act, (NU + 1) // 2)

        @block.vector
        def _(dve):
            for u in range(1, NU, 2):
                dve.wait_ge(unit_done, u + 1)
                dve.tensor_copy(homes[u], m.ps[u % 8][:, :]).then_inc(home_dve, 1)
            dve.wait_ge(home_dve, NU // 2)

        @block.gpsimd
        def _(pool):
            pool.memset(q.QB[:, :, 0:3], 0.0)
            pool.memset(b.LX[:, :, 0:3], 0.0)
            for i in range(NB):
                n = sizes[i]
                pool.wait_ge(w_high, i + 1)
                pool.tensor_tensor(q.WS[:, i % 2, 1, 0:n], q.ring[:, i % 4, 0:n], q.WS[:, i % 2, 0, 0:n].bitcast(F32), ALU.subtract).then_inc(w_low, 1)


def gdn_prepare(nc, m, b, q):
    names = ("act_step", "dve_step", "conv_done", "silu_done", "squares", "sums", "logs", "inv", "biased", "abs_ready", "log_ready",
             "rows_a", "rows_b", "rows_c", "rows_t")
    with stage(nc, "gdn_prepare", *names) as (block, sems):
        act_step, dve_step, conv_done, silu_done, squares, sums, logs, inv, biased, abs_ready, log_ready, rows_a, rows_b, rows_c, rows_t = sems
        R = slice(0, GH)

        @block.vector
        def _(dve):
            link = Chain(dve, dve_step)
            dve.wait_ge(biased, 1)
            dve.scalar_tensor_tensor(out=b.G1[R, :], in0=b.GR[R, :], scalar=-1.0, in1=b.GR[R, :], op0=ALU.mult, op1=ALU.min).then_inc(abs_ready, 1)
            dve.wait_ge(log_ready, 1)
            link(dve.scalar_tensor_tensor(out=b.G1[R, :], in0=b.GR[R, :], scalar=0.0, in1=b.G1[R, :], op0=ALU.max, op1=ALU.add))
            link(dve.tensor_scalar(b.G1[R, :], b.G1[R, :], b.CO[R, 0:1], None, ALU.mult))
            for c in range(NT):
                at = slice(c * P, (c + 1) * P)
                link(dve.tensor_tensor_scan(b.GC[R, at], m.zeros[R, at], b.G1[R, at], 0.0, ALU.add, ALU.add))
            link(dve.tensor_scalar(b.GM[R, :], b.GC[R, :], -1.0, None, ALU.mult))
            last_of_chunk = b.GC[R, :].rearrange("p (c n) -> p c n", c=NT)[:, :, P - 1:P].to_broadcast([GH, NT, P])
            link(dve.tensor_tensor(b.G1[R, :].rearrange("p (c n) -> p c n", c=NT), last_of_chunk,
                                   b.GC[R, :].rearrange("p (c n) -> p c n", c=NT), ALU.subtract))
            dve.sem_inc(rows_a, 1)
            dve.wait_ge(rows_b, 1)
            link(dve.tensor_tensor(b.BE[R, :], b.BT[R, :], b.EG[R, :], ALU.mult))
            dve.sem_inc(rows_c, 1)
            for c in range(12):
                for tap in range(4):
                    w = m.CP[:, K_GC + 4 * c + tap:K_GC + 4 * c + tap + 1]
                    src = q.QB[:, c, tap:tap + S]
                    if tap == 0:
                        link(dve.tensor_scalar(b.XC[:, c, :], src, w, None, ALU.mult))
                    else:
                        link(dve.scalar_tensor_tensor(out=b.XC[:, c, :], in0=src, scalar=w, in1=b.XC[:, c, :], op0=ALU.mult, op1=ALU.add))
                dve.sem_inc(conv_done, 1)
                if c == 0:
                    dve.wait_ge(rows_t, 1)
                    link(dve.tensor_copy(b.GN[:, :], m.ps[7][:, 0:64]))
                elif c <= 8:
                    n = c - 1
                    if n >= 2:
                        dve.wait_ge(sums, n - 1)
                    dve.wait_ge(silu_done, n + 1)
                    dve.tensor_tensor(q.SQ[:, n % 2, :], b.XC[:, n, :], b.XC[:, n, :], ALU.mult).then_inc(squares, 1)
            for c in range(8):
                dve.wait_ge(inv, c + 1)
                link(dve.scalar_tensor_tensor(out=b.XC[:, c, :], in0=b.XC[:, c, :], scalar=(GD ** -0.5 if c < 4 else 1.0),
                                              in1=q.RS[:, c, :], op0=ALU.mult, op1=ALU.mult))

        @block.scalar
        def _(act):
            link = Chain(act, act_step)
            link(act.activation(b.BT[R, :], b.GR[32:32 + GH, :], ACT.Sigmoid))
            link(act.activation(b.CO[R, 0:1], m.CP[R, K_AL:K_AL + 1], ACT.Exp))
            link(act.mul(b.CO[R, 0:1], b.CO[R, 0:1], -1.0))
            link(act.activation(b.GR[R, :], b.GR[R, :], ACT.Identity, bias=m.CP[R, K_DB:K_DB + 1]))
            act.sem_inc(biased, 1)
            act.wait_ge(abs_ready, 1)
            link(act.activation(b.G1[R, :], b.G1[R, :], ACT.Exp))
            act.activation(b.G1[R, :], b.G1[R, :], ACT.Ln, bias=1.0).then_inc(log_ready, 1)
            act.wait_ge(rows_a, 1)
            link(act.activation(b.EG[R, :], b.GC[R, :], ACT.Exp))
            link(act.activation(b.DK[R, :], b.G1[R, :], ACT.Exp))
            act.sem_inc(rows_b, 1)
            for c in range(12):
                act.wait_ge(conv_done, c + 1)
                act.activation(b.XC[:, c, :], b.XC[:, c, :], ACT.Silu).then_inc(silu_done, 1)
            act.wait_ge(silu_done, 12)
            for c in range(8):
                act.wait_ge(sums, c + 1)
                act.activation(q.RS[:, c, :], m.ps[c][:, :], ACT.Ln, bias=1e-6).then_inc(logs, 1)
            for c in range(8):
                act.wait_ge(logs, c + 1)
                act.activation(q.RS[:, c, :], q.RS[:, c, :], ACT.Exp, scale=-0.5).then_inc(inv, 1)

        @block.tensor
        def _(pe):
            pe.wait_ge(rows_c, 1)
            for n, rows in enumerate((b.GM, b.BT, b.BE, b.DK)):
                for t in range(NT):
                    at = (n * NT + t) * GH
                    last = pe.transpose(m.ps[7][:, at:at + GH], rows[R, t * P:(t + 1) * P], m.ident[0:GH, 0:GH])
            last.then_inc(rows_t, 1)
            for c in range(8):
                pe.wait_ge(squares, c + 1)
                pe.matmul(m.ps[c][:, :], m.ones[:, :], q.SQ[:, c % 2, :], start=True, stop=True).then_inc(sums, 1)


def gdn_matrices(nc, m, b, w):
    names = ("dve_step", "nat_done", "nat_home", "row_done", "row_used", "masked", "decay", "tri_done", "tri_home", "ready")
    with stage(nc, "gdn_matrices", *names) as (block, sems):
        dve_step, nat_done, nat_home, row_done, row_used, masked, decay, tri_done, tri_home, ready = sems
        rows = [b.GC, b.BT, b.EG]

        @block.sync
        def _(sp):
            sp.dma_start(w.LM[:, :, :], m.d["level_masks"]).then_inc(ready, 16)
            sp.wait_ge(ready, 16)

        @block.tensor
        def _(pe):
            for c in range(NT):
                for x in range(2):
                    if c >= 2:
                        pe.wait_ge(nat_home, 2 * (c - 2) + x + 1)
                    for h in range(GH):
                        last = pe.transpose(m.ps[2 * x + c % 2][:, h * P:(h + 1) * P], b.XC[:, 4 * (x + 1) + h, c * P:(c + 1) * P], m.ident[:, :])
                    last.then_inc(nat_done, 1)
            for h in range(GH):
                for n in range(3):
                    i = 3 * h + n
                    if i >= 4:
                        pe.wait_ge(row_used, i - 3)
                    pe.matmul(m.ps[4 + i % 4][:, :], m.ident[0:GH, h:h + 1].to_broadcast([GH, P]), rows[n][0:GH, :], start=True, stop=True).then_inc(row_done, 1)
            pe.wait_ge(row_used, 12)
            pe.wait_ge(nat_home, 8)
            for c in range(NT):
                at = slice(c * P, (c + 1) * P)
                for x, right in enumerate((w.KB, None)):
                    i = 2 * c + x
                    if i >= 4:
                        pe.wait_ge(tri_home, i - 3)
                    for h in range(GH):
                        rhs = w.KB[:, h, at] if x == 0 else b.XC[:, h, at]
                        last = pe.matmul(m.ps[i % 4][:, h * P:(h + 1) * P], b.XC[:, 4 + h, at], rhs, start=True, stop=True)
                    last.then_inc(tri_done, 1)

        @block.vector
        def _(dve):
            link = Chain(dve, dve_step)

            def per_head(kind, c):
                at = (kind * NT + c) * GH
                return b.GN[:, at:at + GH].rearrange("p (h a) -> p h a", a=1).to_broadcast([P, GH, P])

            for c in range(NT):
                dve.wait_ge(nat_done, 2 * c + 1)
                k = m.ps[c % 2][:, :].rearrange("p (h n) -> p h n", h=GH)
                link(dve.tensor_tensor(w.KE[:, c, :, :], k, per_head(2, c), ALU.mult))
                dve.tensor_tensor(w.KD[:, c, :, :], k, per_head(3, c), ALU.mult).then_inc(nat_home, 1)
                dve.wait_ge(nat_done, 2 * c + 2)
                v = m.ps[2 + c % 2][:, :].rearrange("p (h n) -> p h n", h=GH)
                dve.tensor_tensor(w.VB[:, c, :, :], v, per_head(1, c), ALU.mult).then_inc(nat_home, 1)
            for h in range(GH):
                i = 3 * h
                dve.wait_ge(row_done, i + 1)
                dve.tensor_tensor(blocks(w.RM[:, h, :]), blocks(m.ps[4 + i % 4][:, :]), every_block(m.mask[:, 0, :]), ALU.add).then_inc(row_used, 1)
                dve.wait_ge(row_done, i + 2)
                dve.tensor_tensor(w.KB[:, h, :], m.ps[4 + (i + 1) % 4][:, :], b.XC[:, 4 + h, :], ALU.mult).then_inc(row_used, 1)
                dve.wait_ge(row_done, i + 3)
                link(dve.tensor_tensor(w.QE[:, h, :], m.ps[4 + (i + 2) % 4][:, :], b.XC[:, h, :], ALU.mult))
                dve.tensor_copy(w.GL[:, h, :], m.ps[4 + (i + 2) % 4][:, P - 1:S:P]).then_inc(row_used, 1)
            for c in range(NT):
                dve.wait_ge(decay, GH * NT)
                for x, out in enumerate((w.AT, w.AQ)):
                    dve.wait_ge(tri_done, 2 * c + x + 1)
                    dve.tensor_tensor(out[:, c, :, :].rearrange("p h n -> p (h n)"), m.ps[(2 * c + x) % 4][:, :],
                                      w.E[:, c, :, :].rearrange("p h n -> p (h n)"), ALU.mult).then_inc(tri_home, 1)
            for c in range(NT):
                for out in (w.T, w.U):
                    link(dve.tensor_copy(out[:, c, :, :], m.ident[:, :].rearrange("p (a n) -> p a n", a=1).to_broadcast([P, GH, P])))
            dve.wait_ge(tri_home, 8)

        @block.scalar
        def _(act):
            for h in range(GH):
                act.wait_ge(row_used, 3 * h + 1)
                for c in range(NT):
                    act.activation(w.E[:, c, h, :], w.RM[:, h, c * P:(c + 1) * P], ACT.Exp, bias=b.GN[:, c * GH + h:c * GH + h + 1]).then_inc(decay, 1)


def gdn_inverse(nc, m, w):
    LEVELS = 7
    with stage(nc, "gdn_inverse", "z_done", "z_home", "t_done", "u_done", "tu_home") as (block, (z_done, z_home, t_done, u_done, tu_home)):

        @block.tensor
        def _(pe):
            with pe.Fori(0, LEVELS) as level:
                for c in range(NT):
                    pe.wait_ge(tu_home, level * 8 + 2 * c + 2)
                    for h in range(GH):
                        last = pe.matmul(m.ps[c][:, h * P:(h + 1) * P], w.AT[:, c, h, :], w.T[:, c, h, :], start=True, stop=True)
                    last.then_inc(z_done, 1)
                for c in range(NT):
                    pe.wait_ge(z_home, level * NT + c + 1)
                    for h in range(GH):
                        last = pe.matmul(m.ps[4 + c][:, h * P:(h + 1) * P], w.U[:, c, h, :], w.Z[:, c, h, :], start=True, stop=True)
                    last.then_inc(t_done, 1)
                    for h in range(GH):
                        last = pe.matmul(m.ps[c][:, h * P:(h + 1) * P], w.Z[:, c, h, :], w.U[:, c, h, :], start=True, stop=True)
                    last.then_inc(u_done, 1)

        @block.vector
        def _(dve):
            dve.sem_inc(tu_home, 8)
            with dve.Fori(0, LEVELS) as level:
                for c in range(NT):
                    dve.wait_ge(z_done, level * NT + c + 1)
                    mask = w.LM[:, bass.ds(level, 1), :].to_broadcast([P, GH, P])
                    dve.tensor_tensor(w.Z[:, c, :, :], m.ps[c][:, :].rearrange("p (h n) -> p h n", h=GH), mask, ALU.mult).then_inc(z_home, 1)
                for c in range(NT):
                    for x, (done, bank, out) in enumerate(((t_done, 4 + c, w.T), (u_done, c, w.U))):
                        dve.wait_ge(u_done, level * NT + c + 1)
                        flat = out[:, c, :, :].rearrange("p h n -> p (h n)")
                        dve.tensor_tensor(flat, flat, m.ps[bank][:, :], ALU.add).then_inc(tu_home, 1)


def gdn_sequence(nc, m, b, w):
    with stage(nc, "gdn_sequence", "w_done", "w_home", "v_done", "v_home", "o_done", "o_home", "s_done", "s_home", "dve_step") as (block, sems):
        w_done, w_home, v_done, v_home, o_done, o_home, s_done, s_home, dve_step = sems

        @block.tensor
        def _(pe):
            for c in range(1, NT):
                for h in range(GH):
                    last = pe.matmul(m.ps[c][:, h * P:(h + 1) * P], w.KE[:, c, h, :], w.U[:, c, h, :], start=True, stop=True)
                last.then_inc(w_done, 1)
            for c in range(NT):
                at = slice(c * P, (c + 1) * P)
                if c:
                    pe.wait_ge(w_home, c)
                    pe.wait_ge(s_home, c)
                    pe.wait_ge(v_home, c)
                for h in range(GH):
                    last = pe.matmul(m.ps[4][:, h * P:(h + 1) * P], w.U[:, c, h, :], w.VB[:, c, h, :], start=True, stop=(c == 0))
                    if c:
                        last = pe.matmul(m.ps[4][:, h * P:(h + 1) * P], w.NW[:, c, h, :], w.S[:, h, :], start=False, stop=True)
                last.then_inc(v_done, 1)
                pe.wait_ge(v_home, c + 1)
                if c:
                    pe.wait_ge(o_home, c)
                for h in range(GH):
                    if c:
                        pe.matmul(m.ps[5][:, h * P:(h + 1) * P], w.S[:, h, :], w.QE[:, h, at], start=True, stop=False)
                    last = pe.matmul(m.ps[5][:, h * P:(h + 1) * P], w.VN[:, h, :], w.AQ[:, c, h, :], start=(c == 0), stop=True)
                last.then_inc(o_done, 1)
                if c < NT - 1:
                    for h in range(GH):
                        last = pe.matmul(m.ps[6][:, h * P:(h + 1) * P], w.KD[:, c, h, :], w.VN[:, h, :], start=True, stop=True)
                    last.then_inc(s_done, 1)

        @block.vector
        def _(dve):
            link = Chain(dve, dve_step)
            for c in range(NT):
                dve.wait_ge(v_done, c + 1)
                if c:
                    dve.wait_ge(s_done, c)
                dve.tensor_copy(w.VN[:, :, :].rearrange("p h n -> p (h n)"), m.ps[4][:, :]).then_inc(v_home, 1)
                if c < NT - 1:
                    S_ = w.S[:, :, :].rearrange("p h n -> p (h n)")
                    dve.wait_ge(s_done, c + 1)
                    if c == 0:
                        dve.tensor_copy(S_, m.ps[6][:, :]).then_inc(s_home, 1)
                        dve.wait_ge(s_home, 1)
                    else:
                        link(dve.tensor_tensor(w.S[:, :, :], w.S[:, :, :], w.GL[:, :, c:c + 1].to_broadcast([P, GH, P]), ALU.mult))
                        dve.tensor_tensor(S_, S_, m.ps[6][:, :], ALU.add).then_inc(s_home, 1)
                        dve.wait_ge(s_home, c + 1)

        @block.scalar
        def _(act):
            for c in range(1, NT):
                act.wait_ge(w_done, c)
                act.mul(w.NW[:, c, :, :].rearrange("p h n -> p (h n)"), m.ps[c][:, :], -1.0).then_inc(w_home, 1)
            for c in range(NT):
                act.wait_ge(o_done, c + 1)
                act.copy(w.OT[:, :, c * P:(c + 1) * P], m.ps[5][:, :].rearrange("p (h n) -> p h n", h=GH)).then_inc(o_home, 1)
            act.wait_ge(o_home, NT)


def gdn_norm(nc, m, b, w):
    with stage(nc, "gdn_norm", "act_step", "dve_step", "squares", "sums", "inv", "silu_done") as (block, sems):
        act_step, dve_step, squares, sums, inv, silu_done = sems

        @block.vector
        def _(dve):
            link = Chain(dve, dve_step)
            for h in range(GH):
                dve.tensor_tensor(w.KB[:, h, :], w.OT[:, h, :], w.OT[:, h, :], ALU.mult).then_inc(squares, 1)
            for h in range(GH):
                dve.wait_ge(inv, h + 1)
                dve.wait_ge(silu_done, h + 1)
                link(dve.scalar_tensor_tensor(out=w.OT[:, h, :], in0=w.OT[:, h, :], scalar=m.CP[:, K_GN:K_GN + 1], in1=w.QE[:, h, :],
                                              op0=ALU.mult, op1=ALU.mult))
                link(dve.tensor_tensor(m.XT[:, h, :], w.OT[:, h, :], b.Z[:, h, :], ALU.mult))

        @block.tensor
        def _(pe):
            for h in range(GH):
                pe.wait_ge(squares, h + 1)
                pe.matmul(m.ps[h][:, :], m.ones[:, :], w.KB[:, h, :], start=True, stop=True).then_inc(sums, 1)

        @block.scalar
        def _(act):
            link = Chain(act, act_step)
            for h in range(GH):
                act.activation(b.Z[:, h, :], b.Z[:, h, :], ACT.Silu).then_inc(silu_done, 1)
            for h in range(GH):
                act.wait_ge(sums, h + 1)
                rstd(act, link, w.QE[:, h, :], m.ps[h][:, :], 1.0 / GD, 1e-6).then_inc(inv, 1)


def lru(nc, m, b, u):
    names = ("act_step", "dve_step", "gate_w_in", "conv_done", "gates_done", "gates_home", "decay_arg", "decay_done", "root_arg", "root_done", "gelu_done")
    with stage(nc, "lru", *names) as (block, sems):
        act_step, dve_step, gate_w_in, conv_done, gates_done, gates_home, decay_arg, decay_done, root_arg, root_done, gelu_done = sems

        @block.sync
        def _(sp):
            sp.dma_start(u.WA[:, :, :], m.d["lru_w"]).then_inc(gate_w_in, 16)
            sp.wait_ge(gate_w_in, 16)

        @block.vector
        def _(dve):
            link = Chain(dve, dve_step)
            for c in range(4):
                for tap in range(4):
                    w = m.CP[:, K_LC + 4 * c + tap:K_LC + 4 * c + tap + 1]
                    src = b.LX[:, c, tap:tap + S]
                    if tap == 0:
                        link(dve.tensor_scalar(u.XR[:, c, :], src, w, m.CP[:, K_LB + c:K_LB + c + 1], ALU.mult, ALU.add))
                    else:
                        link(dve.scalar_tensor_tensor(out=u.XR[:, c, :], in0=src, scalar=w, in1=u.XR[:, c, :], op0=ALU.mult, op1=ALU.add))
                dve.sem_inc(conv_done, 1)
            for c in range(4):
                dve.wait_ge(gates_home, 2 * c + 3)
                dve.tensor_scalar(u.RG[:, c, :], u.RG[:, c, :], u.SPA[:, c:c + 1], None, ALU.mult).then_inc(decay_arg, 1)
            for c in range(4):
                dve.wait_ge(decay_done, 2 * c + 2)
                link(dve.tensor_scalar(u.TH[:, 1, :], u.RT[:, c, :], 1.0, None, ALU.add))
                link(dve.reciprocal(u.TH[:, 1, :], u.TH[:, 1, :]))
                dve.scalar_tensor_tensor(out=u.RT[:, c, :], in0=u.RT[:, c, :], scalar=2.0, in1=u.TH[:, 1, :], op0=ALU.mult, op1=ALU.mult).then_inc(root_arg, 1)
                link(dve.tensor_tensor(u.XR[:, c, :], u.XR[:, c, :], u.IG[:, c, :], ALU.mult))
            for c in range(4):
                dve.wait_ge(root_done, c + 1)
                link(dve.tensor_tensor(u.XR[:, c, :], u.XR[:, c, :], u.RT[:, c, :], ALU.mult))
                link(dve.tensor_tensor_scan(u.RT[:, c, :], u.RG[:, c, :], u.XR[:, c, :], 0.0, ALU.mult, ALU.add))
                dve.wait_ge(gelu_done, c + 1)
                link(dve.tensor_tensor(m.XT[:, 4 + c, :], u.RT[:, c, :], b.LG[:, c, :], ALU.mult))

        @block.tensor
        def _(pe):
            pe.wait_ge(gate_w_in, 16)
            for c in range(4):
                pe.wait_ge(conv_done, c + 1)
                for x in range(2):
                    for half in range(2):
                        rows = slice(64 * half, 64 * half + 64)
                        last = pe.matmul(m.ps[2 * c + x][rows, :], u.WA[rows, 2 * c + x, :], u.XR[rows, c, :], start=True, stop=True)
                    last.then_inc(gates_done, 1)

        @block.scalar
        def _(act):
            link = Chain(act, act_step)
            a = m.CP[:, K_AP:K_AP + 4]
            link(act.activation(u.AB[:, 0:4], a, ACT.Abs))
            link(act.activation(u.AB[:, 0:4], u.AB[:, 0:4], ACT.Exp, scale=-1.0))
            link(act.activation(u.AB[:, 0:4], u.AB[:, 0:4], ACT.Ln, bias=1.0))
            link(act.activation(u.AB[:, 4:8], a, ACT.Relu, scale=-1.0))
            for c in range(4):
                link(act.activation(u.AB[:, c:c + 1], u.AB[:, c:c + 1], ACT.Identity, bias=u.AB[:, 4 + c:5 + c]))
            act.activation(u.SPA[:, :], u.AB[:, 0:4], ACT.Copy, scale=8.0).then_inc(gates_home, 1)
            for c in range(4):
                for x, out in enumerate((u.RG, u.IG)):
                    act.wait_ge(gates_done, 2 * c + x + 1)
                    at = (K_AB, K_XB)[x] + c
                    act.activation(out[:, c, :], m.ps[2 * c + x][:, :], ACT.Sigmoid, bias=m.CP[:, at:at + 1]).then_inc(gates_home, 1)
            for c in range(4):
                act.wait_ge(decay_arg, c + 1)
                act.activation(u.RT[:, c, :], u.RG[:, c, :], ACT.Tanh).then_inc(decay_done, 1)
                act.wait_ge(decay_done, 2 * c + 1)
                act.activation(u.RG[:, c, :], u.RG[:, c, :], ACT.Exp, scale=-1.0).then_inc(decay_done, 1)
            for c in range(4):
                act.wait_ge(root_arg, c + 1)
                act.activation(u.RT[:, c, :], u.RT[:, c, :], ACT.Sqrt).then_inc(root_done, 1)
            for c in range(4):
                act.activation(b.LG[:, c, :], b.LG[:, c, :], ACT.Gelu_apprx_tanh).then_inc(gelu_done, 1)


def out_projection_2(nc, m, f):
    names = ("raw_in", "w_high", "w_low", "xt_high", "xt_low", "block_done", "tile_done", "summed")
    with stage(nc, "out_projection_2", *names) as (block, (raw_in, w_high, w_low, xt_high, xt_low, block_done, tile_done, summed)):

        @block.sync
        def _(sp):
            for q in range(4):
                sp.dma_start(f.ring[:, q, :], m.d["w_out_2"][q]).then_inc(raw_in, 16)
                sp.wait_ge(raw_in, 16 * (q + 1))

        @block.tensor
        def _(pe):
            for q in range(4):
                half, kh = divmod(q, 2)
                pe.wait_ge(w_low, q + 1)
                pe.wait_ge(xt_low, 4 * (kh + 1))
                for t in range(NT):
                    n = 0
                    for k in range(4):
                        for hw, hx in TERMS:
                            last = pe.matmul(m.ps[4 * half + t][:, :], f.XS[:, hx, 4 * kh + k, t * P:(t + 1) * P], f.WS[:, q % 2, hw, k * S:(k + 1) * S],
                                             start=(kh == 0 and n == 0), stop=(kh == 1 and n == 11))
                            n += 1
                    if kh:
                        last.then_inc(tile_done, 1)
                if kh == 0:
                    last.then_inc(block_done, 1)

        @block.scalar
        def _(act):
            for q in range(4):
                if q < 2:
                    for k in range(4):
                        act.copy(f.XS[:, 0, 4 * q + k, :], m.XT[:, 4 * q + k, :]).then_inc(xt_high, 1)
                act.wait_ge(raw_in, 16 * (q + 1))
                if q == 2:
                    act.wait_ge(block_done, 1)
                elif q == 3:
                    act.wait_ge(tile_done, NT)
                act.copy(f.WS[:, q % 2, 0, :], f.ring[:, q, :]).then_inc(w_high, 1)

        @block.gpsimd
        def _(pool):
            for q in range(4):
                pool.wait_ge(w_high, q + 1)
                pool.tensor_tensor(f.WS[:, q % 2, 1, :], f.ring[:, q, :], f.WS[:, q % 2, 0, :].bitcast(F32), ALU.subtract).then_inc(w_low, 1)

        @block.vector
        def _(dve):
            for k in range(KD):
                dve.wait_ge(xt_high, k + 1)
                dve.tensor_tensor(f.XS[:, 1, k, :], m.XT[:, k, :], f.XS[:, 0, k, :].bitcast(F32), ALU.subtract).then_inc(xt_low, 1)
            for v in range(2 * NT):
                half, t = divmod(v, NT)
                cols = slice(half * S, (half + 1) * S)
                dve.wait_ge(tile_done, v + 1)
                dve.tensor_tensor(m.X[:, t, cols], m.X[:, t, cols], m.ps[v][:, :], ALU.add).then_inc(summed, 1)
            dve.wait_ge(summed, 2 * NT)


def feed_forward(nc, m, f):
    names = ("raw0", "raw1", "raw2", "raw3", "w_high", "w_low", "block_done", "unit_done", "tile_done", "relu_done", "squared", "u_high", "u_low", "summed")
    QB = 8
    with stage(nc, "feed_forward", *names) as (block, sems):
        raw, (w_high, w_low, block_done, unit_done, tile_done, relu_done, squared, u_high, u_low, summed) = sems[:4], sems[4:]

        @block.sync
        def _(sp):
            with sp.Fori(0, 4) as part:
                for q in range(QB):
                    sp.wait_ge(w_low, part * QB + q + 1)
                    src = m.d["w_ff1"] if q < 4 else m.d["w_ff2"]
                    sp.dma_start(f.ring[:, q % 4, :], src[bass.ds(part * 4 + q % 4, 1)].rearrange("a p n -> p (a n)")).then_inc(raw[q % 4], 16)

        @block.scalar
        def _(act):
            act.sem_inc(block_done, 1)
            act.sem_inc(tile_done, 8)
            with act.Fori(0, 4) as part:
                for q in range(QB):
                    act.wait_ge(raw[q % 4], part * 32 + (q // 4 + 1) * 16)
                    if q in (0, 6):
                        act.wait_ge(block_done, part * 2 + q // 6 + 1)
                    elif q in (1, 7):
                        act.wait_ge(tile_done, part * 8 + 8 + q // 7 * 4)
                    else:
                        act.wait_ge(unit_done, part * 8 + 2 * (q - 1))
                    act.copy(f.WS[:, q % 2, 0, :], f.ring[:, q % 4, :]).then_inc(w_high, 1)

        @block.gpsimd
        def _(pool):
            pool.sem_inc(w_low, 4)
            with pool.Fori(0, 4) as part:
                for q in range(QB):
                    pool.wait_ge(w_high, part * QB + q + 1)
                    pool.tensor_tensor(f.WS[:, q % 2, 1, :], f.ring[:, q % 4, :], f.WS[:, q % 2, 0, :].bitcast(F32), ALU.subtract).then_inc(w_low, 1)

        @block.tensor
        def _(pe):
            with pe.Fori(0, 2) as two:
                for a in range(2):
                    parts = two * 2 + a
                    mine, other = 4 * a, 4 - 4 * a
                    for q in range(4):
                        pe.wait_ge(w_low, parts * QB + q + 5)
                        for c in range(2):
                            u = 2 * q + c
                            if u == 0:
                                pe.wait_ge(summed, parts * 8 + 4)
                            if u >= 4:
                                pe.wait_ge(relu_done, parts * 8 + u - 3)
                            n = 0
                            for k in range(KD):
                                for hw, hx in TERMS:
                                    last = pe.matmul(m.ps[mine + u % 4][:, :], f.WS[:, q % 2, hw, k * 256 + c * P:k * 256 + (c + 1) * P], f.XS[:, hx, k, :],
                                                     start=(n == 0), stop=(n == 3 * KD - 1))
                                    n += 1
                            last.then_inc(unit_done, 1)
                    for q in range(4, QB):
                        half, kh = divmod(q - 4, 2)
                        pe.wait_ge(w_low, parts * QB + q + 5)
                        pe.wait_ge(u_low, parts * 8 + 4 * (kh + 1))
                        if kh == 0:
                            if half == 0:
                                pe.wait_ge(summed, parts * 8 + 8)
                            else:
                                pe.wait_ge(relu_done, parts * 8 + 8)
                        for t in range(NT):
                            bank = m.ps[(mine if half else other) + t]
                            n = 0
                            for k in range(4):
                                for hw, hx in TERMS:
                                    last = pe.matmul(bank[:, :], f.US[:, hx, 4 * kh + k, t * P:(t + 1) * P], f.WS[:, q % 2, hw, k * S:(k + 1) * S],
                                                     start=(kh == 0 and n == 0), stop=(kh == 1 and n == 11))
                                    n += 1
                            if kh:
                                last.then_inc(tile_done, 1)
                        if kh == 0:
                            last.then_inc(block_done, 1)

        @block.vector
        def _(dve):
            dve.sem_inc(summed, 8)
            with dve.Fori(0, 2) as two:
                for a in range(2):
                    parts = two * 2 + a
                    mine, other = 4 * a, 4 - 4 * a
                    for u in range(8):
                        bank = m.ps[mine + u % 4][:, :]
                        dve.wait_ge(unit_done, parts * 8 + u + 1)
                        dve.tensor_scalar(f.SQ[:, u % 2, :], bank, 0.0, None, ALU.max).then_inc(relu_done, 1)
                        dve.wait_ge(relu_done, parts * 8 + u + 1)
                        dve.tensor_tensor(f.SQ[:, u % 2, :], f.SQ[:, u % 2, :], f.SQ[:, u % 2, :], ALU.mult).then_inc(squared, 1)
                        dve.wait_ge(squared, parts * 8 + u + 1)
                        dve.tensor_copy(f.US[:, 0, u, :], f.SQ[:, u % 2, :]).then_inc(u_high, 1)
                        dve.wait_ge(u_high, parts * 8 + u + 1)
                        dve.tensor_tensor(f.US[:, 1, u, :], f.SQ[:, u % 2, :], f.US[:, 0, u, :].bitcast(F32), ALU.subtract).then_inc(u_low, 1)
                    for v in range(8):
                        half, t = divmod(v, NT)
                        cols = slice(half * S, (half + 1) * S)
                        dve.wait_ge(tile_done, parts * 8 + v + 9)
                        dve.tensor_tensor(m.X[:, t, cols], m.X[:, t, cols], m.ps[(mine if half else other) + t][:, :], ALU.add).then_inc(summed, 1)
            dve.wait_ge(summed, 40)


def final_norm(nc, m, n, out):
    names = ("row_in", "act_step", "inv", "dve_step", "finished", "out_done")
    with stage(nc, "final_norm", *names) as (block, (row_in, act_step, inv, dve_step, finished, out_done)):

        @block.sync
        def _(sp):
            sp.dma_start(n.FN[:, :], m.d["final_norm"].to_broadcast([P, D])).then_inc(row_in, 16)
            for t in range(NT):
                sp.wait_ge(finished, t + 1)
                sp.dma_start(out.rearrange("(t p) d -> t p d", p=P)[t], m.X[:, t, :]).then_inc(out_done, 16)
            sp.wait_ge(out_done, 16 * NT)

        @block.scalar
        def _(act):
            link = Chain(act, act_step)
            for t in range(NT):
                link(act.activation(n.XN[:, t, :], m.X[:, t, :], ACT.Square, accum_out=n.SS[:, t:t + 1]))
            rstd(act, link, n.SS[:, :], n.SS[:, :], 1.0 / D, 1e-6).then_inc(inv, 1)

        @block.vector
        def _(dve):
            dve.wait_ge(row_in, 16)
            dve.wait_ge(inv, 1)
            for t in range(NT):
                dve.scalar_tensor_tensor(out=m.X[:, t, :], in0=m.X[:, t, :], scalar=n.SS[:, t:t + 1], in1=n.FN[:, :],
                                         op0=ALU.mult, op1=ALU.mult).then_inc(finished, 1)


class Bag:
    pass


def sb(nc, ctx, name, *shape):
    return ctx.enter_context(nc.sbuf_tensor(f"{name}_{nc.next_id()}", list(shape), F32))


def sbr(nc, ctx, name, *shape):
    return ctx.enter_context(nc.sbuf_tensor(f"{name}_{nc.next_id()}", list(shape), F32R))


def build(nc, d, out):
    with ExitStack() as ctx:
        m = Bag()
        m.X = sb(nc, ctx, "X", P, NT, D)
        m.XT = sb(nc, ctx, "XT", P, KD, S)
        m.ident = sb(nc, ctx, "ident", P, P)
        m.ones = sb(nc, ctx, "ones", P, P)
        m.zeros = sb(nc, ctx, "zeros", P, S)
        m.mask = sb(nc, ctx, "mask", P, 2, P)
        m.TRI = sb(nc, ctx, "TRI", P, P)
        m.IOTA = sb(nc, ctx, "IOTA", P, P)
        m.TAB = sb(nc, ctx, "TAB", P, S)
        m.dup = sb(nc, ctx, "dup", P, 64)
        m.CC = sb(nc, ctx, "CC", P, 8)
        m.CP = sb(nc, ctx, "CP", P, K_N)
        m.RP = sb(nc, ctx, "RP", P, 276)
        m.WR = sb(nc, ctx, "WR", P, KD, 20)
        m.d = d
        m.x_dram, m.dup_dram = d["x"], d["dup"]
        m.ps = [ctx.enter_context(nc.psum_tensor(f"bank{i}", [P, S], F32)) for i in range(8)]
        m.ring_in = [ctx.enter_context(nc.semaphore(f"ring_in{i}")) for i in range(RING)]
        with ExitStack() as c0:
            m.ang = sb(nc, c0, "ang", P, S)
            m.kk = sb(nc, c0, "kk", P, S)
            m.posi = c0.enter_context(nc.sbuf_tensor("posi", [P, S], I32))
            constants(nc, m, d["consts"], d["positions"])

        with ExitStack() as c1:
            m.ring = sb(nc, c1, "ring", P, RING, SLOT)
            with nc.Fori(0, DEPTH) as layer:
                one = bass.ds(layer, 1)

                def first_loads(sp):
                    for i in range(RING):
                        sp.dma_start(m.ring[:, i, 0:4096], d["w_in_t"][one, i].rearrange("a p n -> p (a n)")).then_inc(m.ring_in[i], 16)

                def layer_params(sp, sem):
                    sp.dma_start(m.CP[:, 0:C_N], d["cols"][one].rearrange("a p n -> p (a n)")).then_inc(sem, 16)
                    sp.dma_start(m.RP[:, :], d["rows"][one, 0:276].to_broadcast([P, 276])).then_inc(sem, 16)
                    sp.dma_start(m.WR[:, :, :].rearrange("p k n -> p (k n)"), d["w_router"][one].rearrange("a p n -> p (a n)")).then_inc(sem, 16)
                    return 3

                transpose_stage(nc, m, first_loads, layer_params)
                with ExitStack() as c2:
                    mx = Bag()
                    mx.V1 = sb(nc, c2, "V1", P, NT, 4, 65)
                    mx.O = sb(nc, c2, "O", P, NT, 256)
                    mx.MQ = sb(nc, c2, "MQ", P, 2, S)
                    mx.MK = sb(nc, c2, "MK", P, 2, S)
                    mx.Z = sb(nc, c2, "Z", P, 2, S)
                    mx.XB = sb(nc, c2, "XB", P, 6, S + 4)
                    mx.SC = sb(nc, c2, "SC", P, S)
                    mx.IG = sb(nc, c2, "IG", P, S)
                    with ExitStack() as c3:
                        mx.CQ = sb(nc, c3, "CQ", P, 3, S)
                        mx.KRT = sb(nc, c3, "KRT", P, S)
                        in_projection(nc, m, layer, mx)
                        a = Bag()
                        a.QT = sb(nc, c3, "QT", P, 4, S)
                        a.KT = sb(nc, c3, "KT", P, 4, S)
                        a.V = sb(nc, c3, "V", P, NT, S)
                        a.PR = sb(nc, c3, "PR", P, 4, S)
                        a.PT = sb(nc, c3, "PT", P, 2, NT, P)
                        a.SQ = sb(nc, c3, "SQ", P, 3, S)
                        a.RS = sb(nc, c3, "RS", P, 2, S)
                        a.MX = sb(nc, c3, "MX", P, 4)
                        a.NM = sb(nc, c3, "NM", P, 4)
                        a.SM = sb(nc, c3, "SM", P, 4)
                        a.RC = sb(nc, c3, "RC", P, 4)
                        mla(nc, m, mx, a)
                    with ExitStack() as c3:
                        g = Bag()
                        g.T1 = sb(nc, c3, "T1", P, S)
                        g.SP = sb(nc, c3, "SP", P, S)
                        g.CS = sb(nc, c3, "CS", P, S)
                        g.FS = sb(nc, c3, "FS", P, S)
                        g.NM = sb(nc, c3, "NM", P, S)
                        g.CO = sb(nc, c3, "CO", P, 2)
                        g.GN = sb(nc, c3, "GN", P, 3, NT, GR)
                        g.EM = sb(nc, c3, "EM", P, NT, GR)
                        g.XC = sb(nc, c3, "XC", P, 6, S)
                        g.XN = sb(nc, c3, "XN", P, NT, 256)
                        g.E = sb(nc, c3, "E", P, 4, S)
                        g.W = sb(nc, c3, "W", P, 4, S)
                        g.RM = sb(nc, c3, "RM", P, 2, S)
                        g.H = sb(nc, c3, "H", P, NT, 4, 64)
                        g.HB = sb(nc, c3, "HB", P, NT, 64)
                        g.DN = sb(nc, c3, "DN", P, 2, NT)
                        g.DT = sb(nc, c3, "DT", P, 2, NT)
                        g.MEAN = sb(nc, c3, "MEAN", P, 2, 16)
                        gates_and_conv(nc, m, mx, g)
                        scans(nc, m, mx, g)
                        mixer_norms(nc, m, mx, g)
                with ExitStack() as c2:
                    ln = Bag()
                    ln.Y = sb(nc, c2, "Y", P, NT, D)
                    ln.GB = m.ring[:, 2, 0:2 * D]
                    ln.ST = sb(nc, c2, "ST", P, NT, 2, 6)
                    ln.MV = sb(nc, c2, "MV", P, NT, 2)
                    ln.IV = sb(nc, c2, "IV", P, NT)
                    norm_stage(nc, m, ln, 0, layer, product=True)
                    transpose_stage(nc, m)
                    with ExitStack() as c3:
                        r = Bag()
                        r.LG = sb(nc, c3, "LG", P, NT, 20)
                        r.hg = sb(nc, c3, "hg", P, NT, 4)
                        r.h1 = sb(nc, c3, "h1", P, NT, 4)
                        r.h2 = sb(nc, c3, "h2", P, NT, 4)
                        r.e4 = sb(nc, c3, "e4", P, NT, 4)
                        r.el = sb(nc, c3, "el", P, NT, 4)
                        r.gm = sb(nc, c3, "gm", P, NT)
                        r.m1 = sb(nc, c3, "m1", P, NT)
                        r.m2 = sb(nc, c3, "m2", P, NT)
                        r.t1 = sb(nc, c3, "t1", P, NT)
                        r.COMB = sb(nc, c3, "COMB", P, NT, NE)
                        r.OH = sb(nc, c3, "OH", P, NT, NE)
                        r.POS = sb(nc, c3, "POS", P, NT, NE + NE // NGR)
                        r.NP = sb(nc, c3, "NP", P, 3)
                        r.NPI = c3.enter_context(nc.sbuf_tensor("passes", [P, 1], I32))
                        r.CW = sbr(nc, c3, "CW", P, NT, NE, 2)
                        r.XH = sbr(nc, c3, "XH", P, NT, D)
                        r.XL = sbr(nc, c3, "XL", P, NT, D)
                        r.SEL = sbr(nc, c3, "SEL", P, NT, 4 * P)
                        r.SELT = sbr(nc, c3, "SELT", P, 4, S)
                        r.YE = sbr(nc, c3, "YE", P, 2, 2, D)
                        r.WS = sb(nc, c3, "WS", P, 4)
                        r.H = sb(nc, c3, "H", P, 2, FE)
                        r.HT = sb(nc, c3, "HT", P, 2, 2 * P)
                        r.SG = sb(nc, c3, "SG", P, 2, FE)
                        r.TRI, r.IOTA = m.TRI, m.IOTA
                        r.Y = ln.Y
                        router(nc, m, r)
                        dispatch(nc, m, r)
                        passes = nc.values_load(r.NPI[0:1, 0:1], min_val=1, max_val=4,
                                                skip_runtime_bounds_check_because="it is one plus three comparisons' results")
                        with nc.Fori(0, passes):
                            experts(nc, m, r, layer)
                            next_pass(nc, r)
                    norm_stage(nc, m, ln, 1, layer)
                nums = [s.num for s in m.ring_in]
                nc.all_engine_barrier(sems_to_clear=range(min(nums), max(nums) + 1))

        with ExitStack() as c1:
            b = Bag()
            b.Z = sb(nc, c1, "Z", P, 4, S)
            b.LG = sb(nc, c1, "LG", P, 4, S)
            b.LX = sb(nc, c1, "LX", P, 4, S + 3)
            b.GR = sb(nc, c1, "GR", P, S)
            b.G1 = sb(nc, c1, "G1", P, S)
            b.GC = sb(nc, c1, "GC", P, S)
            b.GM = sb(nc, c1, "GM", P, S)
            b.BT = sb(nc, c1, "BT", P, S)
            b.EG = sb(nc, c1, "EG", P, S)
            b.DK = sb(nc, c1, "DK", P, S)
            b.BE = sb(nc, c1, "BE", P, S)
            b.CO = sb(nc, c1, "CO", P, 1)
            b.GN = sb(nc, c1, "GN", P, 64)
            with ExitStack() as c2:
                q = Bag()
                q.QB = b.QB = sb(nc, c1, "QB", P, 12, S + 3)

                def params(sp, sem):
                    sp.dma_start(m.CP[:, 0:K_N], d["cols_2"]).then_inc(sem, 16)
                    return 1

                b.XS = sbr(nc, c2, "XS", P, 2, KD, S)
                with ExitStack() as c3:
                    n = Bag()
                    n.XN = sb(nc, c3, "XN", P, NT, D)
                    n.SS = sb(nc, c3, "SS", P, NT)
                    rms_transpose(nc, m, n, b.XS, K_NM, params)
                with ExitStack() as c3:
                    q.ring = sb(nc, c3, "ring", P, 4, KD * 256)
                    q.WS = sbr(nc, c3, "WS", P, 2, 2, KD * 256)
                    in_projection_2(nc, m, b, q)
            b.XC = sb(nc, c1, "XC", P, 12, S)
            with ExitStack() as c2:
                q.SQ = sb(nc, c2, "SQ", P, 2, S)
                q.RS = sb(nc, c2, "RS", P, 8, S)
                gdn_prepare(nc, m, b, q)
            with ExitStack() as c2:
                hd = (P, GH, S)
                ch = (P, NT, GH, P)
                w = Bag()
                w.LM = sb(nc, c2, "LM", P, 7, P)
                old = b.QB[:, :, :].rearrange("p c n -> p (c n)")
                third = lambda n: old[:, n * GH * S:(n + 1) * GH * S].rearrange("p (h n) -> p h n", h=GH)
                w.KB, w.QE, w.RM = third(0), third(1), third(2)
                w.GL = sb(nc, c2, "GL", P, GH, NT)
                w.AT = sb(nc, c2, "AT", *ch)
                w.AQ = sb(nc, c2, "AQ", *ch)
                w.T = sb(nc, c2, "T", *ch)
                w.U = sb(nc, c2, "U", *ch)
                w.KE = sb(nc, c2, "KE", *ch)
                w.KD = sb(nc, c2, "KD", *ch)
                w.VB = sb(nc, c2, "VB", *ch)
                w.VN = sb(nc, c2, "VN", P, GH, P)
                w.S = sb(nc, c2, "S", P, GH, P)
                with ExitStack() as c3:
                    w.E = sb(nc, c3, "E", *ch)
                    gdn_matrices(nc, m, b, w)
                with ExitStack() as c3:
                    w.Z = sb(nc, c3, "Z", *ch)
                    gdn_inverse(nc, m, w)
                w.NW = sb(nc, c2, "NW", *ch)
                w.OT = w.RM
                gdn_sequence(nc, m, b, w)
                gdn_norm(nc, m, b, w)
            with ExitStack() as c2:
                u = Bag()
                u.XR = sb(nc, c2, "XR", *hd)
                u.RG = sb(nc, c2, "RG", *hd)
                u.IG = sb(nc, c2, "IG", *hd)
                u.RT = sb(nc, c2, "RT", *hd)
                u.TH = sb(nc, c2, "TH", P, 2, S)
                u.WA = sb(nc, c2, "WA", P, 8, 64)
                u.AB = sb(nc, c2, "AB", P, 8)
                u.SPA = sb(nc, c2, "SPA", P, 4)
                lru(nc, m, b, u)
        with ExitStack() as c1:
            f = Bag()
            f.ring = sb(nc, c1, "ring", P, 4, KD * 256)
            f.WS = sbr(nc, c1, "WS", P, 2, 2, KD * 256)
            f.XS = sbr(nc, c1, "XS", P, 2, KD, S)
            out_projection_2(nc, m, f)
            with ExitStack() as c2:
                n = Bag()
                n.XN = sb(nc, c2, "XN", P, NT, D)
                n.SS = sb(nc, c2, "SS", P, NT)
                n.FN = sb(nc, c2, "FN", P, D)
                rms_transpose(nc, m, n, f.XS, K_NP)
            with ExitStack() as c2:
                f.US = sbr(nc, c2, "US", P, 2, 8, S)
                f.SQ = sb(nc, c2, "SQ", P, 2, S)
                feed_forward(nc, m, f)
            with ExitStack() as c2:
                n = Bag()
                n.XN = sb(nc, c2, "XN", P, NT, D)
                n.SS = sb(nc, c2, "SS", P, NT)
                n.FN = sb(nc, c2, "FN", P, D)
                final_norm(nc, m, n, out)


def rows_to_tiles(w, cols):
    w = w[:, cols] if cols is not None else w
    return np.ascontiguousarray(w.reshape(-1, P, w.shape[1]).transpose(1, 0, 2).reshape(P, -1))


def layer_arrays(i):
    w_in, L = i["w_in"], DEPTH
    z = np.zeros((L, D, 1), np.float32)

    def take(cols):
        idx = np.array([2488 if c is None else c for c in cols])
        return np.concatenate([w_in, z], -1)[:, :, idx]

    none = [None]
    kr = list(range(384, 416))
    krs = kr[16:] + kr[:16]
    g = lambda j: list(range(1440 + 4 * j, 1444 + 4 * j))
    dt = lambda j: list(range(2480 + 4 * j, 2484 + 4 * j))
    sc = g(1) + dt(0) + none * 24 + g(3) + dt(1)
    ig = g(0) + none * 28 + g(2) + none * 4
    xbc = list(range(1712, 2480))
    block0 = list(range(0, 384)) + sc + none * 24 + kr + krs
    block1 = xbc[:512]
    block2 = xbc[512:] + list(range(1456, 1712))
    block3 = list(range(416, 928))
    vo = list(range(928, 1440))
    tiles = lambda a: np.stack([rows_to_tiles(x, None) for x in a])
    w_t = np.stack([tiles(take(b)) for b in (block0, block1, block2, block3)], 1)
    w_n = np.concatenate([tiles(take(vo)), tiles(take(ig))], -1)

    uq = i["mla_w_uq"].reshape(L, 256, HEADS, NOPE + ROPE)
    swapped = np.concatenate([uq[..., 80:96], uq[..., 64:80]], -1)
    uq = np.concatenate([uq, swapped], -1).reshape(L, 256, HEADS * P)
    ukv = i["mla_w_ukv"].reshape(L, P, HEADS, NOPE + VD)
    w_mla = np.concatenate([tiles(uq), ukv[..., :NOPE].reshape(L, P, 512), ukv[..., NOPE:].reshape(L, P, 512)], -1)

    halves = lambda a: np.stack([rows_to_tiles(a, slice(0, S)), rows_to_tiles(a, slice(S, D))])
    w_out = np.stack([halves(a) for a in i["w_out"]])
    gu = np.concatenate([i["expert_w_gate"], i["expert_w_up"]], -1)
    w_exp = np.concatenate([gu.reshape(L, NE, KD, P, 2 * FE).transpose(0, 1, 3, 2, 4).reshape(L, NE, P, -1),
                            i["expert_w_down"].reshape(L, NE, 2, P, D).transpose(0, 1, 3, 2, 4).reshape(L, NE, P, -1)], -1)
    we = i["router_expert_w"].transpose(0, 2, 1, 3).reshape(L, D, NE)
    w_router = tiles(np.concatenate([i["router_group_w"], we], -1))

    cols = np.zeros((L, P, C_N), np.float32)
    cols[:, :, C_QN:C_QN + 2] = i["mla_q_norm"].reshape(L, 2, P).transpose(0, 2, 1)
    cols[:, :, C_KVN] = i["mla_kv_norm"]
    cols[:, :, C_CW:C_CW + 30] = i["ssd_conv_w"].reshape(L, 5, 6, P).transpose(0, 3, 2, 1).reshape(L, P, 30)
    cols[:, :, C_CB:C_CB + 6] = i["ssd_conv_b"].reshape(L, 6, P).transpose(0, 2, 1)
    cols[:, :, C_DS:C_DS + 2] = np.repeat(i["ssd_d"].reshape(L, 2, 2), 64, axis=2).transpose(0, 2, 1)
    cols[:, :, C_SN:C_SN + 2] = i["ssd_norm"].reshape(L, 2, P).transpose(0, 2, 1)
    for d in range(2):
        lf, dtr = slice(32 * d, 32 * d + 4), slice(32 * d + 4, 32 * d + 8)
        cols[:, lf, C_SGN], cols[:, dtr, C_SGN] = -1.0, 1.0
        cols[:, dtr, C_SB] = i["ssd_dt_bias"][:, d]
        cols[:, lf, C_SB] = i["mlstm_gate_bias"][:, 2 * d + 1]
        cols[:, dtr, C_AL] = i["ssd_a_log"][:, d]
        cols[:, lf, C_IB] = i["mlstm_gate_bias"][:, 2 * d]
    rows = np.concatenate([i["mlstm_norm"], i["router_group_b"], i["router_expert_b"].reshape(L, NE),
                           i["ln1_g"], i["ln1_b"], i["ln2_g"], i["ln2_b"]], -1)
    return {"w_in_t": w_t, "w_in_n": w_n, "w_mla": w_mla, "w_out": w_out, "w_exp": w_exp, "w_router": w_router, "cols": cols, "rows": rows}


def second_arrays(i):
    w = i["w_in_2"][0]
    perm = list(range(0, 1536)) + list(range(1536, 2048)) + list(range(2056, 3080))
    w_in_2 = np.stack([rows_to_tiles(w, np.array(perm[256 * n:256 * (n + 1)])) for n in range(12)])
    gate = np.zeros((D, GR), np.float32)
    gate[:, 0:4], gate[:, 32:36] = w[:, 2052:2056], w[:, 2048:2052]
    gate = rows_to_tiles(gate, None)
    cols = np.zeros((P, K_N), np.float32)
    per = lambda v, n: v.reshape(n, P).T
    cols[:, K_NM:K_NM + 8] = per(i["norm_mix_w_2"][0], 8)
    cols[:, K_NP:K_NP + 8] = per(i["norm_mlp_w_2"][0], 8)
    cols[:, K_GC:K_GC + 48] = i["gdn_conv_w_2"][0].reshape(4, 12, P).transpose(2, 1, 0).reshape(P, 48)
    cols[:, K_LC:K_LC + 16] = i["lru_conv_w_2"][0].reshape(4, 4, P).transpose(2, 1, 0).reshape(P, 16)
    cols[:, K_LB:K_LB + 4] = per(i["lru_conv_b_2"][0], 4)
    cols[:, K_AB:K_AB + 4] = per(i["lru_gate_a_b_2"][0], 4)
    cols[:, K_XB:K_XB + 4] = per(i["lru_gate_x_b_2"][0], 4)
    cols[:, K_AP:K_AP + 4] = per(i["lru_a_param_2"][0], 4)
    cols[:, K_GN] = i["gdn_norm_w_2"][0]
    cols[0:4, K_AL] = i["gdn_A_log_2"][0]
    cols[0:4, K_DB] = i["gdn_dt_bias_2"][0]
    gates = np.stack([i["lru_gate_a_w_2"][0], i["lru_gate_x_w_2"][0]], 1).reshape(4, 2, 2, 64, 64)
    lru_w = np.ascontiguousarray(gates.transpose(1, 3, 0, 2, 4).reshape(P, 8, 64))
    quarters = lambda a: [rows_to_tiles(a[S * kh:S * (kh + 1)], slice(S * half, S * (half + 1))) for half in range(2) for kh in range(2)]
    w_ff1 = np.stack([rows_to_tiles(i["w_ff1_2"][0], slice(256 * n, 256 * (n + 1))) for n in range(16)])
    w_ff2 = np.stack([q for part in range(4) for q in quarters(i["w_ff2_2"][0][D * part:D * (part + 1)])])
    return {"w_in_2": w_in_2, "w_gates_2": gate, "cols_2": cols, "lru_w": lru_w, "w_out_2": np.stack(quarters(i["w_out_2"][0])),
            "w_ff1": w_ff1, "w_ff2": w_ff2, "final_norm": i["final_norm_w_2"].reshape(1, D)}


def shape_constants():
    consts = np.zeros((P, 8), np.float32)
    freq = np.float32(10000.0) ** (-np.arange(0, ROPE, 2, dtype=np.float32) / np.float32(ROPE))
    consts[64:128, 0] = np.tile(freq, 4)
    consts[64:96, 1] = 0.25
    consts[64:96, 2] = math.pi / 2
    consts[64:96, 3], consts[96:112, 3], consts[112:128, 3] = 1.0, -1.0, 1.0
    consts[:, 4:8] = [4.0, 3.0, 2.0, 1.0]
    dup = np.zeros((P, 64), np.float32)
    for r in range(64):
        dup[64 + r, r % 32], dup[64 + r, 32 + r % 32] = 1.0, 1.0
    i, j = np.arange(P)[:, None], np.arange(P)[None, :]
    masks = [-((i // (2 * n) == j // (2 * n)) & (i // n > j // n)).astype(np.float32) for n in (1, 2, 4, 8, 16, 32, 64)]
    return {"consts": consts, "dup": dup, "level_masks": np.ascontiguousarray(np.stack(masks, 1))}


def kernel(**inputs):
    import concourse.bacc as bacc
    from concourse.bass_utils import run_bass_kernel_spmd as run

    i = {k: np.asarray(v) for k, v in inputs.items()}
    arrays = {"x": i["x"].reshape(S, D), "positions": i["positions"].reshape(1, S)}
    arrays.update(shape_constants())
    arrays.update(layer_arrays(i))
    arrays.update(second_arrays(i))
    arrays = {k: np.ascontiguousarray(v) for k, v in arrays.items()}
    nc = bacc.Bacc("TRN2", target_bir_lowering=False, num_devices=1)
    d = {k: nc.dram_tensor(f"in_{k}", v.shape, mybir.dt.from_np(v.dtype), kind="ExternalInput").ap() for k, v in arrays.items()}
    out = nc.dram_tensor("out", (S, D), F32, kind="ExternalOutput").ap()
    build(nc, d, out)
    r = run(nc, [{f"in_{k}": v for k, v in arrays.items()}], core_ids=[0])
    return r.results[0]["out"].reshape(1, S, D)
```

```python
import math
from contextlib import ExitStack, contextmanager

import numpy as np

import concourse.bass as bass
from concourse import mybir

F32 = mybir.dt.float32
F32R = mybir.dt.float32r
I32 = mybir.dt.int32
ALU = mybir.AluOpType
ACT = mybir.ActivationFunctionType
AX = mybir.AxisListType

P = 128
S = 512
NT = S // P
D = 1024
KD = D // P
DEPTH = 2
ALPHA = (2 * DEPTH) ** 0.25
NEG = -1e30

HEADS, NOPE, ROPE, VD = 8, 64, 32, 64
SCALE = (NOPE + ROPE) ** -0.5
NE, FE = 16, 256
NGR = 4

C_QN, C_KVN, C_CW, C_CB, C_DS, C_SN, C_SGN, C_SB, C_AL, C_IB, C_N = 0, 2, 3, 33, 39, 41, 43, 44, 45, 46, 47
R_MN, R_RB, R_L1, R_L2, R_N = 0, 256, 276, 276 + 2 * D, 276 + 4 * D
GR = 40
TERMS = ((0, 0), (0, 1), (1, 0))


class Chain:

    def __init__(self, eng, sem):
        self.eng, self.sem, self.n = eng, sem, 0

    def __call__(self, ins):
        ins.then_inc(self.sem, 1)
        self.n += 1
        self.eng.wait_ge(self.sem, self.n)


@contextmanager
def stage(nc, name, *names):
    with ExitStack() as ctx:
        sems = [ctx.enter_context(nc.semaphore(n)) for n in names]
        with nc.Block(f"{name}_{nc.next_id()}", no_gpsimd_drain=True) as block:
            yield block, sems
        nums = [s.num for s in sems]
        nc.all_engine_barrier(sems_to_clear=range(min(nums), max(nums) + 1))


def rms_parts(act, link, outs, variances, scales, eps, done):
    for out, var, scale in zip(outs, variances, scales):
        link(act.activation(out, var, ACT.Ln, scale=scale, bias=eps))
    for out in outs:
        act.activation(out, out, ACT.Exp, scale=-0.5).then_inc(done, 1)


def blocks(x):
    return x.rearrange("p (b n) -> p b n", b=NT)


def every_block(x):
    return x.rearrange("p (a n) -> p a n", a=1).to_broadcast([P, NT, P])


def constants(nc, m, consts_dram, pos_dram):
    with stage(nc, "constants", "pool_step", "const_in", "pos_in", "dve_step", "angle", "sine") as (block, sems):
        pool_step, const_in, pos_in, dve_step, angle, sine = sems

        @block.sync
        def _(sp):
            sp.dma_start(m.X[:, :, :], m.x_dram.rearrange("(t p) d -> p t d", p=P)).then_inc(const_in, 16)
            sp.dma_start(m.CC[:, :], consts_dram).then_inc(const_in, 16)
            sp.dma_start(m.dup[:, :], m.dup_dram).then_inc(const_in, 16)
            sp.wait_ge(const_in, 48)

        @block.gpsimd
        def _(pool):
            link = Chain(pool, pool_step)
            link(pool.memset(m.ident[:, :], 0.0))
            link(pool.affine_select(out=m.ident[:, :], in_=m.ident[:, :], compare_op=ALU.not_equal, fill=1.0,
                                    base=0, pattern=[[-1, P]], channel_multiplier=1))
            link(pool.memset(m.ones[:, :], 1.0))
            link(pool.memset(m.zeros[:, :], 0.0))
            for d, sign in ((0, 1), (1, -1)):
                link(pool.affine_select(out=m.mask[:, d, :], in_=m.zeros[:, 0:P], compare_op=ALU.is_ge, fill=NEG, base=0,
                                        pattern=[[sign, P]], channel_multiplier=-sign))
            link(pool.affine_select(out=m.TRI[:, :], in_=m.ones[:, :], compare_op=ALU.is_gt, fill=0.0, base=0, pattern=[[1, P]], channel_multiplier=-1))
            link(pool.iota(m.IOTA[:, :], pattern=[[1, P]], base=0, channel_multiplier=0, allow_small_or_imprecise_dtypes=True))

        @block.vector
        def _(dve):
            link = Chain(dve, dve_step)
            dve.wait_ge(pos_in, 16)
            dve.wait_ge(const_in, 48)
            r = slice(64, 128)
            ang, k = m.ang[r, :], m.kk[r, :]
            link(dve.memset(m.TAB[0:64, :], 1.0))
            link(dve.tensor_copy(ang, m.posi[r, :]))
            link(dve.tensor_scalar(ang, ang, m.CC[r, 0:1], None, ALU.mult))
            link(dve.tensor_scalar(k, ang, 1.0 / (2 * math.pi), m.CC[r, 1:2], ALU.mult, ALU.add))
            link(dve.tensor_scalar(k, k, 12582912.0, None, ALU.add))
            link(dve.tensor_scalar(k, k, -12582912.0, None, ALU.add))
            for c in (6.28125, 0.0019350051879882812, 3.0199159819567e-07):
                link(dve.scalar_tensor_tensor(out=ang, in0=k, scalar=-c, in1=ang, op0=ALU.mult, op1=ALU.add))
            link(dve.tensor_scalar(ang, ang, m.CC[r, 2:3], None, ALU.add))
            link(dve.tensor_scalar(ang, ang, 3.1415925, -3.1415925, ALU.min, ALU.max))
            dve.sem_inc(angle, 1)
            dve.wait_ge(sine, 1)
            link(dve.tensor_scalar(m.TAB[r, :], k, m.CC[r, 3:4], None, ALU.mult))

        @block.scalar
        def _(act):
            act.dma_start(m.posi[:, :], pos_dram.to_broadcast([P, S])).then_inc(pos_in, 16)
            act.wait_ge(angle, 1)
            act.activation(m.kk[64:128, :], m.ang[64:128, :], ACT.Sin).then_inc(sine, 1)


def transpose_stage(nc, m, XS=None, loads=None, params=None):
    with stage(nc, "transpose_stage", "transposed", "xt_act", "xt_dve", "param_in") as (block, (transposed, xt_act, xt_dve, param_in)):

        @block.sync
        def _(sp):
            if params:
                n = params(sp, param_in)
            if loads:
                loads(sp)
            if params:
                sp.wait_ge(param_in, 16 * n)

        @block.tensor
        def _(pe):
            for k in range(KD):
                for t in range(NT):
                    last = pe.transpose(m.ps[k][:, t * P:(t + 1) * P], m.X[:, t, k * P:(k + 1) * P], m.ident[:, :])
                last.then_inc(transposed, 1)

        @block.scalar
        def _(act):
            chunks = range(KD) if XS else range(0, KD, 2)
            for k in chunks:
                act.wait_ge(transposed, k + 1)
                act.copy(XS[:, 0, k, :] if XS else m.XT[:, k, :], m.ps[k][:, :]).then_inc(xt_act, 1)
            act.wait_ge(xt_act, len(chunks))

        @block.vector
        def _(dve):
            if XS:
                for k in range(KD):
                    dve.wait_ge(xt_act, k + 1)
                    dve.tensor_tensor(XS[:, 1, k, :], m.ps[k][:, :], XS[:, 0, k, :].bitcast(F32), ALU.subtract).then_inc(xt_dve, 1)
                dve.wait_ge(xt_dve, KD)
            else:
                for k in range(1, KD, 2):
                    dve.wait_ge(transposed, k + 1)
                    dve.tensor_copy(m.XT[:, k, :], m.ps[k][:, :]).then_inc(xt_dve, 1)
                dve.wait_ge(xt_dve, KD // 2)


def in_projection(nc, m, layer, mx, XS, WS):
    with stage(nc, "in_projection", "unit_done", "home", "w_high", "w_low", "conv_step", "margins", "silu_done") as (block, sems):
        unit_done, home, w_high, w_low, conv_step, margins, silu_done = sems
        homes = [[("copy", slice(0, P), mx.CQ[:, c, :])] for c in range(3)]
        homes.append([("copy", slice(0, GR), mx.SC[0:GR, :]), ("rope", slice(64, 128), mx.KRT[64:128, :])])
        homes += [[("copy", slice(0, P), mx.XB[:, c, 2:2 + S])] for c in range(6)]
        homes += [[("copy", slice(0, P), mx.Z[:, c, :])] for c in range(2)]
        homes += [[("copy", slice(0, P), mx.MQ[:, c, :])] for c in range(2)]
        homes += [[("scale", slice(0, P), mx.MK[:, c, :])] for c in range(2)]
        homes.append([("copy", slice(0, GR), mx.IG[0:GR, :])])
        homes += [[("v", None, mx.V1[:, t, :, 0:64]), ("o", None, mx.O[:, t, :])] for t in range(NT)]
        NB = 11
        sizes = [KD * GR if i == 8 else KD * 256 for i in range(NB)]

        @block.sync
        def _(sp):
            for i in range(4, NB):
                sp.wait_ge(w_low, i - 3)
                src = m.d["w_gates"][bass.ds(layer, 1)] if i == 8 else m.d["w_in"][bass.ds(layer, 1), i - i // 9]
                sp.dma_start(m.raw[:, i % 4, 0:sizes[i]], src.rearrange("a p n -> p (a n)")).then_inc(m.raw_in[i % 4], 16)
            sp.wait_ge(w_low, 10)
            sp.dma_start(m.w_mla, m.d["w_mla"][bass.ds(layer, 1)].rearrange("a p n -> p (a n)")).then_inc(m.mla_in, 16)

        @block.tensor
        def _(pe):
            for i in range(9):
                pe.wait_ge(w_low, i + 1)
                n, width = (GR, GR) if i == 8 else (P, 256)
                for g in (2 * i, 2 * i + 1)[:1 if i == 8 else 2]:
                    if g >= 8:
                        pe.wait_ge(home, g - 7)
                    step = 0
                    for k in range(KD):
                        at = k * width + g % 2 * P
                        for hw, hx in TERMS:
                            last = pe.matmul(m.ps[g % 8][0:n, :], WS[:, i % 2, hw, at:at + n], XS[:, hx, k, :], start=(step == 0), stop=(step == 3 * KD - 1))
                            step += 1
                    last.then_inc(unit_done, 1)
            for kh in range(2):
                i = 9 + kh
                pe.wait_ge(w_low, i + 1)
                for t in range(NT):
                    g = 17 + t
                    if kh == 0:
                        pe.wait_ge(home, g - 7)
                    step = 0
                    for k in range(4):
                        for hw, hx in TERMS:
                            last = pe.matmul(m.ps[g % 8][:, :], XS[:, hx, 4 * kh + k, t * P:(t + 1) * P], WS[:, i % 2, hw, k * S:(k + 1) * S],
                                             start=(kh == 0 and step == 0), stop=(kh == 1 and step == 11))
                            step += 1
                    if kh:
                        last.then_inc(unit_done, 1)

        @block.scalar
        def _(act):
            for i in range(NB):
                act.wait_ge(m.raw_in[i % 4], 16 * (i // 4 + 1))
                if i >= 2:
                    act.wait_ge(unit_done, min(2 * (i - 1), 17))
                act.copy(WS[:, i % 2, 0, 0:sizes[i]], m.raw[:, i % 4, 0:sizes[i]]).then_inc(w_high, 1)
            act.wait_ge(home, 12)
            for c in range(6):
                XC = mx.XB[:, c, 2:2 + S]
                act.activation(XC, XC, ACT.Silu, bias=m.CP[:, C_CB + c:C_CB + c + 1]).then_inc(silu_done, 1)
            for c in range(2):
                act.activation(mx.Z[:, c, :], mx.Z[:, c, :], ACT.Silu).then_inc(silu_done, 1)
            act.wait_ge(silu_done, 8)

        @block.vector
        def _(dve):
            link = Chain(dve, conv_step)
            for g, parts in enumerate(homes):
                bank = m.ps[g % 8]
                dve.wait_ge(unit_done, g + 1)
                for kind, rows, dst in parts:
                    if kind == "rope":
                        last = dve.tensor_tensor(dst, bank[rows, :], m.TAB[rows, :], ALU.mult)
                    elif kind == "scale":
                        last = dve.tensor_scalar(dst, bank[rows, :], 0.125, None, ALU.mult)
                    elif kind == "v":
                        last = dve.tensor_copy(dst, bank[:, 0:256].rearrange("p (h d) -> p h d", h=4))
                    else:
                        last = dve.tensor_copy(dst, bank[:, 256:512] if kind == "o" else bank[rows, :])
                last.then_inc(home, 1)
                if 4 <= g < 10:
                    c = g - 4
                    if c == 0:
                        dve.wait_ge(margins, 2)
                    dve.wait_ge(home, g + 1)
                    for tap in (0, 1, 3, 4, 2):
                        w = m.CP[:, C_CW + 5 * c + tap:C_CW + 5 * c + tap + 1]
                        src = mx.XB[:, c, tap:tap + S]
                        if tap == 0:
                            link(dve.tensor_scalar(mx.TP[:, :], src, w, None, ALU.mult))
                        else:
                            link(dve.scalar_tensor_tensor(out=src if tap == 2 else mx.TP[:, :], in0=src, scalar=w, in1=mx.TP[:, :], op0=ALU.mult, op1=ALU.add))
            dve.wait_ge(home, len(homes))

        @block.gpsimd
        def _(pool):
            pool.memset(mx.XB[:, :, 0:2], 0.0).then_inc(margins, 1)
            pool.memset(mx.XB[:, :, 2 + S:4 + S], 0.0).then_inc(margins, 1)
            pool.memset(mx.V1[:, :, :, 64:65], 1.0)
            for i in range(NB):
                n = sizes[i]
                pool.wait_ge(w_high, i + 1)
                pool.tensor_tensor(WS[:, i % 2, 1, 0:n], m.raw[:, i % 4, 0:n], WS[:, i % 2, 0, 0:n].bitcast(F32), ALU.subtract).then_inc(w_low, 1)


def mla(nc, m, layer, mx, a):
    HH = HEADS // 2
    NU = HH * NT
    names = ("act_step", "dve_step", "squares", "sums", "inv_rms", "normed", "q_done", "q_home", "k_done", "k_home", "v_done",
             "v_home", "kr_done", "scores", "neg_max", "probs", "probs_normed", "probs_t", "probs_t_home", "pv", "head_home")
    with stage(nc, "mla", *names) as (block, sems):
        (act_step, dve_step, squares, sums, inv_rms, normed, q_done, q_home, k_done, k_home, v_done,
         v_home, kr_done, scores, neg_max, probs, probs_normed, probs_t, probs_t_home, pv, head_home) = sems
        w = m.w_mla
        wq = w[:, 0:2048].rearrange("p (k n) -> p k n", k=2)
        wk = w[:, 2048:2560]
        wv = w[:, 2560:3072]

        @block.sync
        def _(sp):
            for q in range(2):
                sp.dma_start(m.raw[:, 2 + q, :], m.d["w_out"][bass.ds(layer, 1), q].rearrange("a p n -> p (a n)")).then_inc(m.out_in, 16)

        @block.tensor
        def _(pe):
            pe.wait_ge(m.mla_in, 16)
            pe.wait_ge(squares, 1)
            pe.matmul(m.ps[0][:, :], m.ones[:, :], a.SQ[:, 0, :], start=True, stop=False)
            pe.matmul(m.ps[0][:, :], m.ones[:, :], a.SQ[:, 1, :], start=False, stop=True)
            pe.matmul(m.ps[1][:, :], m.ones[:, :], a.SQ[:, 2, :], start=True, stop=True).then_inc(sums, 1)
            pe.matmul(m.ps[2][64:128, :], m.dup[64:128, :], mx.KRT[64:128, :], start=True, stop=True).then_inc(kr_done, 1)
            pe.wait_ge(normed, 1)
            for t in range(NT):
                if t >= 1:
                    pe.wait_ge(v_home, t)
                pe.matmul(m.ps[3][:, :], mx.CQ[:, 2, t * P:(t + 1) * P], wv, start=True, stop=True).then_inc(v_done, 1)
            for half in range(2):
                for hh in range(HH):
                    h = half * HH + hh
                    if h == 0:
                        pe.wait_ge(inv_rms, 2)
                    if h >= 2:
                        pe.wait_ge(q_home, h - 1)
                        pe.wait_ge(k_home, h)
                    elif h == 0:
                        pe.wait_ge(k_home, 1)
                    elif h == 1:
                        pe.wait_ge(v_home, NT)
                    for k in range(2):
                        last = pe.matmul(m.ps[h % 2][:, :], wq[:, k, h * P:(h + 1) * P], mx.CQ[:, k, :], start=(k == 0), stop=(k == 1))
                    last.then_inc(q_done, 1)
                    pe.matmul(m.ps[2 + h % 2][0:64, :], wk[:, h * 64:(h + 1) * 64], mx.CQ[:, 2, :], start=True, stop=True).then_inc(k_done, 1)
                pe.wait_ge(q_home, (half + 1) * HH)
                pe.wait_ge(k_home, 1 + (half + 1) * HH)
                for step in range(NU + 3):
                    if step < NU:
                        i = half * NU + step
                        hh, t = divmod(step, NT)
                        if i >= 4:
                            pe.wait_ge(probs, i - 3)
                        pe.matmul(m.ps[i % 4][:, :], a.QT[:, hh, t * P:(t + 1) * P], a.KT[:, hh, :], start=True, stop=True).then_inc(scores, 1)
                    if 2 <= step < NU + 2:
                        i = half * NU + step - 2
                        pe.wait_ge(probs_normed, i + 1)
                        if i >= 2:
                            pe.wait_ge(probs_t_home, i - 1)
                        for k in range(NT):
                            last = pe.transpose(m.ps[4 + i % 2][:, k * P:(k + 1) * P], a.PR[:, i % 4, k * P:(k + 1) * P], m.ident[:, :])
                        last.then_inc(probs_t, 1)
                    if step >= 3:
                        i = half * NU + step - 3
                        h, t = divmod(i, NT)
                        pair, rows = h // 2, slice(64 * (h % 2), 64 * (h % 2) + 64)
                        pe.wait_ge(probs_t_home, i + 1)
                        if pair >= 2 and h % 2 == 0 and t == 0:
                            pe.wait_ge(head_home, pair - 1)
                        for k in range(NT):
                            last = pe.matmul(m.ps[6 + pair % 2][rows, t * P:(t + 1) * P], a.V[:, k, h * 64:(h + 1) * 64],
                                             a.PT[:, i % 2, k, :], start=(k == 0), stop=(k == NT - 1))
                        last.then_inc(pv, 1)

        @block.scalar
        def _(act):
            link = Chain(act, act_step)
            act.wait_ge(sums, 1)
            rms_parts(act, link, [a.RS[:, c, :] for c in range(2)], [m.ps[c][:, :] for c in range(2)], [1.0 / 256, 1.0 / 128], 1e-6, inv_rms)
            act.wait_ge(kr_done, 1)
            act.copy(a.KT[64:128, :, :], m.ps[2][64:128, :].rearrange("p (a n) -> p a n", a=1).to_broadcast([64, HH, S])).then_inc(k_home, 1)
            for t in range(NT):
                act.wait_ge(v_done, t + 1)
                act.copy(a.V[:, t, :], m.ps[3][:, :]).then_inc(v_home, 1)
            for half in range(2):
                if half:
                    act.wait_ge(scores, NU)
                for h in range(half * HH, (half + 1) * HH):
                    act.wait_ge(k_done, h + 1)
                    act.copy(a.KT[0:64, h % HH, :], m.ps[2 + h % 2][0:64, :]).then_inc(k_home, 1)
                for step in range(NU + 2):
                    if step < NU:
                        i = half * NU + step
                        act.wait_ge(neg_max, i + 1)
                        if i >= 4:
                            act.wait_ge(probs_t, i - 3)
                        act.activation(a.PR[:, i % 4, :], m.ps[i % 4][:, :], ACT.Exp, bias=a.NM[:, i % 4:i % 4 + 1],
                                       scale=SCALE, accum_out=a.SM[:, i % 4:i % 4 + 1]).then_inc(probs, 1)
                    if step >= 2:
                        i = half * NU + step - 2
                        act.wait_ge(probs_t, i + 1)
                        if i >= 2:
                            act.wait_ge(pv, i - 1)
                        act.copy(a.PT[:, i % 2, :, :].rearrange("p k n -> p (k n)"), m.ps[4 + i % 2][:, :]).then_inc(probs_t_home, 1)

        @block.vector
        def _(dve):
            link = Chain(dve, dve_step)
            cq = mx.CQ[:, :, :].rearrange("p a n -> p (a n)")
            dve.tensor_tensor(a.SQ[:, :, :].rearrange("p a n -> p (a n)"), cq, cq, ALU.mult).then_inc(squares, 1)
            dve.wait_ge(inv_rms, 2)
            for c in range(3):
                last = dve.scalar_tensor_tensor(out=mx.CQ[:, c, :], in0=mx.CQ[:, c, :], scalar=m.CP[:, C_QN + c:C_QN + c + 1],
                                                in1=a.RS[:, c // 2, :], op0=ALU.mult, op1=ALU.mult)
            last.then_inc(normed, 1)
            for half in range(2):
                if half:
                    dve.wait_ge(scores, NU)
                for h in range(half * HH, (half + 1) * HH):
                    dve.wait_ge(q_done, h + 1)
                    dve.tensor_tensor(a.QT[:, h % HH, :], m.ps[h % 2][:, :], m.TAB[:, :], ALU.mult).then_inc(q_home, 1)
                for step in range(NU + 2):
                    if step < NU:
                        i = half * NU + step
                        dve.wait_ge(scores, i + 1)
                        if i >= 4:
                            dve.wait_ge(probs, i - 3)
                        link(dve.reduce_max(a.MX[:, i % 4:i % 4 + 1], m.ps[i % 4][:, :], AX.X))
                        dve.tensor_scalar(a.NM[:, i % 4:i % 4 + 1], a.MX[:, i % 4:i % 4 + 1], -SCALE, None, ALU.mult).then_inc(neg_max, 1)
                    if 1 <= step <= NU:
                        i = half * NU + step - 1
                        dve.wait_ge(probs, i + 1)
                        link(dve.reciprocal(a.RC[:, i % 4:i % 4 + 1], a.SM[:, i % 4:i % 4 + 1]))
                        dve.tensor_scalar(a.PR[:, i % 4, :], a.PR[:, i % 4, :], a.RC[:, i % 4:i % 4 + 1], None, ALU.mult).then_inc(probs_normed, 1)
                    if step >= 2:
                        i = half * NU + step - 2
                        h, t = divmod(i, NT)
                        if h % 2 == 1 and t == NT - 1:
                            dve.wait_ge(pv, i + 1)
                            dve.tensor_copy(m.XT[:, h // 2, :], m.ps[6 + (h // 2) % 2][:, :]).then_inc(head_home, 1)
            dve.wait_ge(head_home, HEADS // 2)


def gate_rows(nc, m, mx, g):
    names = ("act_step", "dve_step", "biased", "abs_ready", "log_ready", "coef", "rows_done",
             "sigmoid_done", "gates_t", "x_t", "em_ready")
    with stage(nc, "gate_rows", *names) as (block, sems):
        act_step, dve_step, biased, abs_ready, log_ready, coef, rows_done, sigmoid_done, gates_t, x_t, em_ready = sems
        R = slice(0, GR)

        @block.scalar
        def _(act):
            link = Chain(act, act_step)
            link(act.activation(g.CO[R, 0:1], m.CP[R, C_AL:C_AL + 1], ACT.Exp))
            link(act.mul(g.CO[R, 0:1], g.CO[R, 0:1], -1.0))
            link(act.activation(g.CO[R, 1:2], m.CP[R, C_SB:C_SB + 1], ACT.Identity, scale=m.CP[R, C_SGN:C_SGN + 1]))
            link(act.activation(mx.SC[R, :], mx.SC[R, :], ACT.Identity, scale=m.CP[R, C_SGN:C_SGN + 1], bias=g.CO[R, 1:2]))
            link(act.activation(mx.IG[R, :], mx.IG[R, :], ACT.Identity, bias=m.CP[R, C_IB:C_IB + 1]))
            act.sem_inc(biased, 1)
            act.wait_ge(abs_ready, 1)
            link(act.activation(g.T1[R, :], g.T1[R, :], ACT.Exp))
            act.activation(g.T1[R, :], g.T1[R, :], ACT.Ln, bias=1.0).then_inc(log_ready, 1)
            act.wait_ge(gates_t, 2)
            act.activation(g.EM[:, :, :], g.GN[:, 1, :, :], ACT.Exp, scale=-1.0).then_inc(em_ready, 1)
            act.wait_ge(em_ready, 1)
            act.activation(mx.O[:, :, :], mx.O[:, :, :], ACT.Sigmoid).then_inc(sigmoid_done, 1)
            act.wait_ge(sigmoid_done, 1)

        @block.vector
        def _(dve):
            link = Chain(dve, dve_step)
            for c in range(2):
                dve.wait_ge(x_t, c + 1)
                link(dve.tensor_copy(g.XN[:, :, c * P:(c + 1) * P], m.ps[1 + c][:, :].rearrange("p (t n) -> p t n", t=NT)))
            dve.wait_ge(biased, 1)
            dve.scalar_tensor_tensor(out=g.T1[R, :], in0=mx.SC[R, :], scalar=-1.0, in1=mx.SC[R, :], op0=ALU.mult, op1=ALU.min).then_inc(abs_ready, 1)
            dve.wait_ge(log_ready, 1)
            link(dve.scalar_tensor_tensor(out=g.SP[R, :], in0=mx.SC[R, :], scalar=0.0, in1=g.T1[R, :], op0=ALU.max, op1=ALU.add))
            link(dve.tensor_scalar(g.T1[R, :], g.SP[R, :], g.CO[R, 0:1], None, ALU.mult))
            link(dve.memset(g.CS[R, :], 0.0))
            link(dve.tensor_tensor_scan(g.CS[0:8, :], m.zeros[0:8, :], g.T1[0:8, :], 0.0, ALU.add, ALU.add))
            link(dve.tensor_tensor_scan(g.CS[32:40, ::-1], m.zeros[32:40, ::-1], g.T1[32:40, ::-1], 0.0, ALU.add, ALU.add))
            link(dve.tensor_tensor(g.FS[R, :], mx.IG[R, :], g.CS[R, :], ALU.subtract))
            link(dve.memset(g.NM[R, :], 0.0))
            link(dve.tensor_tensor_scan(g.NM[0:8, :], m.zeros[0:8, :], g.FS[0:8, :], -3e38, ALU.add, ALU.max))
            link(dve.tensor_tensor_scan(g.NM[32:40, ::-1], m.zeros[32:40, ::-1], g.FS[32:40, ::-1], -3e38, ALU.add, ALU.max))
            link(dve.tensor_tensor(g.T1[R, :], g.CS[R, :], g.NM[R, :], ALU.add))
            dve.tensor_scalar(g.NM[R, :], g.NM[R, :], -1.0, None, ALU.mult).then_inc(rows_done, 1)
            dve.wait_ge(gates_t, 1)
            dve.tensor_copy(g.GN[:, :, :, :].rearrange("p a t r -> p (a t r)"), m.ps[0][:, 0:12 * GR]).then_inc(gates_t, 1)

        @block.tensor
        def _(pe):
            for c in range(2):
                for t in range(NT):
                    last = pe.transpose(m.ps[1 + c][:, t * P:(t + 1) * P], g.XC[:, c, t * P:(t + 1) * P], m.ident[:, :])
                last.then_inc(x_t, 1)
            pe.wait_ge(rows_done, 1)
            for n, rows in enumerate((g.FS, g.T1, g.SP)):
                for t in range(NT):
                    at = (n * NT + t) * GR
                    last = pe.transpose(m.ps[0][:, at:at + GR], rows[0:GR, t * P:(t + 1) * P], m.ident[0:GR, 0:GR])
            last.then_inc(gates_t, 1)


def scans(nc, m, mx, g):
    streams = [("mlstm", h, d, h) for h in range(4) for d in range(2)]
    streams += [("ssd", h, d, 4 + h // 2) for h in range(4) for d in range(2)]
    NS = len(streams)
    last_of_base = {b: max(s for s, x in enumerate(streams) if x[3] == b) for b in range(6)}
    names = ("dve_step", "row_done", "row_masked", "decay", "base_done", "weighted", "applied", "head_out", "y_out")
    with stage(nc, "scans", *names) as (block, sems):
        dve_step, row_done, row_masked, decay, base_done, weighted, applied, head_out, y_out = sems

        def span(d, j):
            return slice(j * P, S) if d == 0 else slice(0, (j + 1) * P)

        def base_operands(b):
            if b < 4:
                rows = slice(64 * (b % 2), 64 * (b % 2) + 64)
                return mx.MK[rows, b // 2, :], mx.MQ[rows, b // 2, :]
            return g.XC[:, 2 + b - 4, :], g.XC[:, 4 + b - 4, :]

        @block.tensor
        def _(pe):
            def row(s):
                kind, h, d, _ = streams[s]
                r = 32 * d + h + (4 if kind == "ssd" else 0)
                if s >= 2:
                    pe.wait_ge(decay, 4 * (s - 1))
                pe.matmul(m.ps[4 + s % 2][:, :], m.ident[0:GR, r:r + 1].to_broadcast([GR, P]), g.NM[0:GR, :],
                          start=True, stop=True).then_inc(row_done, 1)

            def base(b, j):
                k, q = base_operands(b)
                pe.matmul(m.ps[j][:, :], k[:, j * P:(j + 1) * P], q, start=True, stop=True).then_inc(base_done, 1)

            row(0)
            row(1)
            for j in range(NT):
                base(0, j)
            for s, (kind, h, d, b) in enumerate(streams):
                for j in range(NT):
                    if j == NT - 1 and s + 2 < NS:
                        row(s + 2)
                    pe.wait_ge(weighted, 4 * s + j + 1)
                    w = g.W[:, (4 * s + j) % 4, :]
                    if kind == "mlstm":
                        if j == 0 and h >= 1:
                            pe.wait_ge(head_out, 2 * (h - 1) + d + 1)
                        tiles = range(j, NT) if d == 0 else range(0, j + 1)
                        for t in tiles:
                            last = pe.matmul(m.ps[6 + d][:, t * 65:(t + 1) * 65], w[:, t * P:(t + 1) * P], mx.V1[:, j, h, :],
                                             start=(j == 0 and t == tiles[0]), stop=(j == NT - 1 and t == tiles[-1]), skip_group_check=True)
                    else:
                        if s == 8:
                            pe.wait_ge(head_out, 8)
                        e = h % 2
                        last = pe.matmul(m.ps[6 + h // 2][64 * e:64 * e + 64, span(d, j)], g.XN[:, j, h * 64:(h + 1) * 64], w[:, span(d, j)],
                                         start=(d == 0 and j == 0), stop=(d == 1 and j == NT - 1), skip_group_check=True)
                    last.then_inc(applied, 1)
                    if s == last_of_base[b] and b < 5:
                        base(b + 1, j)

        @block.scalar
        def _(act):
            for s, (kind, h, d, b) in enumerate(streams):
                r = 32 * d + h + (4 if kind == "ssd" else 0)
                for j in range(NT):
                    i = 4 * s + j
                    if j == 0:
                        act.wait_ge(row_masked, s + 1)
                    if i >= 4:
                        act.wait_ge(weighted, i - 3)
                    diag = slice(j * P, (j + 1) * P)
                    off = slice((j + 1) * P, S) if d == 0 else slice(0, j * P)
                    bias = g.GN[:, 0, j, r:r + 1]
                    last = act.activation(g.E[:, i % 4, diag], g.RM[:, s % 2, diag], ACT.Exp, bias=bias)
                    if off.stop > off.start:
                        last = act.activation(g.E[:, i % 4, off], m.ps[4 + s % 2][:, off], ACT.Exp, bias=bias)
                    last.then_inc(decay, 1)

        @block.vector
        def _(dve):
            link = Chain(dve, dve_step)

            def mask_row(s):
                dve.wait_ge(row_done, s + 1)
                if s >= 2:
                    dve.wait_ge(decay, 4 * (s - 1))
                dve.tensor_tensor(blocks(g.RM[:, s % 2, :]), blocks(m.ps[4 + s % 2][:, :]), every_block(m.mask[:, streams[s][2], :]), ALU.add).then_inc(row_masked, 1)

            def outputs(s):
                kind, h, d, b = streams[s]
                r = 32 * d + h
                if kind == "mlstm":
                    dve.wait_ge(applied, 4 * s + 4)
                    nd = m.ps[6 + d][:, 0:NT * 65].rearrange("p (t n) -> p t n", t=NT)
                    den = g.DN[:, d, :].rearrange("p (t a) -> p t a", a=1)
                    link(dve.tensor_scalar(g.DT[:, d, :].rearrange("p (t a) -> p t a", a=1), nd[:, :, 64:65], -1.0, None, ALU.mult))
                    link(dve.tensor_tensor(den, g.DT[:, d, :].rearrange("p (t a) -> p t a", a=1), nd[:, :, 64:65], ALU.max))
                    link(dve.tensor_tensor(den, den, g.EM[:, :, r:r + 1], ALU.max))
                    link(dve.reciprocal(g.DN[:, d, :], g.DN[:, d, :]))
                    dst = g.H[:, :, h, :] if d == 0 else g.HB[:, :, :]
                    dve.tensor_tensor(dst, nd[:, :, 0:64], den.to_broadcast([P, NT, 64]), ALU.mult).then_inc(head_out, 1)
                    if d == 1:
                        dve.wait_ge(head_out, 2 * h + d + 1)
                        link(dve.tensor_tensor(g.H[:, :, h, :], g.H[:, :, h, :], g.HB[:, :, :], ALU.add))
                elif h % 2 == 1 and d == 1:
                    dve.wait_ge(applied, 4 * s + 4)
                    c = h // 2
                    dve.scalar_tensor_tensor(out=m.XT[:, 6 + c, :], in0=g.XC[:, c, :], scalar=m.CP[:, C_DS + c:C_DS + c + 1], in1=m.ps[6 + c][:, :],
                                             op0=ALU.mult, op1=ALU.add).then_inc(y_out, 1)

            mask_row(0)
            for s, (kind, h, d, b) in enumerate(streams):
                r = 32 * d + h + (4 if kind == "ssd" else 0)
                for j in range(NT):
                    i = 4 * s + j
                    dve.wait_ge(decay, i + 1)
                    dve.wait_ge(base_done, 4 * b + j + 1)
                    if i >= 4:
                        dve.wait_ge(applied, i - 3)
                    at = span(d, j)
                    if kind == "mlstm":
                        ins = dve.tensor_tensor(g.W[:, i % 4, at], g.E[:, i % 4, at], m.ps[j][:, at], ALU.mult)
                    else:
                        ins = dve.scalar_tensor_tensor(out=g.W[:, i % 4, at], in0=g.E[:, i % 4, at], scalar=g.GN[:, 2, j, r:r + 1],
                                                       in1=m.ps[j][:, at], op0=ALU.mult, op1=ALU.mult)
                    ins.then_inc(weighted, 1)
                    if j == 0 and s + 1 < NS:
                        mask_row(s + 1)
                    if j == 1 and s:
                        outputs(s - 1)
            outputs(NS - 1)
            dve.wait_ge(y_out, 2)


def mixer_norms(nc, m, mx, g):
    names = ("act_step", "dve_step", "y_squares", "y_sums", "y_inv", "h_squares", "h_var", "h_inv", "h_ready", "h_t")
    with stage(nc, "mixer_norms", *names) as (block, sems):
        act_step, dve_step, y_squares, y_sums, y_inv, h_squares, h_var, h_inv, h_ready, h_t = sems
        H = g.H[:, :, :, :].rearrange("p t h d -> p (t h) d")
        Hf = g.H[:, :, :, :].rearrange("p t h d -> p (t h d)")
        H2 = g.E[:, 0:2, :].rearrange("p a n -> p (a n)")
        mean = g.MEAN[:, 0, :]
        var = g.MEAN[:, 1, :]

        @block.vector
        def _(dve):
            link = Chain(dve, dve_step)
            Y = m.XT[:, 6:8, :].rearrange("p a n -> p (a n)")
            link(dve.tensor_tensor(Y, Y, mx.Z[:, :, :].rearrange("p a n -> p (a n)"), ALU.mult))
            dve.tensor_tensor(g.W[:, 0:2, :].rearrange("p a n -> p (a n)"), Y, Y, ALU.mult).then_inc(y_squares, 1)
            link(dve.reduce_sum(mean, H, AX.X))
            link(dve.tensor_scalar(mean, mean, 1.0 / 64, None, ALU.mult))
            link(dve.tensor_tensor(H, H, mean.rearrange("p (n a) -> p n a", a=1).to_broadcast([P, 16, 64]), ALU.subtract))
            link(dve.tensor_tensor(H2, Hf, Hf, ALU.mult))
            dve.reduce_sum(var, H2.rearrange("p (n d) -> p n d", d=64), AX.X).then_inc(h_var, 1)
            dve.wait_ge(y_inv, 2)
            for c in range(2):
                link(dve.scalar_tensor_tensor(out=m.XT[:, 6 + c, :], in0=m.XT[:, 6 + c, :], scalar=m.CP[:, C_SN + c:C_SN + c + 1],
                                              in1=g.RM[:, c, :], op0=ALU.mult, op1=ALU.mult))
            dve.wait_ge(h_inv, 1)
            link(dve.tensor_tensor(H, H, var.rearrange("p (n a) -> p n a", a=1).to_broadcast([P, 16, 64]), ALU.mult))
            H3 = g.H[:, :, :, :].rearrange("p t h d -> p t (h d)")
            link(dve.tensor_tensor(H3, H3, m.RP[:, R_MN:R_MN + 256].rearrange("p (a n) -> p a n", a=1).to_broadcast([P, NT, 256]), ALU.mult))
            dve.tensor_tensor(Hf, Hf, mx.O[:, :, :].rearrange("p t n -> p (t n)"), ALU.mult).then_inc(h_ready, 1)
            for c in range(2):
                dve.wait_ge(h_t, c + 1)
                link(dve.tensor_copy(m.XT[:, 4 + c, :], m.ps[2 + c][:, :]))

        @block.tensor
        def _(pe):
            pe.wait_ge(y_squares, 1)
            for c in range(2):
                pe.matmul(m.ps[c][:, :], m.ones[:, :], g.W[:, c, :], start=True, stop=True).then_inc(y_sums, 1)
            pe.wait_ge(h_ready, 1)
            H3 = g.H[:, :, :, :].rearrange("p t h d -> p t (h d)")
            for c in range(2):
                for t in range(NT):
                    last = pe.transpose(m.ps[2 + c][:, t * P:(t + 1) * P], H3[:, t, c * P:(c + 1) * P], m.ident[:, :])
                last.then_inc(h_t, 1)

        @block.scalar
        def _(act):
            link = Chain(act, act_step)
            act.wait_ge(y_sums, 2)
            rms_parts(act, link, [g.RM[:, c, :] for c in range(2)], [m.ps[c][:, :] for c in range(2)], [1.0 / 128] * 2, 1e-6, y_inv)
            act.wait_ge(h_var, 1)
            rms_parts(act, link, [var], [var], [1.0 / 64], 1e-5, h_inv)


def norm_stage(nc, m, ln, which, layer, XS=None, WS=None):
    names = ("rows_in", "raw_in", "w_high", "w_low", "xt_high", "xt_low", "tile_done", "dve_step", "var_ready", "inv_ready", "scaled", "pool_step")
    with stage(nc, "norm_stage", *names) as (block, sems):
        rows_in, raw_in, w_high, w_low, xt_high, xt_low, tile_done, dve_step, var_ready, inv_ready, scaled, pool_step = sems
        at = (R_L1, R_L2)[which]
        groups = [[t] for t in range(NT)] if XS else [list(range(NT))]

        @block.sync
        def _(sp):
            if XS:
                for q in (2, 3):
                    sp.dma_start(m.raw[:, q - 2, :], m.d["w_out"][bass.ds(layer, 1), q].rearrange("a p n -> p (a n)")).then_inc(raw_in, 16)
                    sp.wait_ge(raw_in, 16 * (q - 1))
            sp.dma_start(ln.GB[:, :], m.d["rows"][bass.ds(layer, 1), at:at + 2 * D].to_broadcast([P, 2 * D])).then_inc(rows_in, 16)
            sp.wait_ge(rows_in, 16)

        @block.tensor
        def _(pe):
            if XS:
                for kh in range(2):
                    pe.wait_ge(xt_low, 4 * (kh + 1))
                    for n in range(2 * NT):
                        half, t = (n % 2, n // 2) if kh else (n // NT, n % NT)
                        pe.wait_ge(w_low, 2 * kh + half + 1)
                        step = 0
                        for k in range(4):
                            for hw, hx in TERMS:
                                last = pe.matmul(m.ps[2 * t + half][:, :], XS[:, hx, 4 * kh + k, t * P:(t + 1) * P], WS[:, 2 * kh + half, hw, k * S:(k + 1) * S],
                                                 start=(kh == 0 and step == 0), stop=(kh == 1 and step == 11))
                                step += 1
                        if kh:
                            last.then_inc(tile_done, 1)

        @block.vector
        def _(dve):
            link = Chain(dve, dve_step)
            if XS:
                for k in range(KD):
                    dve.wait_ge(xt_high, k + 1)
                    dve.tensor_tensor(XS[:, 1, k, :], m.XT[:, k, :], XS[:, 0, k, :].bitcast(F32), ALU.subtract).then_inc(xt_low, 1)
            for n, tiles in enumerate(groups):
                for t in tiles:
                    for half in range(2):
                        cols = slice(half * S, (half + 1) * S)
                        if XS:
                            dve.wait_ge(tile_done, 2 * t + half + 1)
                            y = m.ps[2 * t + half][:, :]
                        else:
                            y = ln.Y[:, t, cols]
                        link(dve.scalar_tensor_tensor(out=m.X[:, t, cols], in0=m.X[:, t, cols], scalar=ALPHA, in1=y, op0=ALU.mult, op1=ALU.add))
                        link(dve.bn_stats(ln.ST[:, t, half, :], m.X[:, t, cols]))
                    link(dve.bn_aggr(ln.MV[:, t, :], ln.ST[:, t, :, :]))
                dve.sem_inc(var_ready, 1)
                dve.wait_ge(inv_ready, n + 1)
                at = slice(tiles[0], tiles[-1] + 1)
                link(dve.reciprocal(ln.IV[:, at], ln.IV[:, at]))
                for t in tiles:
                    link(dve.tensor_scalar(m.X[:, t, :], m.X[:, t, :], ln.MV[:, t, 0:1], ln.IV[:, t:t + 1], ALU.subtract, ALU.mult))
                    if t == 0:
                        dve.wait_ge(rows_in, 16)
                    link(dve.tensor_tensor(m.X[:, t, :], m.X[:, t, :], ln.GB[:, 0:D], ALU.mult))
                    dve.sem_inc(scaled, 1)

        @block.scalar
        def _(act):
            if XS:
                for k in range(KD):
                    act.copy(XS[:, 0, k, :], m.XT[:, k, :]).then_inc(xt_high, 1)
                    if k in (3, 7):
                        q = k // 4
                        act.wait_ge(m.out_in, 32)
                        act.copy(WS[:, q, 0, :], m.raw[:, 2 + q, :]).then_inc(w_high, 1)
                for q in (2, 3):
                    act.wait_ge(raw_in, 16 * (q - 1))
                    act.copy(WS[:, q, 0, :], m.raw[:, q - 2, :]).then_inc(w_high, 1)
            for n, tiles in enumerate(groups):
                act.wait_ge(var_ready, n + 1)
                at = slice(tiles[0], tiles[-1] + 1)
                act.activation(ln.IV[:, at], ln.MV[:, at, 1], ACT.Sqrt, bias=1e-5).then_inc(inv_ready, 1)

        @block.gpsimd
        def _(pool):
            link = Chain(pool, pool_step)
            if XS:
                for q in range(4):
                    pool.wait_ge(w_high, q + 1)
                    pool.tensor_tensor(WS[:, q, 1, :], m.raw[:, (q + 2) % 4, :], WS[:, q, 0, :].bitcast(F32), ALU.subtract).then_inc(w_low, 1)
            pool.wait_ge(rows_in, 16)
            for t in range(NT):
                pool.wait_ge(scaled, t + 1)
                link(pool.tensor_tensor(m.X[:, t, :], m.X[:, t, :], ln.GB[:, D:2 * D], ALU.add))


def router(nc, m, r):
    with stage(nc, "router", "logits_done", "dve_step", "exp_in", "exp_done", "x_hi", "x_lo") as (block, (logits_done, dve_step, exp_in, exp_done, x_hi, x_lo)):

        @block.tensor
        def _(pe):
            for t in range(NT):
                for k in range(KD):
                    last = pe.matmul(m.ps[0][:, t * 20:(t + 1) * 20], m.XT[:, k, t * P:(t + 1) * P], m.WR[:, k, :],
                                     start=(k == 0), stop=(k == KD - 1))
            last.then_inc(logits_done, 1)

        @block.vector
        def _(dve):
            link = Chain(dve, dve_step)

            def wide(x, n=4):
                return x.rearrange("p (t a) -> p t a", a=1).to_broadcast([P, NT, n])

            def first_max(hot, top, x):
                link(dve.reduce_max(top, x, AX.X))
                link(dve.tensor_tensor(hot, x, wide(top), ALU.is_equal))
                link(dve.tensor_tensor(hot, hot, m.CC[:, 4:8].rearrange("p (a n) -> p a n", a=1).to_broadcast([P, NT, 4]), ALU.mult))
                link(dve.reduce_max(r.t1[:, :], hot, AX.X))
                link(dve.tensor_tensor(hot, hot, wide(r.t1[:, :]), ALU.is_equal))

            lg = r.LG
            dve.wait_ge(logits_done, 1)
            link(dve.tensor_tensor(lg[:, :, :], m.ps[0][:, 0:80].rearrange("p (t n) -> p t n", t=NT),
                                   m.RP[:, R_RB:R_RB + 20].rearrange("p (a n) -> p a n", a=1).to_broadcast([P, NT, 20]), ALU.add))
            first_max(r.hg[:, :, :], r.gm[:, :], lg[:, :, 0:4])
            link(dve.tensor_tensor(r.e4[:, :, :], lg[:, :, 0:4], wide(r.gm[:, :]), ALU.subtract))
            for g in range(NGR):
                hot = r.hg[:, :, g:g + 1].to_broadcast([P, NT, 4])
                part = lg[:, :, 4 + 4 * g:8 + 4 * g]
                if g == 0:
                    link(dve.tensor_tensor(r.el[:, :, :], part, hot, ALU.mult))
                else:
                    link(dve.tensor_tensor(r.h2[:, :, :], part, hot, ALU.mult))
                    link(dve.tensor_tensor(r.el[:, :, :], r.el[:, :, :], r.h2[:, :, :], ALU.add))
            first_max(r.h1[:, :, :], r.m1[:, :], r.el[:, :, :])
            link(dve.scalar_tensor_tensor(out=r.el[:, :, :], in0=r.h1[:, :, :], scalar=NEG, in1=r.el[:, :, :], op0=ALU.mult, op1=ALU.add))
            first_max(r.h2[:, :, :], r.m2[:, :], r.el[:, :, :])
            link(dve.tensor_tensor(r.m2[:, :], r.m2[:, :], r.m1[:, :], ALU.subtract))
            dve.sem_inc(exp_in, 1)
            dve.wait_ge(exp_done, 2)
            link(dve.tensor_tensor(r.el[:, :, :], r.h1[:, :, :], r.h2[:, :, :], ALU.add))
            for g in range(NGR):
                link(dve.tensor_tensor(r.OH[:, :, 4 * g:4 * g + 4], r.el[:, :, :], r.hg[:, :, g:g + 1].to_broadcast([P, NT, 4]), ALU.mult))
            link(dve.reduce_sum(r.gm[:, :], r.e4[:, :, :], AX.X))
            link(dve.tensor_scalar(r.m1[:, :], r.m2[:, :], 1.0, None, ALU.add))
            link(dve.tensor_tensor(r.gm[:, :], r.gm[:, :], r.m1[:, :], ALU.mult))
            link(dve.reciprocal(r.gm[:, :], r.gm[:, :]))
            link(dve.tensor_tensor(r.m2[:, :], r.gm[:, :], r.m2[:, :], ALU.mult))
            link(dve.tensor_tensor(r.h1[:, :, :], r.h1[:, :, :], wide(r.gm[:, :]), ALU.mult))
            link(dve.tensor_tensor(r.h2[:, :, :], r.h2[:, :, :], wide(r.m2[:, :]), ALU.mult))
            link(dve.tensor_tensor(r.h1[:, :, :], r.h1[:, :, :], r.h2[:, :, :], ALU.add))
            for g in range(NGR):
                link(dve.tensor_tensor(r.COMB[:, :, 4 * g:4 * g + 4], r.h1[:, :, :], r.hg[:, :, g:g + 1].to_broadcast([P, NT, 4]), ALU.mult))

        @block.scalar
        def _(act):
            for t in range(NT):
                act.copy(r.XH[:, t, :], m.X[:, t, :]).then_inc(x_hi, 1)
            act.wait_ge(exp_in, 1)
            act.activation(r.e4[:, :, :], r.e4[:, :, :], ACT.Exp).then_inc(exp_done, 1)
            act.activation(r.m2[:, :], r.m2[:, :], ACT.Exp).then_inc(exp_done, 1)
            act.wait_ge(exp_done, 2)

        @block.gpsimd
        def _(pool):
            pool.memset(r.Y[:, :, :], 0.0).then_inc(x_lo, 1)
            for t in range(NT):
                pool.wait_ge(x_hi, t + 1)
                pool.tensor_tensor(r.XL[:, t, :], m.X[:, t, :], r.XH[:, t, :].bitcast(F32), ALU.subtract).then_inc(x_lo, 1)
            pool.wait_ge(x_lo, NT + 1)


def dispatch(nc, m, r):
    names = ("pe_rank", "pe_total", "dve_step")
    with stage(nc, "dispatch", *names) as (block, (pe_rank, pe_total, dve_step)):

        @block.tensor
        def _(pe):
            for t in range(NT):
                for u in range(t):
                    pe.matmul(m.ps[0][:, t * NE:(t + 1) * NE], m.ones[:, :], r.OH[:, u, :], start=(u == 0), stop=False)
                last = pe.matmul(m.ps[0][:, t * NE:(t + 1) * NE], r.TRI[:, :], r.OH[:, t, :], start=(t == 0), stop=True)
            last.then_inc(pe_rank, 1)
            for t in range(NT):
                last = pe.matmul(m.ps[1][:, 0:NE], m.ones[:, :], r.OH[:, t, :], start=(t == 0), stop=(t == NT - 1))
            last.then_inc(pe_total, 1)

        @block.vector
        def _(dve):
            link = Chain(dve, dve_step)
            dve.memset(r.POS[:, :, NE:], -10000.0)
            dve.wait_ge(pe_rank, 1)
            link(dve.tensor_scalar(r.POS[:, :, 0:NE], r.OH[:, :, :], 10000.0, -10000.0, ALU.mult, ALU.add))
            link(dve.tensor_tensor(r.POS[:, :, 0:NE], r.POS[:, :, 0:NE], m.ps[0][:, 0:NT * NE].rearrange("p (t e) -> p t e", t=NT), ALU.add))
            dve.wait_ge(pe_total, 1)
            link(dve.reduce_max(r.NP[:, 0:1], m.ps[1][:, 0:NE], AX.X))
            link(dve.tensor_scalar(r.NP[:, 1:2], r.NP[:, 0:1], 128.0, 1.0, ALU.is_gt, ALU.add))
            for n in (256.0, 384.0):
                link(dve.tensor_scalar(r.NP[:, 2:3], r.NP[:, 0:1], n, None, ALU.is_gt))
                link(dve.tensor_tensor(r.NP[:, 1:2], r.NP[:, 1:2], r.NP[:, 2:3], ALU.add))
            link(dve.tensor_copy(r.NPI[:, :], r.NP[:, 1:2]))
            link(dve.tensor_copy(r.CW[:, :, :, 0], r.COMB[:, :, :]))
            link(dve.tensor_tensor(r.CW[:, :, :, 1], r.COMB[:, :, :], r.CW[:, :, :, 0].bitcast(F32), ALU.subtract))


def experts(nc, m, r, layer):
    GE = NE // NGR
    names = ("gu_in0", "gu_in1", "dn_in0", "dn_in1", "sel_ready", "sel_free", "gathered", "xe_act", "xe_dve", "weights_done", "dve_step", "selt_done", "selt_home",
             "gate_up", "silu_done", "hidden", "ht_done", "ht_home", "down", "ye_hi", "ye_home", "scattered", "added")
    with stage(nc, "experts", *names) as (block, sems):
        (gu_in0, gu_in1, dn_in0, dn_in1, sel_ready, sel_free, gathered, xe_act, xe_dve, weights_done, dve_step, selt_done, selt_home,
         gate_up, silu_done, hidden, ht_done, ht_home, down, ye_hi, ye_home, scattered, added) = sems
        gu_in, dn_in = (gu_in0, gu_in1), (dn_in0, dn_in1)
        GU = KD * S
        XE = m.XT

        slots = [m.raw[:, 2 * b:2 * b + 2, :].rearrange("p a n -> p (a n)") for b in range(2)]

        def load_gate_up(sp, n, b):
            sp.dma_start(slots[b], m.d["w_exp"][bass.ds(layer, 1), bass.ds(n, 1), :, 0:GU].rearrange("a b p n -> p (a b n)")).then_inc(gu_in[b], 16)

        def load_down(sp, n, b):
            sp.dma_start(r.DN[:, b, :], m.d["w_exp"][bass.ds(layer, 1), bass.ds(n, 1), :, GU:].rearrange("a b p n -> p (a b n)")).then_inc(dn_in[b], 16)

        @block.sync
        def _(sp):
            for b in range(2):
                load_gate_up(sp, b, b)
            for b in range(2):
                load_down(sp, b, b)
            with sp.Fori(0, NE // 2 - 1) as i:
                for b in range(2):
                    sp.wait_ge(gate_up, i * 2 + b + 1)
                    load_gate_up(sp, i * 2 + (b + 2), b)
                    sp.wait_ge(down, i * 4 + 2 * (b + 1))
                    load_down(sp, i * 2 + (b + 2), b)

        @block.tensor
        def _(pe):
            with pe.Fori(0, NGR) as g:

                def gate_up_of(e):
                    pe.wait_ge(gu_in[e % 2], g * 32 + 16 * (e // 2 + 1))
                    if e >= 2:
                        pe.wait_ge(hidden, g * GE + e - 1)
                    for k in range(KD):
                        last = pe.matmul(m.ps[4 + e % 2][:, :], XE[:, k, e * P:(e + 1) * P], slots[e % 2][:, k * S:(k + 1) * S],
                                         start=(k == 0), stop=(k == KD - 1))
                    last.then_inc(gate_up, 1)

                def hidden_t(e):
                    pe.wait_ge(hidden, g * GE + e + 1)
                    for f in range(2):
                        last = pe.transpose(m.ps[6 + e % 2][:, f * P:(f + 1) * P], r.H[:, e % 2, f * P:(f + 1) * P], m.ident[:, :])
                    last.then_inc(ht_done, 1)

                def sel_t(e):
                    if e >= 2:
                        pe.wait_ge(selt_home, g * GE + e - 1)
                    for t in range(NT):
                        last = pe.transpose(m.ps[2 + e % 2][:, t * P:(t + 1) * P], r.SEL[:, t, e * P:(e + 1) * P].bitcast(F32), m.ident[:, :])
                    last.then_inc(selt_done, 1)

                def down_of(e):
                    pe.wait_ge(dn_in[e % 2], g * 32 + 16 * (e // 2 + 1))
                    pe.wait_ge(ht_home, g * GE + e + 1)
                    if e == 0:
                        pe.wait_ge(selt_home, g * GE + GE)
                    for half in range(2):
                        if e:
                            pe.wait_ge(ye_home, g * 8 + 2 * (e - 1) + half + 1)
                        for f in range(2):
                            at = f * D + half * S
                            last = pe.matmul(m.ps[2 + half][:, :], r.HT[:, e % 2, f * P:(f + 1) * P], r.DN[:, e % 2, at:at + S], start=(f == 0), stop=(f == 1))
                        last.then_inc(down, 1)

                def scatter(pair):
                    pe.wait_ge(ye_home, g * 8 + 4 * (pair + 1))
                    for v in range(2 * NT):
                        t, half = divmod(v, 2)
                        pe.wait_ge(added, g * 16 + 8 * pair + v + 1)
                        n = 0
                        for e in range(2):
                            for part in range(2):
                                last = pe.matmul(m.ps[v % 2][:, :], r.SELT[:, 2 * pair + e, t * P:(t + 1) * P],
                                                 r.YE[:, part, e, half * S:(half + 1) * S], start=(n == 0), stop=(n == 3))
                                n += 1
                        last.then_inc(scattered, 1)

                pe.wait_ge(sel_ready, g * NT + NT)
                for k in range(KD):
                    if k < 2:
                        pe.wait_ge(added, g * 16 + k + 1)
                    else:
                        pe.wait_ge((xe_act, xe_dve)[k % 2], g * 4 + k // 2)
                    n = 0
                    for t in range(NT):
                        for part in (r.XH, r.XL):
                            last = pe.matmul(m.ps[k % 2][:, :], part[:, t, k * P:(k + 1) * P], r.SEL[:, t, :], start=(n == 0), stop=(n == 7))
                            n += 1
                    last.then_inc(gathered, 1)
                for e in range(GE):
                    for t in range(NT):
                        last = pe.matmul(m.ps[7][:, 2 * e:2 * e + 2], r.SEL[:, t, e * P:(e + 1) * P],
                                         r.CW[:, t, bass.ds(g * GE + e, 1), :].rearrange("p a b -> p (a b)"), start=(t == 0), stop=(t == NT - 1))
                last.then_inc(weights_done, 1)
                sel_t(0)
                sel_t(1)
                pe.wait_ge(xe_act, g * 4 + 4)
                pe.wait_ge(xe_dve, g * 4 + 4)
                gate_up_of(0)
                sel_t(2)
                gate_up_of(1)
                hidden_t(0)
                sel_t(3)
                down_of(0)
                hidden_t(1)
                gate_up_of(2)
                down_of(1)
                gate_up_of(3)
                hidden_t(2)
                scatter(0)
                hidden_t(3)
                down_of(2)
                down_of(3)
                scatter(1)

        @block.scalar
        def _(act):
            with act.Fori(0, NGR) as g:

                def silu(e):
                    act.wait_ge(gate_up, g * GE + e + 1)
                    act.activation(r.SG[:, e % 2, :], m.ps[4 + e % 2][:, 0:FE], ACT.Silu).then_inc(silu_done, 1)

                def sel_home(e):
                    act.wait_ge(selt_done, g * GE + e + 1)
                    if e == GE - 1:
                        act.sem_inc(sel_free, 1)
                    act.copy(r.SELT[:, e, :], m.ps[2 + e % 2][:, :]).then_inc(selt_home, 1)

                def hidden_home(e):
                    act.wait_ge(ht_done, g * GE + e + 1)
                    act.copy(r.HT[:, e % 2, :], m.ps[6 + e % 2][:, 0:2 * P]).then_inc(ht_home, 1)

                def high_part(e):
                    for half in range(2):
                        act.wait_ge(down, g * 8 + 2 * e + half + 1)
                        act.copy(r.YE[:, 0, e % 2, half * S:(half + 1) * S], m.ps[2 + half][:, :]).then_inc(ye_hi, 1)

                for k in range(0, KD, 2):
                    act.wait_ge(gathered, g * KD + k + 1)
                    act.copy(XE[:, k, :], m.ps[0][:, :]).then_inc(xe_act, 1)
                sel_home(0)
                sel_home(1)
                silu(0)
                sel_home(2)
                silu(1)
                hidden_home(0)
                sel_home(3)
                high_part(0)
                hidden_home(1)
                silu(2)
                high_part(1)
                silu(3)
                hidden_home(2)
                hidden_home(3)
                high_part(2)
                high_part(3)

        @block.vector
        def _(dve):
            dve.sem_inc(added, 2)

            def select(turn):
                for t in range(NT):
                    for e in range(GE):
                        at = r.POS[:, t, e:e + 1] if turn is None else r.POS[:, t, bass.ds(turn * GE + (GE + e), 1)]
                        last = dve.tensor_scalar(r.SEL[:, t, e * P:(e + 1) * P], r.IOTA[:, :], at, None, ALU.is_equal)
                    last.then_inc(sel_ready, 1)

            select(None)
            with dve.Fori(0, NGR) as g:

                def hidden_of(e):
                    dve.wait_ge(silu_done, g * GE + e + 1)
                    dve.scalar_tensor_tensor(out=r.H[:, e % 2, :], in0=m.ps[4 + e % 2][:, FE:2 * FE], scalar=r.WS[:, e:e + 1],
                                             in1=r.SG[:, e % 2, :], op0=ALU.mult, op1=ALU.mult).then_inc(hidden, 1)

                def low_part(e):
                    for half in range(2):
                        cols = slice(half * S, (half + 1) * S)
                        dve.wait_ge(ye_hi, g * 8 + 2 * e + half + 1)
                        dve.tensor_tensor(r.YE[:, 1, e % 2, cols], m.ps[2 + half][:, :], r.YE[:, 0, e % 2, cols].bitcast(F32),
                                          ALU.subtract).then_inc(ye_home, 1)

                def add(pair):
                    for v in range(2 * NT):
                        t, cols = v // 2, slice((v % 2) * S, (v % 2 + 1) * S)
                        dve.wait_ge(scattered, g * 16 + 8 * pair + v + 1)
                        dve.wait_ge(added, g * 16 + 8 * pair + v + 2)
                        dve.tensor_tensor(r.Y[:, t, cols], r.Y[:, t, cols], m.ps[v % 2][:, :], ALU.add).then_inc(added, 1)

                for k in range(1, KD, 2):
                    dve.wait_ge(gathered, g * KD + k + 1)
                    dve.tensor_copy(XE[:, k, :], m.ps[1][:, :]).then_inc(xe_dve, 1)
                dve.wait_ge(weights_done, g + 1)
                dve.reduce_sum(r.WS[:, :], m.ps[7][:, 0:2 * GE].rearrange("p (e a) -> p e a", a=2), AX.X).then_inc(dve_step, 1)
                dve.wait_ge(dve_step, g + 1)
                hidden_of(0)
                hidden_of(1)
                low_part(0)
                dve.wait_ge(sel_free, g + 1)
                select(g)
                hidden_of(2)
                low_part(1)
                hidden_of(3)
                add(0)
                low_part(2)
                low_part(3)
                add(1)


def next_pass(nc, r):
    with stage(nc, "next_pass", "moved") as (block, (moved,)):

        @block.vector
        def _(dve):
            dve.tensor_scalar(r.POS[:, :, :], r.POS[:, :, :], -float(P), None, ALU.add).then_inc(moved, 1)
            dve.wait_ge(moved, 1)


GH, GD = 4, 128
FF = 4096
K_NM, K_NP, K_GC, K_LC, K_LB, K_AB, K_XB, K_AP, K_GN, K_AL, K_DB, K_N = 0, 8, 16, 64, 80, 84, 88, 92, 96, 97, 98, 99


def rms_transpose(nc, m, n, XS, gain, extra=None):
    names = ("squared", "inv", "act_step", "dve_step", "normed", "transposed", "xt_act", "xt_dve", "param_in")
    with stage(nc, "rms_transpose", *names) as (block, (squared, inv, act_step, dve_step, normed, transposed, xt_act, xt_dve, param_in)):

        @block.sync
        def _(sp):
            if extra:
                sp.wait_ge(param_in, 16 * extra(sp, param_in))

        @block.scalar
        def _(act):
            for t in range(NT):
                act.activation(n.XN[:, t, :], m.X[:, t, :], ACT.Square, accum_out=n.SS[:, t:t + 1]).then_inc(act_step, 1)
            act.wait_ge(act_step, NT)
            act.activation(n.SS[:, :], n.SS[:, :], ACT.Sqrt, scale=1.0 / D, bias=1e-6).then_inc(inv, 1)
            if extra:
                act.wait_ge(param_in, 16)
            for k in range(KD):
                act.wait_ge(transposed, k + 1)
                act.activation(XS[:, 0, k, :], m.ps[k][:, :], ACT.Copy, scale=m.CP[:, gain + k:gain + k + 1]).then_inc(xt_act, 1)
            act.wait_ge(xt_act, KD)

        @block.vector
        def _(dve):
            dve.wait_ge(inv, 1)
            dve.reciprocal(n.SS[:, :], n.SS[:, :]).then_inc(dve_step, 1)
            dve.wait_ge(dve_step, 1)
            for t in range(NT):
                dve.tensor_scalar(n.DG[:, t, :], m.ident[:, :], n.SS[:, t:t + 1], None, ALU.mult).then_inc(normed, 1)
            if extra:
                dve.wait_ge(param_in, 16)
            for k in range(KD):
                dve.wait_ge(xt_act, k + 1)
                dve.scalar_tensor_tensor(out=XS[:, 1, k, :], in0=m.ps[k][:, :], scalar=m.CP[:, gain + k:gain + k + 1],
                                         in1=XS[:, 0, k, :].bitcast(F32), op0=ALU.mult, op1=ALU.subtract).then_inc(xt_dve, 1)
            dve.wait_ge(xt_dve, KD)

        @block.tensor
        def _(pe):
            for k in range(KD):
                for t in range(NT):
                    if k == 0:
                        pe.wait_ge(normed, t + 1)
                    last = pe.matmul(m.ps[k][:, t * P:(t + 1) * P], m.X[:, t, k * P:(k + 1) * P], n.DG[:, t, :], start=True, stop=True)
                last.then_inc(transposed, 1)


def in_projection_2(nc, m, b, q):
    names = ("unit_done", "home_act", "home_dve", "w_high", "w_low", "conv_step", "conv_done", "margins",
             "silu_done", "raw0", "raw1", "raw2", "raw3")
    with stage(nc, "in_projection_2", *names) as (block, (unit_done, home_act, home_dve, w_high, w_low, conv_step, conv_done, margins, silu_done, *raw)):
        homes = [q.QB[:, c, 3:3 + S] for c in range(12)] + [b.Z[:, c, :] for c in range(4)]
        homes += [b.LX[:, c, 3:3 + S] for c in range(4)] + [b.LG[:, c, :] for c in range(4)]
        NU = len(homes) + 1
        NB = NU // 2 + 1
        sizes = [KD * 256] * (NB - 1) + [KD * GR]

        @block.sync
        def _(sp):
            for i in range(NB):
                if i >= 4:
                    sp.wait_ge(w_low, i - 3)
                src = m.d["w_in_2"][i] if i < NB - 1 else m.d["w_gates_2"]
                sp.dma_start(q.ring[:, i % 4, 0:sizes[i]], src).then_inc(raw[i % 4], 16)

        @block.tensor
        def _(pe):
            for u in range(NU):
                i, c = divmod(u, 2)
                if c == 0:
                    pe.wait_ge(w_low, i + 1)
                if u >= 8:
                    pe.wait_ge((home_act, home_dve)[u % 2], (u - 8) // 2 + 1)
                width, n = (GR, GR) if u == NU - 1 else (256, P)
                step = 0
                for k in range(KD):
                    for hw, hx in TERMS:
                        at = k * width + c * P
                        last = pe.matmul(m.ps[u % 8][0:n, :], q.WS[:, i % 2, hw, at:at + n], b.XS[:, hx, k, :], start=(step == 0), stop=(step == 3 * KD - 1))
                        step += 1
                last.then_inc(unit_done, 1)

        @block.scalar
        def _(act):
            for i in range(NB):
                act.wait_ge(raw[i % 4], 16 * (i // 4 + 1))
                if i >= 2:
                    act.wait_ge(unit_done, 2 * (i - 1))
                act.copy(q.WS[:, i % 2, 0, 0:sizes[i]], q.ring[:, i % 4, 0:sizes[i]]).then_inc(w_high, 1)
                if i:
                    u = 2 * i - 2
                    act.wait_ge(unit_done, u + 1)
                    act.copy(homes[u], m.ps[u % 8][:, :]).then_inc(home_act, 1)
            for c in range(12):
                act.wait_ge(conv_done, c + 1)
                act.activation(b.XC[:, c, :], b.XC[:, c, :], ACT.Silu).then_inc(silu_done, 1)
            act.wait_ge(silu_done, 12)
            act.wait_ge(unit_done, NU)
            act.copy(b.GR[0:GR, :], m.ps[(NU - 1) % 8][0:GR, :]).then_inc(home_act, 1)
            act.wait_ge(home_act, (NU + 1) // 2)

        @block.vector
        def _(dve):
            link = Chain(dve, conv_step)
            for u in range(NU):
                if u % 2:
                    dve.wait_ge(unit_done, u + 1)
                    dve.tensor_copy(homes[u], m.ps[u % 8][:, :]).then_inc(home_dve, 1)
                for c in (u - 1, u) if u % 2 and u < 12 else ():
                    dve.wait_ge((home_act, home_dve)[c % 2], c // 2 + 1)
                    if c == 0:
                        dve.wait_ge(margins, 1)
                    for tap in range(4):
                        w = m.CP[:, K_GC + 4 * c + tap:K_GC + 4 * c + tap + 1]
                        src = q.QB[:, c, tap:tap + S]
                        if tap == 0:
                            link(dve.tensor_scalar(q.TP[:, :], src, w, None, ALU.mult))
                        else:
                            link(dve.scalar_tensor_tensor(out=src if tap == 3 else q.TP[:, :], in0=src, scalar=w, in1=q.TP[:, :], op0=ALU.mult, op1=ALU.add))
                    dve.sem_inc(conv_done, 1)
            dve.wait_ge(home_dve, NU // 2)

        @block.gpsimd
        def _(pool):
            pool.memset(q.QB[:, :, 0:3], 0.0).then_inc(margins, 1)
            pool.memset(b.LX[:, :, 0:3], 0.0)
            for i in range(NB):
                n = sizes[i]
                pool.wait_ge(w_high, i + 1)
                pool.tensor_tensor(q.WS[:, i % 2, 1, 0:n], q.ring[:, i % 4, 0:n], q.WS[:, i % 2, 0, 0:n].bitcast(F32), ALU.subtract).then_inc(w_low, 1)


def gdn_prepare(nc, m, b, q):
    names = ("act_step", "dve_step", "squares", "sums", "logs", "inv", "biased", "abs_ready", "log_ready",
             "rows_a", "rows_b", "rows_c", "rows_t")
    with stage(nc, "gdn_prepare", *names) as (block, sems):
        act_step, dve_step, squares, sums, logs, inv, biased, abs_ready, log_ready, rows_a, rows_b, rows_c, rows_t = sems
        R = slice(0, GH)

        @block.vector
        def _(dve):
            link = Chain(dve, dve_step)

            def square(n):
                if n >= 2:
                    dve.wait_ge(sums, n - 1)
                dve.tensor_tensor(q.SQ[:, n % 2, :], b.XC[:, n, :], b.XC[:, n, :], ALU.mult).then_inc(squares, 1)

            square(0)
            square(1)
            dve.wait_ge(biased, 1)
            dve.scalar_tensor_tensor(out=b.G1[R, :], in0=b.GR[R, :], scalar=-1.0, in1=b.GR[R, :], op0=ALU.mult, op1=ALU.min).then_inc(abs_ready, 1)
            square(2)
            square(3)
            dve.wait_ge(log_ready, 1)
            link(dve.scalar_tensor_tensor(out=b.G1[R, :], in0=b.GR[R, :], scalar=0.0, in1=b.G1[R, :], op0=ALU.max, op1=ALU.add))
            link(dve.tensor_scalar(b.G1[R, :], b.G1[R, :], b.CO[R, 0:1], None, ALU.mult))
            for c in range(NT):
                at = slice(c * P, (c + 1) * P)
                link(dve.tensor_tensor_scan(b.GC[R, at], m.zeros[R, at], b.G1[R, at], 0.0, ALU.add, ALU.add))
            link(dve.tensor_scalar(b.GM[R, :], b.GC[R, :], -1.0, None, ALU.mult))
            last_of_chunk = b.GC[R, :].rearrange("p (c n) -> p c n", c=NT)[:, :, P - 1:P].to_broadcast([GH, NT, P])
            link(dve.tensor_tensor(b.G1[R, :].rearrange("p (c n) -> p c n", c=NT), last_of_chunk,
                                   b.GC[R, :].rearrange("p (c n) -> p c n", c=NT), ALU.subtract))
            dve.sem_inc(rows_a, 1)
            square(4)
            square(5)
            dve.wait_ge(rows_b, 1)
            link(dve.tensor_tensor(b.BE[R, :], b.BT[R, :], b.EG[R, :], ALU.mult))
            dve.sem_inc(rows_c, 1)
            square(6)
            dve.wait_ge(rows_t, 1)
            link(dve.tensor_copy(b.GN[:, :], m.ps[7][:, 0:64]))
            square(7)
            for c in range(8):
                dve.wait_ge(inv, c + 1)
                link(dve.scalar_tensor_tensor(out=b.XC[:, c, :], in0=b.XC[:, c, :], scalar=(GD ** -0.5 if c < 4 else 1.0),
                                              in1=q.RS[:, c, :], op0=ALU.mult, op1=ALU.mult))

        @block.scalar
        def _(act):
            link = Chain(act, act_step)
            link(act.activation(b.BT[R, :], b.GR[32:32 + GH, :], ACT.Sigmoid))
            link(act.activation(b.CO[R, 0:1], m.CP[R, K_AL:K_AL + 1], ACT.Exp))
            link(act.mul(b.CO[R, 0:1], b.CO[R, 0:1], -1.0))
            link(act.activation(b.GR[R, :], b.GR[R, :], ACT.Identity, bias=m.CP[R, K_DB:K_DB + 1]))
            act.sem_inc(biased, 1)
            act.wait_ge(abs_ready, 1)
            link(act.activation(b.G1[R, :], b.G1[R, :], ACT.Exp))
            act.activation(b.G1[R, :], b.G1[R, :], ACT.Ln, bias=1.0).then_inc(log_ready, 1)
            act.wait_ge(rows_a, 1)
            link(act.activation(b.EG[R, :], b.GC[R, :], ACT.Exp))
            link(act.activation(b.DK[R, :], b.G1[R, :], ACT.Exp))
            act.sem_inc(rows_b, 1)
            for c in range(8):
                act.wait_ge(sums, c + 1)
                act.activation(q.RS[:, c, :], m.ps[c][:, :], ACT.Ln, bias=1e-6).then_inc(logs, 1)
            for c in range(8):
                act.wait_ge(logs, c + 1)
                act.activation(q.RS[:, c, :], q.RS[:, c, :], ACT.Exp, scale=-0.5).then_inc(inv, 1)

        @block.tensor
        def _(pe):
            for c in range(6):
                pe.wait_ge(squares, c + 1)
                pe.matmul(m.ps[c][:, :], m.ones[:, :], q.SQ[:, c % 2, :], start=True, stop=True).then_inc(sums, 1)
            pe.wait_ge(rows_c, 1)
            for n, rows in enumerate((b.GM, b.BT, b.BE, b.DK)):
                for t in range(NT):
                    at = (n * NT + t) * GH
                    last = pe.transpose(m.ps[7][:, at:at + GH], rows[R, t * P:(t + 1) * P], m.ident[0:GH, 0:GH])
            last.then_inc(rows_t, 1)
            for c in (6, 7):
                pe.wait_ge(squares, c + 1)
                pe.matmul(m.ps[c][:, :], m.ones[:, :], q.SQ[:, c % 2, :], start=True, stop=True).then_inc(sums, 1)


def gdn_matrices(nc, m, b, w):
    names = ("dve_step", "nat_done", "nat_home", "row_done", "row_used", "masked", "decay", "tri_done", "tri_home", "ready")
    with stage(nc, "gdn_matrices", *names) as (block, sems):
        dve_step, nat_done, nat_home, row_done, row_used, masked, decay, tri_done, tri_home, ready = sems
        rows = [b.GC, b.BT, b.EG]

        @block.sync
        def _(sp):
            sp.dma_start(w.LM[:, :, :], m.d["level_masks"]).then_inc(ready, 16)
            sp.wait_ge(ready, 16)

        @block.tensor
        def _(pe):
            for c in range(NT):
                for x in range(2):
                    if c >= 2:
                        pe.wait_ge(nat_home, 2 * (c - 2) + x + 1)
                    for h in range(GH):
                        last = pe.transpose(m.ps[2 * x + c % 2][:, h * P:(h + 1) * P], b.XC[:, 4 * (x + 1) + h, c * P:(c + 1) * P], m.ident[:, :])
                    last.then_inc(nat_done, 1)
            for h in range(GH):
                for n in range(3):
                    i = 3 * h + n
                    if i >= 4:
                        pe.wait_ge(row_used, i - 3)
                    pe.matmul(m.ps[4 + i % 4][:, :], m.ident[0:GH, h:h + 1].to_broadcast([GH, P]), rows[n][0:GH, :], start=True, stop=True).then_inc(row_done, 1)
            pe.wait_ge(row_used, 12)
            pe.wait_ge(nat_home, 8)
            for c in range(NT):
                at = slice(c * P, (c + 1) * P)
                for x, right in enumerate((w.KB, None)):
                    i = 2 * c + x
                    if i >= 4:
                        pe.wait_ge(tri_home, i - 3)
                    for h in range(GH):
                        rhs = w.KB[:, h, at] if x == 0 else b.XC[:, h, at]
                        last = pe.matmul(m.ps[i % 4][:, h * P:(h + 1) * P], b.XC[:, 4 + h, at], rhs, start=True, stop=True)
                    last.then_inc(tri_done, 1)

        @block.vector
        def _(dve):
            link = Chain(dve, dve_step)

            def per_head(kind, c):
                at = (kind * NT + c) * GH
                return b.GN[:, at:at + GH].rearrange("p (h a) -> p h a", a=1).to_broadcast([P, GH, P])

            for c in range(NT):
                dve.wait_ge(nat_done, 2 * c + 1)
                k = m.ps[c % 2][:, :].rearrange("p (h n) -> p h n", h=GH)
                link(dve.tensor_tensor(w.KE[:, c, :, :], k, per_head(2, c), ALU.mult))
                dve.tensor_tensor(w.KD[:, c, :, :], k, per_head(3, c), ALU.mult).then_inc(nat_home, 1)
                dve.wait_ge(nat_done, 2 * c + 2)
                v = m.ps[2 + c % 2][:, :].rearrange("p (h n) -> p h n", h=GH)
                dve.tensor_tensor(w.VB[:, c, :, :], v, per_head(1, c), ALU.mult).then_inc(nat_home, 1)
            for h in range(GH):
                i = 3 * h
                dve.wait_ge(row_done, i + 1)
                dve.tensor_tensor(blocks(w.RM[:, h, :]), blocks(m.ps[4 + i % 4][:, :]), every_block(m.mask[:, 0, :]), ALU.add).then_inc(row_used, 1)
                dve.wait_ge(row_done, i + 2)
                dve.tensor_tensor(w.KB[:, h, :], m.ps[4 + (i + 1) % 4][:, :], b.XC[:, 4 + h, :], ALU.mult).then_inc(row_used, 1)
                dve.wait_ge(row_done, i + 3)
                link(dve.tensor_tensor(w.QE[:, h, :], m.ps[4 + (i + 2) % 4][:, :], b.XC[:, h, :], ALU.mult))
                dve.tensor_copy(w.GL[:, h, :], m.ps[4 + (i + 2) % 4][:, P - 1:S:P]).then_inc(row_used, 1)
            for c in range(NT):
                dve.wait_ge(decay, GH * NT)
                for x, out in enumerate((w.AT, w.AQ)):
                    dve.wait_ge(tri_done, 2 * c + x + 1)
                    dve.tensor_tensor(out[:, c, :, :].rearrange("p h n -> p (h n)"), m.ps[(2 * c + x) % 4][:, :],
                                      w.E[:, c, :, :].rearrange("p h n -> p (h n)"), ALU.mult).then_inc(tri_home, 1)
            for c in range(NT):
                for out in (w.T, w.U):
                    link(dve.tensor_copy(out[:, c, :, :], m.ident[:, :].rearrange("p (a n) -> p a n", a=1).to_broadcast([P, GH, P])))
            dve.wait_ge(tri_home, 8)

        @block.scalar
        def _(act):
            for h in range(GH):
                act.wait_ge(row_used, 3 * h + 1)
                for c in range(NT):
                    act.activation(w.E[:, c, h, :], w.RM[:, h, c * P:(c + 1) * P], ACT.Exp, bias=b.GN[:, c * GH + h:c * GH + h + 1]).then_inc(decay, 1)


def gdn_inverse(nc, m, b, w, XR):
    LEVELS = 7
    with stage(nc, "gdn_inverse", "z_done", "z_home", "t_done", "u_done", "tu_home", "gates_done", "pool_step") as (block, sems):
        z_done, z_home, t_done, u_done, tu_home, gates_done, pool_step = sems

        @block.scalar
        def _(act):
            for h in range(GH):
                act.activation(b.Z[:, h, :], b.Z[:, h, :], ACT.Silu).then_inc(gates_done, 1)
            for c in range(4):
                act.activation(b.LG[:, c, :], b.LG[:, c, :], ACT.Gelu_apprx_tanh).then_inc(gates_done, 1)
            act.wait_ge(gates_done, GH + 4)

        @block.gpsimd
        def _(pool):
            link = Chain(pool, pool_step)
            for c in range(4):
                for tap in range(4):
                    w_tap = m.CP[:, K_LC + 4 * c + tap:K_LC + 4 * c + tap + 1]
                    src = b.LX[:, c, tap:tap + S]
                    if tap == 0:
                        link(pool.tensor_scalar(XR[:, c, :], src, w_tap, m.CP[:, K_LB + c:K_LB + c + 1], ALU.mult, ALU.add))
                    else:
                        link(pool.tensor_scalar(w.TP[:, :], src, w_tap, None, ALU.mult))
                        link(pool.tensor_tensor(XR[:, c, :], XR[:, c, :], w.TP[:, :], ALU.add))

        @block.tensor
        def _(pe):
            with pe.Fori(0, LEVELS) as level:
                for c in range(NT):
                    pe.wait_ge(tu_home, level * 8 + 2 * c + 2)
                    for h in range(GH):
                        last = pe.matmul(m.ps[c][:, h * P:(h + 1) * P], w.AT[:, c, h, :], w.T[:, c, h, :], start=True, stop=True)
                    last.then_inc(z_done, 1)
                for c in range(NT):
                    pe.wait_ge(z_home, level * NT + c + 1)
                    for h in range(GH):
                        last = pe.matmul(m.ps[4 + c][:, h * P:(h + 1) * P], w.U[:, c, h, :], w.Z[:, c, h, :], start=True, stop=True)
                    last.then_inc(t_done, 1)
                    for h in range(GH):
                        last = pe.matmul(m.ps[c][:, h * P:(h + 1) * P], w.Z[:, c, h, :], w.U[:, c, h, :], start=True, stop=True)
                    last.then_inc(u_done, 1)

        @block.vector
        def _(dve):
            dve.sem_inc(tu_home, 8)
            with dve.Fori(0, LEVELS) as level:
                for c in range(NT):
                    dve.wait_ge(z_done, level * NT + c + 1)
                    mask = w.LM[:, bass.ds(level, 1), :].to_broadcast([P, GH, P])
                    dve.tensor_tensor(w.Z[:, c, :, :], m.ps[c][:, :].rearrange("p (h n) -> p h n", h=GH), mask, ALU.mult).then_inc(z_home, 1)
                for c in range(NT):
                    for x, (done, bank, out) in enumerate(((t_done, 4 + c, w.T), (u_done, c, w.U))):
                        dve.wait_ge(u_done, level * NT + c + 1)
                        flat = out[:, c, :, :].rearrange("p h n -> p (h n)")
                        dve.tensor_tensor(flat, flat, m.ps[bank][:, :], ALU.add).then_inc(tu_home, 1)


def gdn_sequence(nc, m, b, w):
    with stage(nc, "gdn_sequence", "w_done", "w_home", "v_done", "v_home", "o_done", "o_home", "s_done", "s_home", "dve_step") as (block, sems):
        w_done, w_home, v_done, v_home, o_done, o_home, s_done, s_home, dve_step = sems

        @block.tensor
        def _(pe):
            for c in range(1, NT):
                for h in range(GH):
                    last = pe.matmul(m.ps[c][:, h * P:(h + 1) * P], w.KE[:, c, h, :], w.U[:, c, h, :], start=True, stop=True)
                last.then_inc(w_done, 1)
            for c in range(NT):
                at = slice(c * P, (c + 1) * P)
                if c:
                    pe.wait_ge(w_home, c)
                    pe.wait_ge(s_home, c)
                    pe.wait_ge(v_home, c)
                for h in range(GH):
                    last = pe.matmul(m.ps[4][:, h * P:(h + 1) * P], w.U[:, c, h, :], w.VB[:, c, h, :], start=True, stop=(c == 0))
                    if c:
                        last = pe.matmul(m.ps[4][:, h * P:(h + 1) * P], w.NW[:, c, h, :], w.S[:, h, :], start=False, stop=True)
                last.then_inc(v_done, 1)
                pe.wait_ge(v_home, c + 1)
                if c:
                    pe.wait_ge(o_home, c)
                for h in range(GH):
                    if c:
                        pe.matmul(m.ps[5][:, h * P:(h + 1) * P], w.S[:, h, :], w.QE[:, h, at], start=True, stop=False)
                    last = pe.matmul(m.ps[5][:, h * P:(h + 1) * P], w.VN[:, h, :], w.AQ[:, c, h, :], start=(c == 0), stop=True)
                last.then_inc(o_done, 1)
                if c < NT - 1:
                    for h in range(GH):
                        last = pe.matmul(m.ps[6][:, h * P:(h + 1) * P], w.KD[:, c, h, :], w.VN[:, h, :], start=True, stop=True)
                    last.then_inc(s_done, 1)

        @block.vector
        def _(dve):
            link = Chain(dve, dve_step)
            for c in range(NT):
                dve.wait_ge(v_done, c + 1)
                if c:
                    dve.wait_ge(s_done, c)
                dve.tensor_copy(w.VN[:, :, :].rearrange("p h n -> p (h n)"), m.ps[4][:, :]).then_inc(v_home, 1)
                if c < NT - 1:
                    S_ = w.S[:, :, :].rearrange("p h n -> p (h n)")
                    dve.wait_ge(s_done, c + 1)
                    if c == 0:
                        dve.tensor_copy(S_, m.ps[6][:, :]).then_inc(s_home, 1)
                        dve.wait_ge(s_home, 1)
                    else:
                        link(dve.tensor_tensor(w.S[:, :, :], w.S[:, :, :], w.GL[:, :, c:c + 1].to_broadcast([P, GH, P]), ALU.mult))
                        dve.tensor_tensor(S_, S_, m.ps[6][:, :], ALU.add).then_inc(s_home, 1)
                        dve.wait_ge(s_home, c + 1)

        @block.scalar
        def _(act):
            for c in range(1, NT):
                act.wait_ge(w_done, c)
                act.mul(w.NW[:, c, :, :].rearrange("p h n -> p (h n)"), m.ps[c][:, :], -1.0).then_inc(w_home, 1)
            for c in range(NT):
                act.wait_ge(o_done, c + 1)
                act.copy(w.OT[:, :, c * P:(c + 1) * P], m.ps[5][:, :].rearrange("p (h n) -> p h n", h=GH)).then_inc(o_home, 1)
            act.wait_ge(o_home, NT)


def gdn_norm(nc, m, b, w):
    with stage(nc, "gdn_norm", "act_step", "dve_step", "squares", "sums", "inv") as (block, sems):
        act_step, dve_step, squares, sums, inv = sems

        @block.vector
        def _(dve):
            link = Chain(dve, dve_step)
            for h in range(GH):
                dve.tensor_tensor(w.KB[:, h, :], w.OT[:, h, :], w.OT[:, h, :], ALU.mult).then_inc(squares, 1)
            for h in range(GH):
                dve.wait_ge(inv, h + 1)
                link(dve.scalar_tensor_tensor(out=w.OT[:, h, :], in0=w.OT[:, h, :], scalar=m.CP[:, K_GN:K_GN + 1], in1=w.QE[:, h, :],
                                              op0=ALU.mult, op1=ALU.mult))
                link(dve.tensor_tensor(m.XT[:, h, :], w.OT[:, h, :], b.Z[:, h, :], ALU.mult))

        @block.tensor
        def _(pe):
            for h in range(GH):
                pe.wait_ge(squares, h + 1)
                pe.matmul(m.ps[h][:, :], m.ones[:, :], w.KB[:, h, :], start=True, stop=True).then_inc(sums, 1)

        @block.scalar
        def _(act):
            for h in range(GH):
                act.wait_ge(sums, h + 1)
                act.activation(w.QE[:, h, :], m.ps[h][:, :], ACT.Ln, scale=1.0 / GD, bias=1e-6).then_inc(act_step, 1)
            for h in range(GH):
                act.wait_ge(act_step, h + 1)
                act.activation(w.QE[:, h, :], w.QE[:, h, :], ACT.Exp, scale=-0.5).then_inc(inv, 1)


def lru(nc, m, b, u):
    names = ("act_step", "dve_step", "gate_w_in", "gates_done", "gates_home", "decay_arg", "decay_done", "root_arg", "root_done")
    with stage(nc, "lru", *names) as (block, sems):
        act_step, dve_step, gate_w_in, gates_done, gates_home, decay_arg, decay_done, root_arg, root_done = sems

        @block.sync
        def _(sp):
            sp.dma_start(u.WA[:, :, :], m.d["lru_w"]).then_inc(gate_w_in, 16)
            sp.wait_ge(gate_w_in, 16)

        @block.vector
        def _(dve):
            link = Chain(dve, dve_step)
            for c in range(4):
                dve.wait_ge(gates_home, 2 * c + 3)
                dve.tensor_scalar(u.RG[:, c, :], u.RG[:, c, :], u.SPA[:, c:c + 1], None, ALU.mult).then_inc(decay_arg, 1)
            for c in range(4):
                dve.wait_ge(decay_done, c + 1)
                link(dve.tensor_scalar(u.TH[:, 1, :], u.RT[:, c, :], 1.0, None, ALU.add))
                link(dve.reciprocal(u.TH[:, 1, :], u.TH[:, 1, :]))
                dve.scalar_tensor_tensor(out=u.RT[:, c, :], in0=u.RT[:, c, :], scalar=2.0, in1=u.TH[:, 1, :], op0=ALU.mult, op1=ALU.mult).then_inc(root_arg, 1)
                link(dve.tensor_tensor(u.XR[:, c, :], u.XR[:, c, :], u.IG[:, c, :], ALU.mult))
            for c in range(4):
                dve.wait_ge(root_done, c + 1)
                dve.wait_ge(decay_done, 4 + c + 1)
                link(dve.tensor_tensor(u.XR[:, c, :], u.XR[:, c, :], u.RT[:, c, :], ALU.mult))
                link(dve.tensor_tensor_scan(u.RT[:, c, :], u.RG[:, c, :], u.XR[:, c, :], 0.0, ALU.mult, ALU.add))
                link(dve.tensor_tensor(m.XT[:, 4 + c, :], u.RT[:, c, :], b.LG[:, c, :], ALU.mult))

        @block.tensor
        def _(pe):
            pe.wait_ge(gate_w_in, 16)
            for c in range(4):
                for x in range(2):
                    for half in range(2):
                        rows = slice(64 * half, 64 * half + 64)
                        last = pe.matmul(m.ps[2 * c + x][rows, :], u.WA[rows, 2 * c + x, :], u.XR[rows, c, :], start=True, stop=True)
                    last.then_inc(gates_done, 1)

        @block.scalar
        def _(act):
            link = Chain(act, act_step)
            a = m.CP[:, K_AP:K_AP + 4]
            link(act.activation(u.AB[:, 0:4], a, ACT.Abs))
            link(act.activation(u.AB[:, 0:4], u.AB[:, 0:4], ACT.Exp, scale=-1.0))
            link(act.activation(u.AB[:, 0:4], u.AB[:, 0:4], ACT.Ln, bias=1.0))
            link(act.activation(u.AB[:, 4:8], a, ACT.Relu, scale=-1.0))
            for c in range(4):
                link(act.activation(u.AB[:, c:c + 1], u.AB[:, c:c + 1], ACT.Identity, bias=u.AB[:, 4 + c:5 + c]))
            act.activation(u.SPA[:, :], u.AB[:, 0:4], ACT.Copy, scale=8.0).then_inc(gates_home, 1)
            for c in range(4):
                for x, out in enumerate((u.RG, u.IG)):
                    act.wait_ge(gates_done, 2 * c + x + 1)
                    at = (K_AB, K_XB)[x] + c
                    act.activation(out[:, c, :], m.ps[2 * c + x][:, :], ACT.Sigmoid, bias=m.CP[:, at:at + 1]).then_inc(gates_home, 1)
            for c in range(4):
                act.wait_ge(decay_arg, c + 1)
                act.activation(u.RT[:, c, :], u.RG[:, c, :], ACT.Tanh).then_inc(decay_done, 1)
            for c in range(4):
                act.wait_ge(decay_done, c + 1)
                act.activation(u.RG[:, c, :], u.RG[:, c, :], ACT.Exp, scale=-1.0).then_inc(decay_done, 1)
            for c in range(4):
                act.wait_ge(root_arg, c + 1)
                act.activation(u.RT[:, c, :], u.RT[:, c, :], ACT.Sqrt).then_inc(root_done, 1)

def out_projection_2(nc, m, f):
    names = ("raw_in", "w_high", "w_low", "xt_high", "xt_low", "block_done", "tile_done", "summed")
    with stage(nc, "out_projection_2", *names) as (block, (raw_in, w_high, w_low, xt_high, xt_low, block_done, tile_done, summed)):

        @block.sync
        def _(sp):
            for q in range(4):
                sp.dma_start(f.ring[:, q, :], m.d["w_out_2"][q]).then_inc(raw_in, 16)
                sp.wait_ge(raw_in, 16 * (q + 1))

        @block.tensor
        def _(pe):
            for q in range(4):
                half, kh = divmod(q, 2)
                pe.wait_ge(w_low, q + 1)
                pe.wait_ge(xt_low, 4 * (kh + 1))
                for t in range(NT):
                    n = 0
                    for k in range(4):
                        for hw, hx in TERMS:
                            last = pe.matmul(m.ps[4 * half + t][:, :], f.XS[:, hx, 4 * kh + k, t * P:(t + 1) * P], f.WS[:, q % 2, hw, k * S:(k + 1) * S],
                                             start=(kh == 0 and n == 0), stop=(kh == 1 and n == 11))
                            n += 1
                    if kh:
                        last.then_inc(tile_done, 1)
                if kh == 0:
                    last.then_inc(block_done, 1)

        @block.scalar
        def _(act):
            for q in range(4):
                if q < 2:
                    for k in range(4):
                        act.copy(f.XS[:, 0, 4 * q + k, :], m.XT[:, 4 * q + k, :]).then_inc(xt_high, 1)
                act.wait_ge(raw_in, 16 * (q + 1))
                if q == 2:
                    act.wait_ge(block_done, 1)
                elif q == 3:
                    act.wait_ge(tile_done, NT)
                act.copy(f.WS[:, q % 2, 0, :], f.ring[:, q, :]).then_inc(w_high, 1)

        @block.gpsimd
        def _(pool):
            for q in range(4):
                pool.wait_ge(w_high, q + 1)
                pool.tensor_tensor(f.WS[:, q % 2, 1, :], f.ring[:, q, :], f.WS[:, q % 2, 0, :].bitcast(F32), ALU.subtract).then_inc(w_low, 1)

        @block.vector
        def _(dve):
            for k in range(KD):
                dve.wait_ge(xt_high, k + 1)
                dve.tensor_tensor(f.XS[:, 1, k, :], m.XT[:, k, :], f.XS[:, 0, k, :].bitcast(F32), ALU.subtract).then_inc(xt_low, 1)
            for v in range(2 * NT):
                half, t = divmod(v, NT)
                cols = slice(half * S, (half + 1) * S)
                dve.wait_ge(tile_done, v + 1)
                dve.tensor_tensor(m.X[:, t, cols], m.X[:, t, cols], m.ps[v][:, :], ALU.add).then_inc(summed, 1)
            dve.wait_ge(summed, 2 * NT)


def feed_forward(nc, m, f):
    names = ("raw0", "raw1", "raw2", "raw3", "w_high", "w_low", "block_done", "unit_done", "tile_done", "relu_done", "squared", "u_high", "u_low", "summed")
    QB = 8
    with stage(nc, "feed_forward", *names) as (block, sems):
        raw, (w_high, w_low, block_done, unit_done, tile_done, relu_done, squared, u_high, u_low, summed) = sems[:4], sems[4:]

        @block.sync
        def _(sp):
            with sp.Fori(0, 4) as part:
                for q in range(QB):
                    sp.wait_ge(w_low, part * QB + q + 1)
                    src = m.d["w_ff1"] if q < 4 else m.d["w_ff2"]
                    sp.dma_start(f.ring[:, q % 4, :], src[bass.ds(part * 4 + q % 4, 1)].rearrange("a p n -> p (a n)")).then_inc(raw[q % 4], 16)

        @block.scalar
        def _(act):
            act.sem_inc(block_done, 1)
            act.sem_inc(tile_done, 8)
            with act.Fori(0, 4) as part:
                for q in range(QB):
                    act.wait_ge(raw[q % 4], part * 32 + (q // 4 + 1) * 16)
                    if q in (0, 6):
                        act.wait_ge(block_done, part * 2 + q // 6 + 1)
                    elif q in (1, 7):
                        act.wait_ge(tile_done, part * 8 + 8 + q // 7 * 4)
                    else:
                        act.wait_ge(unit_done, part * 8 + 2 * (q - 1))
                    act.copy(f.WS[:, q % 2, 0, :], f.ring[:, q % 4, :]).then_inc(w_high, 1)

        @block.gpsimd
        def _(pool):
            pool.sem_inc(w_low, 4)
            with pool.Fori(0, 4) as part:
                for q in range(QB):
                    pool.wait_ge(w_high, part * QB + q + 1)
                    pool.tensor_tensor(f.WS[:, q % 2, 1, :], f.ring[:, q % 4, :], f.WS[:, q % 2, 0, :].bitcast(F32), ALU.subtract).then_inc(w_low, 1)

        @block.tensor
        def _(pe):
            with pe.Fori(0, 2) as two:
                for a in range(2):
                    parts = two * 2 + a
                    mine, other = 4 * a, 4 - 4 * a
                    for q in range(4):
                        pe.wait_ge(w_low, parts * QB + q + 5)
                        for c in range(2):
                            u = 2 * q + c
                            if u == 0:
                                pe.wait_ge(summed, parts * 8 + 4)
                            if u >= 4:
                                pe.wait_ge(relu_done, parts * 8 + u - 3)
                            n = 0
                            for k in range(KD):
                                for hw, hx in TERMS:
                                    last = pe.matmul(m.ps[mine + u % 4][:, :], f.WS[:, q % 2, hw, k * 256 + c * P:k * 256 + (c + 1) * P], f.XS[:, hx, k, :],
                                                     start=(n == 0), stop=(n == 3 * KD - 1))
                                    n += 1
                            last.then_inc(unit_done, 1)
                    for q in range(4, QB):
                        half, kh = divmod(q - 4, 2)
                        pe.wait_ge(w_low, parts * QB + q + 5)
                        pe.wait_ge(u_low, parts * 8 + 4 * (kh + 1))
                        if kh == 0:
                            if half == 0:
                                pe.wait_ge(summed, parts * 8 + 8)
                            else:
                                pe.wait_ge(relu_done, parts * 8 + 8)
                        for t in range(NT):
                            bank = m.ps[(mine if half else other) + t]
                            n = 0
                            for k in range(4):
                                for hw, hx in TERMS:
                                    last = pe.matmul(bank[:, :], f.US[:, hx, 4 * kh + k, t * P:(t + 1) * P], f.WS[:, q % 2, hw, k * S:(k + 1) * S],
                                                     start=(kh == 0 and n == 0), stop=(kh == 1 and n == 11))
                                    n += 1
                            if kh:
                                last.then_inc(tile_done, 1)
                        if kh == 0:
                            last.then_inc(block_done, 1)

        @block.vector
        def _(dve):
            dve.sem_inc(summed, 8)
            with dve.Fori(0, 2) as two:
                for a in range(2):
                    parts = two * 2 + a
                    mine, other = 4 * a, 4 - 4 * a
                    for u in range(8):
                        bank = m.ps[mine + u % 4][:, :]
                        dve.wait_ge(unit_done, parts * 8 + u + 1)
                        dve.tensor_scalar(f.SQ[:, u % 2, :], bank, 0.0, None, ALU.max).then_inc(relu_done, 1)
                        dve.wait_ge(relu_done, parts * 8 + u + 1)
                        dve.tensor_tensor(f.SQ[:, u % 2, :], f.SQ[:, u % 2, :], f.SQ[:, u % 2, :], ALU.mult).then_inc(squared, 1)
                        dve.wait_ge(squared, parts * 8 + u + 1)
                        dve.tensor_copy(f.US[:, 0, u, :], f.SQ[:, u % 2, :]).then_inc(u_high, 1)
                        dve.wait_ge(u_high, parts * 8 + u + 1)
                        dve.tensor_tensor(f.US[:, 1, u, :], f.SQ[:, u % 2, :], f.US[:, 0, u, :].bitcast(F32), ALU.subtract).then_inc(u_low, 1)
                    for v in range(8):
                        half, t = divmod(v, NT)
                        cols = slice(half * S, (half + 1) * S)
                        dve.wait_ge(tile_done, parts * 8 + v + 9)
                        dve.tensor_tensor(m.X[:, t, cols], m.X[:, t, cols], m.ps[(mine if half else other) + t][:, :], ALU.add).then_inc(summed, 1)
            dve.wait_ge(summed, 40)


def final_norm(nc, m, n, out):
    names = ("row_in", "act_step", "inv", "dve_step", "finished", "out_done")
    with stage(nc, "final_norm", *names) as (block, (row_in, act_step, inv, dve_step, finished, out_done)):

        @block.sync
        def _(sp):
            sp.dma_start(n.FN[:, :], m.d["final_norm"].to_broadcast([P, D])).then_inc(row_in, 16)
            for t in range(NT):
                sp.wait_ge(finished, t + 1)
                sp.dma_start(out.rearrange("(t p) d -> t p d", p=P)[t], m.X[:, t, :]).then_inc(out_done, 16)
            sp.wait_ge(out_done, 16 * NT)

        @block.scalar
        def _(act):
            for t in range(NT):
                act.activation(n.XN[:, t, :], m.X[:, t, :], ACT.Square, accum_out=n.SS[:, t:t + 1]).then_inc(act_step, 1)
            act.wait_ge(act_step, NT)
            act.activation(n.SS[:, :], n.SS[:, :], ACT.Sqrt, scale=1.0 / D, bias=1e-6).then_inc(inv, 1)

        @block.vector
        def _(dve):
            dve.wait_ge(row_in, 16)
            dve.wait_ge(inv, 1)
            dve.reciprocal(n.SS[:, :], n.SS[:, :]).then_inc(dve_step, 1)
            dve.wait_ge(dve_step, 1)
            for t in range(NT):
                dve.scalar_tensor_tensor(out=m.X[:, t, :], in0=m.X[:, t, :], scalar=n.SS[:, t:t + 1], in1=n.FN[:, :],
                                         op0=ALU.mult, op1=ALU.mult).then_inc(finished, 1)


class Bag:
    pass


def sb(nc, ctx, name, *shape):
    return ctx.enter_context(nc.sbuf_tensor(f"{name}_{nc.next_id()}", list(shape), F32))


def sbr(nc, ctx, name, *shape):
    return ctx.enter_context(nc.sbuf_tensor(f"{name}_{nc.next_id()}", list(shape), F32R))


def build(nc, d, out):
    with ExitStack() as ctx:
        m = Bag()
        m.X = sb(nc, ctx, "X", P, NT, D)
        m.XT = sb(nc, ctx, "XT", P, KD, S)
        m.ident = sb(nc, ctx, "ident", P, P)
        m.ones = sb(nc, ctx, "ones", P, P)
        m.zeros = sb(nc, ctx, "zeros", P, S)
        m.mask = sb(nc, ctx, "mask", P, 2, P)
        m.TRI = sb(nc, ctx, "TRI", P, P)
        m.IOTA = sb(nc, ctx, "IOTA", P, P)
        m.TAB = sb(nc, ctx, "TAB", P, S)
        m.dup = sb(nc, ctx, "dup", P, 64)
        m.CC = sb(nc, ctx, "CC", P, 8)
        m.CP = sb(nc, ctx, "CP", P, K_N)
        m.RP = sb(nc, ctx, "RP", P, 276)
        m.WR = sb(nc, ctx, "WR", P, KD, 20)
        m.d = d
        m.x_dram, m.dup_dram = d["x"], d["dup"]
        m.ps = [ctx.enter_context(nc.psum_tensor(f"bank{i}", [P, S], F32)) for i in range(8)]
        m.raw_in = [ctx.enter_context(nc.semaphore(f"raw_in{i}")) for i in range(4)]
        m.mla_in = ctx.enter_context(nc.semaphore("mla_in"))
        m.out_in = ctx.enter_context(nc.semaphore("out_in"))
        with ExitStack() as c0:
            m.ang = sb(nc, c0, "ang", P, S)
            m.kk = sb(nc, c0, "kk", P, S)
            m.posi = c0.enter_context(nc.sbuf_tensor("posi", [P, S], I32))
            constants(nc, m, d["consts"], d["positions"])

        with ExitStack() as c1:
            m.raw = sb(nc, c1, "raw", P, 4, KD * 256)
            m.w_mla = m.raw[:, 0:2, :].rearrange("p a n -> p (a n)")[:, 0:3072]
            with nc.Fori(0, DEPTH) as layer:
                one = bass.ds(layer, 1)

                def first_loads(sp):
                    for i in range(4):
                        sp.dma_start(m.raw[:, i, :], d["w_in"][one, i].rearrange("a p n -> p (a n)")).then_inc(m.raw_in[i], 16)

                def layer_params(sp, sem):
                    sp.dma_start(m.CP[:, 0:C_N], d["cols"][one].rearrange("a p n -> p (a n)")).then_inc(sem, 16)
                    sp.dma_start(m.RP[:, :], d["rows"][one, 0:276].to_broadcast([P, 276])).then_inc(sem, 16)
                    sp.dma_start(m.WR[:, :, :].rearrange("p k n -> p (k n)"), d["w_router"][one].rearrange("a p n -> p (a n)")).then_inc(sem, 16)
                    return 3

                with ExitStack() as c2:
                    mx = Bag()
                    mx.V1 = sb(nc, c2, "V1", P, NT, 4, 65)
                    mx.O = sb(nc, c2, "O", P, NT, 256)
                    mx.MQ = sb(nc, c2, "MQ", P, 2, S)
                    mx.MK = sb(nc, c2, "MK", P, 2, S)
                    mx.Z = sb(nc, c2, "Z", P, 2, S)
                    mx.XB = sb(nc, c2, "XB", P, 6, S + 4)
                    mx.SC = sb(nc, c2, "SC", P, S)
                    mx.IG = sb(nc, c2, "IG", P, S)
                    with ExitStack() as c3:
                        mx.CQ = sb(nc, c3, "CQ", P, 3, S)
                        mx.KRT = sb(nc, c3, "KRT", P, S)
                        mx.TP = sb(nc, c3, "TP", P, S)
                        with ExitStack() as c4:
                            XS = sbr(nc, c4, "XS", P, 2, KD, S)
                            WS = sbr(nc, c4, "WS", P, 2, 2, KD * 256)
                            transpose_stage(nc, m, XS, first_loads, layer_params)
                            in_projection(nc, m, layer, mx, XS, WS)
                        a = Bag()
                        a.QT = sb(nc, c3, "QT", P, 4, S)
                        a.KT = sb(nc, c3, "KT", P, 4, S)
                        a.V = sb(nc, c3, "V", P, NT, S)
                        a.PR = sb(nc, c3, "PR", P, 4, S)
                        a.PT = sb(nc, c3, "PT", P, 2, NT, P)
                        a.SQ = sb(nc, c3, "SQ", P, 3, S)
                        a.RS = sb(nc, c3, "RS", P, 2, S)
                        a.MX = sb(nc, c3, "MX", P, 4)
                        a.NM = sb(nc, c3, "NM", P, 4)
                        a.SM = sb(nc, c3, "SM", P, 4)
                        a.RC = sb(nc, c3, "RC", P, 4)
                        mla(nc, m, layer, mx, a)
                    with ExitStack() as c3:
                        g = Bag()
                        g.T1 = sb(nc, c3, "T1", P, S)
                        g.SP = sb(nc, c3, "SP", P, S)
                        g.CS = sb(nc, c3, "CS", P, S)
                        g.FS = sb(nc, c3, "FS", P, S)
                        g.NM = sb(nc, c3, "NM", P, S)
                        g.CO = sb(nc, c3, "CO", P, 2)
                        g.GN = sb(nc, c3, "GN", P, 3, NT, GR)
                        g.EM = sb(nc, c3, "EM", P, NT, GR)
                        g.XC = mx.XB[:, :, 2:2 + S]
                        g.XN = sb(nc, c3, "XN", P, NT, 256)
                        g.E = sb(nc, c3, "E", P, 4, S)
                        g.W = sb(nc, c3, "W", P, 4, S)
                        g.RM = sb(nc, c3, "RM", P, 2, S)
                        g.H = sb(nc, c3, "H", P, NT, 4, 64)
                        g.HB = sb(nc, c3, "HB", P, NT, 64)
                        g.DN = sb(nc, c3, "DN", P, 2, NT)
                        g.DT = sb(nc, c3, "DT", P, 2, NT)
                        g.MEAN = sb(nc, c3, "MEAN", P, 2, 16)
                        gate_rows(nc, m, mx, g)
                        scans(nc, m, mx, g)
                        mixer_norms(nc, m, mx, g)
                with ExitStack() as c2:
                    ln = Bag()
                    ln.Y = sb(nc, c2, "Y", P, NT, D)
                    ln.GB = sb(nc, c2, "GB", P, 2 * D)
                    ln.ST = sb(nc, c2, "ST", P, NT, 2, 6)
                    ln.MV = sb(nc, c2, "MV", P, NT, 2)
                    ln.IV = sb(nc, c2, "IV", P, NT)
                    with ExitStack() as c3:
                        XS = sbr(nc, c3, "XS", P, 2, KD, S)
                        WS = sbr(nc, c3, "WS", P, 4, 2, KD * 256)
                        norm_stage(nc, m, ln, 0, layer, XS, WS)
                    transpose_stage(nc, m)
                    with ExitStack() as c3:
                        r = Bag()
                        r.LG = sb(nc, c3, "LG", P, NT, 20)
                        r.hg = sb(nc, c3, "hg", P, NT, 4)
                        r.h1 = sb(nc, c3, "h1", P, NT, 4)
                        r.h2 = sb(nc, c3, "h2", P, NT, 4)
                        r.e4 = sb(nc, c3, "e4", P, NT, 4)
                        r.el = sb(nc, c3, "el", P, NT, 4)
                        r.gm = sb(nc, c3, "gm", P, NT)
                        r.m1 = sb(nc, c3, "m1", P, NT)
                        r.m2 = sb(nc, c3, "m2", P, NT)
                        r.t1 = sb(nc, c3, "t1", P, NT)
                        r.COMB = sb(nc, c3, "COMB", P, NT, NE)
                        r.OH = sb(nc, c3, "OH", P, NT, NE)
                        r.POS = sb(nc, c3, "POS", P, NT, NE + NE // NGR)
                        r.NP = sb(nc, c3, "NP", P, 3)
                        r.NPI = c3.enter_context(nc.sbuf_tensor("passes", [P, 1], I32))
                        r.CW = sbr(nc, c3, "CW", P, NT, NE, 2)
                        r.XH = sbr(nc, c3, "XH", P, NT, D)
                        r.XL = sbr(nc, c3, "XL", P, NT, D)
                        r.SEL = sbr(nc, c3, "SEL", P, NT, 4 * P)
                        r.SELT = sbr(nc, c3, "SELT", P, 4, S)
                        r.YE = sbr(nc, c3, "YE", P, 2, 2, D)
                        r.WS = sb(nc, c3, "WS", P, 4)
                        r.DN = sb(nc, c3, "DN", P, 2, 2 * D)
                        r.H = sb(nc, c3, "H", P, 2, FE)
                        r.HT = sb(nc, c3, "HT", P, 2, 2 * P)
                        r.SG = sb(nc, c3, "SG", P, 2, FE)
                        r.TRI, r.IOTA = m.TRI, m.IOTA
                        r.Y = ln.Y
                        router(nc, m, r)
                        dispatch(nc, m, r)
                        passes = nc.values_load(r.NPI[0:1, 0:1], min_val=1, max_val=4,
                                                skip_runtime_bounds_check_because="it is one plus three comparisons' results")
                        with nc.Fori(0, passes):
                            experts(nc, m, r, layer)
                            next_pass(nc, r)
                    norm_stage(nc, m, ln, 1, layer)
                nums = [s.num for s in (*m.raw_in, m.mla_in, m.out_in)]
                nc.all_engine_barrier(sems_to_clear=range(min(nums), max(nums) + 1))

        with ExitStack() as c1:
            b = Bag()
            b.Z = sb(nc, c1, "Z", P, 4, S)
            b.LG = sb(nc, c1, "LG", P, 4, S)
            b.LX = sb(nc, c1, "LX", P, 4, S + 3)
            b.GR = sb(nc, c1, "GR", P, S)
            b.G1 = sb(nc, c1, "G1", P, S)
            b.GC = sb(nc, c1, "GC", P, S)
            b.GM = sb(nc, c1, "GM", P, S)
            b.BT = sb(nc, c1, "BT", P, S)
            b.EG = sb(nc, c1, "EG", P, S)
            b.DK = sb(nc, c1, "DK", P, S)
            b.BE = sb(nc, c1, "BE", P, S)
            b.CO = sb(nc, c1, "CO", P, 1)
            b.GN = sb(nc, c1, "GN", P, 64)
            with ExitStack() as c2:
                q = Bag()
                q.QB = sb(nc, c1, "QB", P, 12, S + 3)
                b.XC = q.QB[:, :, 3:3 + S]

                def params(sp, sem):
                    sp.dma_start(m.CP[:, 0:K_N], d["cols_2"]).then_inc(sem, 16)
                    return 1

                b.XS = sbr(nc, c2, "XS", P, 2, KD, S)
                with ExitStack() as c3:
                    n = Bag()
                    n.XN = sb(nc, c3, "XN", P, NT, D)
                    n.SS = sb(nc, c3, "SS", P, NT)
                    n.DG = sb(nc, c3, "DG", P, NT, P)
                    rms_transpose(nc, m, n, b.XS, K_NM, params)
                with ExitStack() as c3:
                    q.ring = sb(nc, c3, "ring", P, 4, KD * 256)
                    q.WS = sbr(nc, c3, "WS", P, 2, 2, KD * 256)
                    q.TP = sb(nc, c3, "TP", P, S)
                    in_projection_2(nc, m, b, q)
            with ExitStack() as c2:
                q.SQ = sb(nc, c2, "SQ", P, 2, S)
                q.RS = sb(nc, c2, "RS", P, 8, S)
                gdn_prepare(nc, m, b, q)
            with ExitStack() as c2:
                hd = (P, GH, S)
                ch = (P, NT, GH, P)
                w = Bag()
                w.LM = sb(nc, c2, "LM", P, 7, P)
                w.KB = sb(nc, c2, "KB", *hd)
                w.QE = sb(nc, c2, "QE", *hd)
                w.RM = sb(nc, c2, "RM", *hd)
                w.GL = sb(nc, c2, "GL", P, GH, NT)
                w.AT = sb(nc, c2, "AT", *ch)
                w.AQ = sb(nc, c2, "AQ", *ch)
                w.T = sb(nc, c2, "T", *ch)
                w.U = sb(nc, c2, "U", *ch)
                w.KE = sb(nc, c2, "KE", *ch)
                w.KD = sb(nc, c2, "KD", *ch)
                w.VB = sb(nc, c2, "VB", *ch)
                w.VN = sb(nc, c2, "VN", P, GH, P)
                w.S = sb(nc, c2, "S", P, GH, P)
                with ExitStack() as c3:
                    w.E = sb(nc, c3, "E", *ch)
                    gdn_matrices(nc, m, b, w)
                with ExitStack() as c3:
                    w.Z = sb(nc, c3, "Z", *ch)
                    w.TP = sb(nc, c3, "TP", P, S)
                    gdn_inverse(nc, m, b, w, m.XT[:, 4:8, :])
                w.NW = sb(nc, c2, "NW", *ch)
                w.OT = w.RM
                gdn_sequence(nc, m, b, w)
                gdn_norm(nc, m, b, w)
            with ExitStack() as c2:
                u = Bag()
                u.XR = m.XT[:, 4:8, :]
                u.RG = sb(nc, c2, "RG", *hd)
                u.IG = sb(nc, c2, "IG", *hd)
                u.RT = sb(nc, c2, "RT", *hd)
                u.TH = sb(nc, c2, "TH", P, 2, S)
                u.WA = sb(nc, c2, "WA", P, 8, 64)
                u.AB = sb(nc, c2, "AB", P, 8)
                u.SPA = sb(nc, c2, "SPA", P, 4)
                lru(nc, m, b, u)
        with ExitStack() as c1:
            f = Bag()
            f.ring = sb(nc, c1, "ring", P, 4, KD * 256)
            f.WS = sbr(nc, c1, "WS", P, 2, 2, KD * 256)
            f.XS = sbr(nc, c1, "XS", P, 2, KD, S)
            out_projection_2(nc, m, f)
            with ExitStack() as c2:
                n = Bag()
                n.XN = sb(nc, c2, "XN", P, NT, D)
                n.SS = sb(nc, c2, "SS", P, NT)
                n.DG = sb(nc, c2, "DG", P, NT, P)
                rms_transpose(nc, m, n, f.XS, K_NP)
            with ExitStack() as c2:
                f.US = sbr(nc, c2, "US", P, 2, 8, S)
                f.SQ = sb(nc, c2, "SQ", P, 2, S)
                feed_forward(nc, m, f)
            with ExitStack() as c2:
                n = Bag()
                n.XN = sb(nc, c2, "XN", P, NT, D)
                n.SS = sb(nc, c2, "SS", P, NT)
                n.FN = sb(nc, c2, "FN", P, D)
                final_norm(nc, m, n, out)


def rows_to_tiles(w, cols):
    w = w[:, cols] if cols is not None else w
    return np.ascontiguousarray(w.reshape(-1, P, w.shape[1]).transpose(1, 0, 2).reshape(P, -1))


def layer_arrays(i):
    w_in, L = i["w_in"], DEPTH
    z = np.zeros((L, D, 1), np.float32)

    def take(cols):
        idx = np.array([2488 if c is None else c for c in cols])
        return np.concatenate([w_in, z], -1)[:, :, idx]

    none = [None]
    kr = list(range(384, 416))
    krs = kr[16:] + kr[:16]
    g = lambda j: list(range(1440 + 4 * j, 1444 + 4 * j))
    dt = lambda j: list(range(2480 + 4 * j, 2484 + 4 * j))
    sc = g(1) + dt(0) + none * 24 + g(3) + dt(1)
    ig = g(0) + none * 28 + g(2) + none * 4
    xbc = list(range(1712, 2480))
    block0 = list(range(0, 384)) + sc + none * 24 + kr + krs
    block1 = xbc[:512]
    block2 = xbc[512:] + list(range(1456, 1712))
    block3 = list(range(416, 928))
    vo = list(range(928, 1440))
    tiles = lambda a: np.stack([rows_to_tiles(x, None) for x in a])
    order = block0 + block1 + block2 + block3
    columns = [tiles(take(order[256 * n:256 * (n + 1)])) for n in range(8)]
    rows = [tiles(take(vo)[:, S * kh:S * (kh + 1)]) for kh in range(2)]
    w_blocks = np.stack(columns + rows, 1)

    uq = i["mla_w_uq"].reshape(L, 256, HEADS, NOPE + ROPE)
    swapped = np.concatenate([uq[..., 80:96], uq[..., 64:80]], -1)
    uq = np.concatenate([uq, swapped], -1).reshape(L, 256, HEADS * P)
    ukv = i["mla_w_ukv"].reshape(L, P, HEADS, NOPE + VD)
    w_mla = np.concatenate([tiles(uq), ukv[..., :NOPE].reshape(L, P, 512), ukv[..., NOPE:].reshape(L, P, 512)], -1)

    w_out = np.stack([tiles(i["w_out"][:, S * kh:S * (kh + 1), S * half:S * (half + 1)]) for kh in range(2) for half in range(2)], 1)
    gu = np.concatenate([i["expert_w_gate"], i["expert_w_up"]], -1)
    w_exp = np.concatenate([gu.reshape(L, NE, KD, P, 2 * FE).transpose(0, 1, 3, 2, 4).reshape(L, NE, P, -1),
                            i["expert_w_down"].reshape(L, NE, 2, P, D).transpose(0, 1, 3, 2, 4).reshape(L, NE, P, -1)], -1)
    we = i["router_expert_w"].transpose(0, 2, 1, 3).reshape(L, D, NE)
    w_router = tiles(np.concatenate([i["router_group_w"], we], -1))

    cols = np.zeros((L, P, C_N), np.float32)
    cols[:, :, C_QN:C_QN + 2] = i["mla_q_norm"].reshape(L, 2, P).transpose(0, 2, 1)
    cols[:, :, C_KVN] = i["mla_kv_norm"]
    cols[:, :, C_CW:C_CW + 30] = i["ssd_conv_w"].reshape(L, 5, 6, P).transpose(0, 3, 2, 1).reshape(L, P, 30)
    cols[:, :, C_CB:C_CB + 6] = i["ssd_conv_b"].reshape(L, 6, P).transpose(0, 2, 1)
    cols[:, :, C_DS:C_DS + 2] = np.repeat(i["ssd_d"].reshape(L, 2, 2), 64, axis=2).transpose(0, 2, 1)
    cols[:, :, C_SN:C_SN + 2] = i["ssd_norm"].reshape(L, 2, P).transpose(0, 2, 1)
    for d in range(2):
        lf, dtr = slice(32 * d, 32 * d + 4), slice(32 * d + 4, 32 * d + 8)
        cols[:, lf, C_SGN], cols[:, dtr, C_SGN] = -1.0, 1.0
        cols[:, dtr, C_SB] = i["ssd_dt_bias"][:, d]
        cols[:, lf, C_SB] = i["mlstm_gate_bias"][:, 2 * d + 1]
        cols[:, dtr, C_AL] = i["ssd_a_log"][:, d]
        cols[:, lf, C_IB] = i["mlstm_gate_bias"][:, 2 * d]
    rows = np.concatenate([i["mlstm_norm"], i["router_group_b"], i["router_expert_b"].reshape(L, NE),
                           i["ln1_g"], i["ln1_b"], i["ln2_g"], i["ln2_b"]], -1)
    return {"w_in": w_blocks, "w_gates": tiles(take(ig)), "w_mla": w_mla, "w_out": w_out, "w_exp": w_exp, "w_router": w_router, "cols": cols, "rows": rows}


def second_arrays(i):
    w = i["w_in_2"][0]
    perm = list(range(0, 1536)) + list(range(1536, 2048)) + list(range(2056, 3080))
    w_in_2 = np.stack([rows_to_tiles(w, np.array(perm[256 * n:256 * (n + 1)])) for n in range(12)])
    gate = np.zeros((D, GR), np.float32)
    gate[:, 0:4], gate[:, 32:36] = w[:, 2052:2056], w[:, 2048:2052]
    gate = rows_to_tiles(gate, None)
    cols = np.zeros((P, K_N), np.float32)
    per = lambda v, n: v.reshape(n, P).T
    cols[:, K_NM:K_NM + 8] = per(i["norm_mix_w_2"][0], 8)
    cols[:, K_NP:K_NP + 8] = per(i["norm_mlp_w_2"][0], 8)
    cols[:, K_GC:K_GC + 48] = i["gdn_conv_w_2"][0].reshape(4, 12, P).transpose(2, 1, 0).reshape(P, 48)
    cols[:, K_LC:K_LC + 16] = i["lru_conv_w_2"][0].reshape(4, 4, P).transpose(2, 1, 0).reshape(P, 16)
    cols[:, K_LB:K_LB + 4] = per(i["lru_conv_b_2"][0], 4)
    cols[:, K_AB:K_AB + 4] = per(i["lru_gate_a_b_2"][0], 4)
    cols[:, K_XB:K_XB + 4] = per(i["lru_gate_x_b_2"][0], 4)
    cols[:, K_AP:K_AP + 4] = per(i["lru_a_param_2"][0], 4)
    cols[:, K_GN] = i["gdn_norm_w_2"][0]
    cols[0:4, K_AL] = i["gdn_A_log_2"][0]
    cols[0:4, K_DB] = i["gdn_dt_bias_2"][0]
    gates = np.stack([i["lru_gate_a_w_2"][0], i["lru_gate_x_w_2"][0]], 1).reshape(4, 2, 2, 64, 64)
    lru_w = np.ascontiguousarray(gates.transpose(1, 3, 0, 2, 4).reshape(P, 8, 64))
    quarters = lambda a: [rows_to_tiles(a[S * kh:S * (kh + 1)], slice(S * half, S * (half + 1))) for half in range(2) for kh in range(2)]
    w_ff1 = np.stack([rows_to_tiles(i["w_ff1_2"][0], slice(256 * n, 256 * (n + 1))) for n in range(16)])
    w_ff2 = np.stack([q for part in range(4) for q in quarters(i["w_ff2_2"][0][D * part:D * (part + 1)])])
    return {"w_in_2": w_in_2, "w_gates_2": gate, "cols_2": cols, "lru_w": lru_w, "w_out_2": np.stack(quarters(i["w_out_2"][0])),
            "w_ff1": w_ff1, "w_ff2": w_ff2, "final_norm": i["final_norm_w_2"].reshape(1, D)}


def shape_constants():
    consts = np.zeros((P, 8), np.float32)
    freq = np.float32(10000.0) ** (-np.arange(0, ROPE, 2, dtype=np.float32) / np.float32(ROPE))
    consts[64:128, 0] = np.tile(freq, 4)
    consts[64:96, 1] = 0.25
    consts[64:96, 2] = math.pi / 2
    consts[64:96, 3], consts[96:112, 3], consts[112:128, 3] = 1.0, -1.0, 1.0
    consts[:, 4:8] = [4.0, 3.0, 2.0, 1.0]
    dup = np.zeros((P, 64), np.float32)
    for r in range(64):
        dup[64 + r, r % 32], dup[64 + r, 32 + r % 32] = 1.0, 1.0
    i, j = np.arange(P)[:, None], np.arange(P)[None, :]
    masks = [-((i // (2 * n) == j // (2 * n)) & (i // n > j // n)).astype(np.float32) for n in (1, 2, 4, 8, 16, 32, 64)]
    return {"consts": consts, "dup": dup, "level_masks": np.ascontiguousarray(np.stack(masks, 1))}


def kernel(**inputs):
    import concourse.bacc as bacc
    from concourse.bass_utils import run_bass_kernel_spmd as run

    i = {k: np.asarray(v) for k, v in inputs.items()}
    arrays = {"x": i["x"].reshape(S, D), "positions": i["positions"].reshape(1, S)}
    arrays.update(shape_constants())
    arrays.update(layer_arrays(i))
    arrays.update(second_arrays(i))
    arrays = {k: np.ascontiguousarray(v) for k, v in arrays.items()}
    nc = bacc.Bacc("TRN2", target_bir_lowering=False, num_devices=1)
    d = {k: nc.dram_tensor(f"in_{k}", v.shape, mybir.dt.from_np(v.dtype), kind="ExternalInput").ap() for k, v in arrays.items()}
    out = nc.dram_tensor("out", (S, D), F32, kind="ExternalOutput").ap()
    build(nc, d, out)
    r = run(nc, [{f"in_{k}": v for k, v in arrays.items()}], core_ids=[0])
    return r.results[0]["out"].reshape(1, S, D)
```
